# Optimizing a Trainium2 kernel written in Bass

```python
import math
import jax, jax.numpy as jnp
from jax import lax
import numpy as np

D_MODEL = 1024
BATCH = 1
SEQ = 512
DEPTH = 2

CONV_WIDTH = 512
CONV_KSIZE = 3
ATTN_HEADS = 8
HEAD_DIM = 64
ATTN_WIDTH = ATTN_HEADS * HEAD_DIM
IDX_HEADS = 8
IDX_DIM = 64
INDEX_TOPK = 256
Q_BLOCK = 128
ROPE_THETA = 10000.0
POOL_WINDOWS = (2, 4, 8, 16)
POOL_GROUPS = 4
POOL_WIDTH = 512
POOL_GROUP_DIM = POOL_WIDTH // POOL_GROUPS
N_BRANCHES = 3
RMS_EPS = 1e-6

IN_SPLITS = (CONV_WIDTH, CONV_WIDTH, CONV_WIDTH, CONV_WIDTH,
             ATTN_WIDTH, ATTN_WIDTH, ATTN_WIDTH, ATTN_WIDTH,
             IDX_HEADS * IDX_DIM, IDX_DIM, IDX_HEADS,
             POOL_WIDTH, POOL_WIDTH,
             N_BRANCHES * D_MODEL)
IN_WIDTH = 4 * CONV_WIDTH + 4 * ATTN_WIDTH + IDX_HEADS * IDX_DIM + IDX_DIM + IDX_HEADS + 2 * POOL_WIDTH + N_BRANCHES * D_MODEL


def rms_norm(x, g):
    xf = x.astype(jnp.float32)
    y = xf * lax.rsqrt(jnp.mean(xf * xf, axis=-1, keepdims=True) + RMS_EPS)
    return (y * g.astype(jnp.float32)).astype(x.dtype)

def split_columns(p):
    out = []
    off = 0
    for n in IN_SPLITS:
        out.append(p[..., off:off + n])
        off += n
    return out

def rope_tables(seq_len, dim):
    inv = 1.0 / (ROPE_THETA ** (jnp.arange(0, dim, 2, dtype=jnp.float32) / dim))
    ang = jnp.arange(seq_len, dtype=jnp.float32)[:, None] * inv[None, :]
    return jnp.cos(ang), jnp.sin(ang)

def apply_rope(x, cos, sin):
    xf = x.astype(jnp.float32)
    half = xf.shape[-1] // 2
    x1, x2 = xf[..., :half], xf[..., half:]
    c, s = cos[None, :, None, :], sin[None, :, None, :]
    return jnp.concatenate([x1 * c - x2 * s, x2 * c + x1 * s], axis=-1).astype(x.dtype)

def short_conv_mixer(b, c, xin, gate, conv_w, w_out):
    S = xin.shape[1]
    z = c * xin
    zp = jnp.pad(z, ((0, 0), (CONV_KSIZE - 1, 0), (0, 0)))
    y = conv_w[0] * zp[:, 0:S]
    for j in range(1, CONV_KSIZE):
        y = y + conv_w[j] * zp[:, j:j + S]
    y = b * y * jax.nn.silu(gate)
    return y @ w_out

def sparse_attention_mixer(q, k, v, gate, iq, ik, iw, q_g, k_g, cos, sin, w_out):
    B, S, _ = q.shape
    q = apply_rope(rms_norm(q.reshape(B, S, ATTN_HEADS, HEAD_DIM), q_g), cos, sin)
    k = apply_rope(rms_norm(k.reshape(B, S, ATTN_HEADS, HEAD_DIM), k_g), cos, sin)
    v = v.reshape(B, S, ATTN_HEADS, HEAD_DIM)
    iq = apply_rope(iq.reshape(B, S, IDX_HEADS, IDX_DIM), cos, sin)
    ik = apply_rope(ik[:, :, None, :], cos, sin)[:, :, 0, :]
    top_k = min(INDEX_TOPK, S // 4)
    nb = S // Q_BLOCK

    def to_blocks(a):
        return jnp.swapaxes(a.reshape((B, nb, Q_BLOCK) + a.shape[2:]), 0, 1)

    starts = jnp.arange(nb, dtype=jnp.int32) * Q_BLOCK
    key_pos = jnp.arange(S, dtype=jnp.int32)

    def block_fn(args):
        qb, iqb, iwb, t0 = args
        tq = t0 + jnp.arange(Q_BLOCK, dtype=jnp.int32)
        sc = jnp.einsum('bqhd,bsd->bqhs', iqb, ik).astype(jnp.float32) * (IDX_DIM ** -0.5)
        score = jnp.einsum('bqhs,bqh->bqs', jax.nn.relu(sc), iwb.astype(jnp.float32)) * (IDX_HEADS ** -0.5)
        admissible = key_pos[None, :] <= tq[:, None]
        score = jnp.where(admissible[None], score, -jnp.inf)
        _, idx = lax.top_k(score, top_k)
        valid = idx <= tq[None, :, None]
        k_sel = jax.vmap(lambda kb, ib: kb[ib])(k, idx)
        v_sel = jax.vmap(lambda vb, ib: vb[ib])(v, idx)
        s = jnp.einsum('bqhd,bqkhd->bhqk', qb, k_sel).astype(jnp.float32) * (HEAD_DIM ** -0.5)
        s = jnp.where(valid[:, None], s, -jnp.inf)
        p = jax.nn.softmax(s, axis=-1).astype(v.dtype)
        return jnp.einsum('bhqk,bqkhd->bqhd', p, v_sel)

    o = lax.map(block_fn, (to_blocks(q), to_blocks(iq), to_blocks(iw), starts))
    o = jnp.swapaxes(o, 0, 1).reshape(B, S, ATTN_WIDTH)
    return (o * jax.nn.silu(gate)) @ w_out

def pool_mixer(u, gate, pool_w, pool_scale, w_out):
    B, S, _ = u.shape
    ug = u.reshape(B, S, POOL_GROUPS, POOL_GROUP_DIM)
    cs = jnp.cumsum(ug.astype(jnp.float32), axis=1)
    t = jnp.arange(S)
    means = []
    for gi, w in enumerate(POOL_WINDOWS):
        c = cs[:, :, gi]
        lagged = jnp.pad(c, ((0, 0), (w, 0), (0, 0)))[:, :S]
        cnt = jnp.minimum(t + 1, w).astype(jnp.float32)[None, :, None]
        means.append((c - lagged) / cnt)
    pooled = (jnp.stack(means, axis=2) - ug.astype(jnp.float32)).astype(u.dtype)
    mixed = jnp.einsum('bsgc,gcd->bsgd', pooled, pool_w).reshape(B, S, POOL_WIDTH)
    y = mixed * pool_scale * jax.nn.silu(gate)
    return y @ w_out

def first_inputs(seed: int = 0) -> dict:
    key = jax.random.key(seed)
    ks = jax.random.split(key, 13)
    f32 = jnp.float32
    L = DEPTH
    return {
        "x": jax.random.normal(ks[0], (BATCH, SEQ, D_MODEL), f32),
        "norm_g": 1.0 + 0.1 * jax.random.normal(ks[1], (L, D_MODEL), f32),
        "w_in": jax.random.normal(ks[2], (L, D_MODEL, IN_WIDTH), f32) * D_MODEL ** -0.5,
        "conv_w": jax.random.normal(ks[3], (L, CONV_KSIZE, CONV_WIDTH), f32) * CONV_KSIZE ** -0.5,
        "w_out_conv": jax.random.normal(ks[4], (L, CONV_WIDTH, D_MODEL), f32) * CONV_WIDTH ** -0.5,
        "q_norm_g": 1.0 + 0.1 * jax.random.normal(ks[5], (L, HEAD_DIM), f32),
        "k_norm_g": 1.0 + 0.1 * jax.random.normal(ks[6], (L, HEAD_DIM), f32),
        "w_out_attn": jax.random.normal(ks[7], (L, ATTN_WIDTH, D_MODEL), f32) * ATTN_WIDTH ** -0.5,
        "pool_w": jax.random.normal(ks[8], (L, POOL_GROUPS, POOL_GROUP_DIM, POOL_GROUP_DIM), f32) * POOL_GROUP_DIM ** -0.5,
        "pool_scale": 1.0 + 0.1 * jax.random.normal(ks[9], (L, POOL_WIDTH), f32),
        "w_out_pool": jax.random.normal(ks[10], (L, POOL_WIDTH, D_MODEL), f32) * POOL_WIDTH ** -0.5,
        "w_o": jax.random.normal(ks[11], (L, D_MODEL, D_MODEL), f32) * D_MODEL ** -0.5,
    }

def first_block(x, norm_g, w_in, conv_w, w_out_conv, q_norm_g, k_norm_g, w_out_attn, pool_w, pool_scale, w_out_pool, w_o):
    B, S, D = x.shape
    cos, sin = rope_tables(S, HEAD_DIM)
    for l in range(DEPTH):
        h = rms_norm(x, norm_g[l])
        p = h @ w_in[l]
        (cb, cc, cx, cgate, q, k, v, agate, iq, ik, iw, pu, pgate, mgate) = split_columns(p)
        y_a = short_conv_mixer(cb, cc, cx, cgate, conv_w[l], w_out_conv[l])
        y_b = sparse_attention_mixer(q, k, v, agate, iq, ik, iw, q_norm_g[l], k_norm_g[l], cos, sin, w_out_attn[l])
        y_c = pool_mixer(pu, pgate, pool_w[l], pool_scale[l], w_out_pool[l])
        g = jax.nn.sigmoid(mgate.reshape(B, S, N_BRANCHES, D))
        merged = g[:, :, 0] * y_a + g[:, :, 1] * y_b + g[:, :, 2] * y_c
        x = x + merged @ w_o[l]
    return x


GRID_W = 64
ATT_Q_HEADS = 8
ATT_KV_HEADS = 2
ATT_Q_W = ATT_Q_HEADS * HEAD_DIM
ATT_KV_W = ATT_KV_HEADS * HEAD_DIM
HY_WIDTH = 512
HY_ORDER = 2
HY_BANDS = 16
HY_EMB = 1 + 2 * HY_BANDS
HY_FFN = 64
HY_FAST_DECAY = 0.3
HY_SLOW_DECAY = 1.5
HY_TARGET = 1e-2
GLA_HEADS = 4
GLA_DK = 64
GLA_DV = 128
GLA_RANK = 16
GLA_NORMALIZER = 16.0
GLA_CHUNK = 64
GLA_K_W = GLA_HEADS * GLA_DK
GLA_V_W = GLA_HEADS * GLA_DV
MEM_LEN = 256
X_HEADS = 4
X_HEAD_DIM = D_MODEL // X_HEADS
D_FF = 4 * D_MODEL
N_BRANCH = 3
EPS = 1e-6
IN_SPLITS_2 = (ATT_Q_W, ATT_KV_W, ATT_KV_W, 3 * HY_WIDTH, GLA_K_W, GLA_K_W, GLA_V_W, GLA_V_W,
             2 * GLA_RANK, N_BRANCH * D_MODEL)
N_IN = ATT_Q_W + 2 * ATT_KV_W + 3 * HY_WIDTH + 2 * GLA_K_W + 2 * GLA_V_W + 2 * GLA_RANK + N_BRANCH * D_MODEL


F32 = jnp.float32

def rmsnorm(x, g):
    xf = x.astype(F32)
    y = xf * lax.rsqrt(jnp.mean(xf * xf, axis=-1, keepdims=True) + EPS)
    return (y * g.astype(F32)).astype(x.dtype)

def split_cols(u, sizes):
    idx = [int(i) for i in np.cumsum(sizes)[:-1]]
    return jnp.split(u, idx, axis=-1)

def axial_rope_angles(L):
    rows = L // GRID_W
    r, c = jnp.meshgrid(jnp.arange(rows), jnp.arange(GRID_W), indexing="ij")
    n_freq = HEAD_DIM // 4
    inv = ROPE_THETA ** (-jnp.arange(n_freq, dtype=F32) / n_freq)
    pos = jnp.stack([r.reshape(-1), c.reshape(-1)], axis=1).astype(F32)
    ang = pos[:, :, None] * inv
    return jnp.cos(ang), jnp.sin(ang)

def apply_rope_2(x, cos, sin):
    xs = x.reshape(x.shape[:-1] + (2, 2, HEAD_DIM // 4)).astype(F32)
    x1, x2 = xs[..., 0, :], xs[..., 1, :]
    out = jnp.stack([x1 * cos - x2 * sin, x1 * sin + x2 * cos], axis=-2)
    return out.reshape(x.shape).astype(x.dtype)

def attention_mixer(q, k, v, qn, kn, cos, sin):
    B, L, _ = q.shape
    G = ATT_Q_HEADS // ATT_KV_HEADS
    q = rmsnorm(q.reshape(B, L, ATT_Q_HEADS, HEAD_DIM), qn).transpose(0, 2, 1, 3)
    k = rmsnorm(k.reshape(B, L, ATT_KV_HEADS, HEAD_DIM), kn).transpose(0, 2, 1, 3)
    v = v.reshape(B, L, ATT_KV_HEADS, HEAD_DIM).transpose(0, 2, 1, 3)
    q = apply_rope_2(q, cos, sin).reshape(B, ATT_KV_HEADS, G, L, HEAD_DIM)
    k = apply_rope_2(k, cos, sin)
    nb = L // Q_BLOCK
    qb = jnp.moveaxis(q.reshape(B, ATT_KV_HEADS, G, nb, Q_BLOCK, HEAD_DIM), 3, 0)
    scale = HEAD_DIM ** -0.5

    def block(qblk):
        s = jnp.einsum("bkgqd,bktd->bkgqt", qblk, k).astype(F32) * scale
        p = jax.nn.softmax(s, axis=-1).astype(v.dtype)
        return jnp.einsum("bkgqt,bktd->bkgqd", p, v)

    o = lax.map(block, qb)
    o = jnp.moveaxis(o, 0, 3).reshape(B, ATT_Q_HEADS, L, HEAD_DIM)
    return o.transpose(0, 2, 1, 3).reshape(B, L, ATT_Q_W)

def short_conv(u, w):
    up = jnp.pad(u, ((0, 0), (1, 1), (0, 0)))
    return up[:, :-2] * w[0] + up[:, 1:-1] * w[1] + up[:, 2:] * w[2]

def hyena_pos_features(L):
    t = jnp.arange(L, dtype=F32)
    t_norm = t / max(L - 1, 1)
    w = 2.0 * math.pi * t / L
    f = jnp.linspace(1e-4, HY_BANDS - 1, HY_BANDS, dtype=F32)
    fw = w[:, None] * f
    z = jnp.concatenate([t_norm[:, None], jnp.cos(fw), -jnp.sin(fw)], axis=-1)
    deltas = jnp.abs(jnp.linspace(math.log(HY_TARGET) / HY_FAST_DECAY,
                                  math.log(HY_TARGET) / HY_SLOW_DECAY, HY_WIDTH, dtype=F32))
    window = jnp.exp(-t_norm[:, None] * deltas)
    return z, window

def hyena_filter_spectra(z, window, w1, b1, w2, b2, w3, b3, freq):
    L = z.shape[0]
    c = lambda a: a.astype(F32)
    h = jnp.sin(c(freq[0]) * (z @ c(w1) + c(b1)))
    h = jnp.sin(c(freq[1]) * (h @ c(w2) + c(b2)))
    h = (h @ c(w3) + c(b3)).reshape(L, HY_ORDER, 2, HY_WIDTH) * window[:, None, None, :]
    fwd, bwd = h[:, :, 0], h[:, :, 1]
    f = jnp.concatenate([fwd, jnp.zeros((1, HY_ORDER, HY_WIDTH), F32), bwd[1:][::-1]], axis=0)
    f = f / (jnp.sum(jnp.abs(f), axis=0, keepdims=True) + EPS)
    return jnp.fft.rfft(f, axis=0)

def long_conv(u, spec, skip):
    L = u.shape[1]
    uf = u.astype(F32)
    y = jnp.fft.irfft(jnp.fft.rfft(uf, n=2 * L, axis=1) * spec, n=2 * L, axis=1)[:, :L]
    return (y + uf * skip.astype(F32)).astype(u.dtype)

def hyena_mixer(u, conv_w, spec, skip):
    u = short_conv(u, conv_w)
    v, x1, x2 = jnp.split(u, 3, axis=-1)
    z = x1 * long_conv(v, spec[:, 0], skip[0])
    return x2 * long_conv(z, spec[:, 1], skip[1])

def gla_scan(q, k, v, g, include_diag):
    B, H, L, dk = q.shape
    dv = v.shape[-1]
    C = GLA_CHUNK
    N = L // C
    q, k, g = (a.reshape(B, H, N, C, dk) for a in (q, k, g))
    v = v.reshape(B, H, N, C, dv)
    b = jnp.cumsum(g, axis=3)
    b_last = b[:, :, :, -1:, :]
    q_dec = q * jnp.exp(b)
    a = jnp.einsum("bhncd,bhnsd->bhncs", q_dec, k * jnp.exp(-b))
    mask = jnp.tril(jnp.ones((C, C), dtype=bool), k=0 if include_diag else -1)
    o = jnp.einsum("bhncs,bhnse->bhnce", jnp.where(mask, a, 0.0), v)
    d_state = jnp.einsum("bhncd,bhnce->bhnde", k * jnp.exp(b_last - b), v)
    decay = jnp.exp(b_last[:, :, :, 0, :])

    def step(S, inp):
        dec, ds = inp
        return dec[..., None] * S + ds, S

    _, s_prev = lax.scan(step, jnp.zeros((B, H, dk, dv), F32),
                         (jnp.moveaxis(decay, 2, 0), jnp.moveaxis(d_state, 2, 0)))
    s_prev = jnp.moveaxis(s_prev, 0, 2)
    o = o + jnp.einsum("bhncd,bhnde->bhnce", q_dec, s_prev)
    return o.reshape(B, H, L, dv)

def gla_mixer(q, k, v, og, lr, w_lr, b_lr, onorm):
    B, L, _ = q.shape
    heads = lambda a, d: a.astype(F32).reshape(B, L, GLA_HEADS, d).transpose(0, 2, 1, 3)
    q = heads(q, GLA_DK) * (GLA_DK ** -0.5)
    k = heads(k, GLA_DK)
    v = heads(v, GLA_DV)
    logit = jnp.einsum("btsr,srd->btsd", lr.astype(F32).reshape(B, L, 2, GLA_RANK),
                       w_lr.astype(F32)) + b_lr.astype(F32)
    g = jax.nn.log_sigmoid(logit) / GLA_NORMALIZER
    g_f = heads(g[:, :, 0], GLA_DK)
    g_b = heads(g[:, :, 1], GLA_DK)
    fl = lambda a: jnp.flip(a, axis=2)
    o_f = gla_scan(q, k, v, g_f, True)
    o_b = fl(gla_scan(fl(q), fl(k), fl(v), fl(g_b), False))
    o = (o_f + o_b).transpose(0, 2, 1, 3)
    o = rmsnorm(o, onorm) * jax.nn.silu(og.astype(F32).reshape(B, L, GLA_HEADS, GLA_DV))
    return o.reshape(B, L, GLA_V_W).astype(og.dtype)

def memory_cross_attention(hn, mn, wq, wk, wv, wo, qn, kn):
    B, L, _ = hn.shape
    M = mn.shape[1]
    q = rmsnorm((hn @ wq).reshape(B, L, X_HEADS, X_HEAD_DIM), qn)
    k = rmsnorm((mn @ wk).reshape(B, M, X_HEADS, X_HEAD_DIM), kn)
    v = (mn @ wv).reshape(B, M, X_HEADS, X_HEAD_DIM)
    s = jnp.einsum("blhd,bmhd->bhlm", q, k).astype(F32) * (X_HEAD_DIM ** -0.5)
    p = jax.nn.softmax(s, axis=-1).astype(v.dtype)
    o = jnp.einsum("bhlm,bmhd->blhd", p, v).reshape(B, L, D_MODEL)
    return o @ wo

def second_inputs(seed: int = 0) -> dict:
    key = jax.random.key(seed)
    ks = iter(jax.random.split(key, 40))

    def nrm(shape, s):
        return jax.random.normal(next(ks), shape, F32) * s

    def gain(shape):
        return 1.0 + nrm(shape, 0.02)

    Ld = DEPTH
    return {
        "x": nrm((BATCH, SEQ, D_MODEL), 1.0),
        "mem": nrm((BATCH, MEM_LEN, D_MODEL), 1.0),
        "ln_mix": gain((Ld, D_MODEL)),
        "w_in": nrm((Ld, D_MODEL, N_IN), D_MODEL ** -0.5),
        "attn_qnorm": gain((Ld, HEAD_DIM)),
        "attn_knorm": gain((Ld, HEAD_DIM)),
        "hy_conv": nrm((Ld, 3, 3 * HY_WIDTH), 3 ** -0.5),
        "hy_w1": nrm((Ld, HY_EMB, HY_FFN), HY_EMB ** -0.5),
        "hy_b1": nrm((Ld, HY_FFN), 0.1),
        "hy_w2": nrm((Ld, HY_FFN, HY_FFN), HY_FFN ** -0.5),
        "hy_b2": nrm((Ld, HY_FFN), 0.1),
        "hy_w3": nrm((Ld, HY_FFN, HY_ORDER * 2 * HY_WIDTH), HY_FFN ** -0.5),
        "hy_b3": nrm((Ld, HY_ORDER * 2 * HY_WIDTH), 0.1),
        "hy_freq": 1.0 + nrm((Ld, 2, HY_FFN), 0.1),
        "hy_skip": nrm((Ld, HY_ORDER, HY_WIDTH), 0.5),
        "gla_w_lr": nrm((Ld, 2, GLA_RANK, GLA_K_W), GLA_RANK ** -0.5),
        "gla_b_lr": nrm((Ld, 2, GLA_K_W), 0.1),
        "gla_onorm": gain((Ld, GLA_DV)),
        "w_br_attn": nrm((Ld, ATT_Q_W, D_MODEL), ATT_Q_W ** -0.5),
        "w_br_hyena": nrm((Ld, HY_WIDTH, D_MODEL), HY_WIDTH ** -0.5),
        "w_br_gla": nrm((Ld, GLA_V_W, D_MODEL), GLA_V_W ** -0.5),
        "w_out": nrm((Ld, D_MODEL, D_MODEL), D_MODEL ** -0.5),
        "ln_x": gain((Ld, D_MODEL)),
        "ln_mem": gain((Ld, D_MODEL)),
        "x_wq": nrm((Ld, D_MODEL, D_MODEL), D_MODEL ** -0.5),
        "x_wk": nrm((Ld, D_MODEL, D_MODEL), D_MODEL ** -0.5),
        "x_wv": nrm((Ld, D_MODEL, D_MODEL), D_MODEL ** -0.5),
        "x_wo": nrm((Ld, D_MODEL, D_MODEL), D_MODEL ** -0.5),
        "x_qnorm": gain((Ld, X_HEAD_DIM)),
        "x_knorm": gain((Ld, X_HEAD_DIM)),
        "ln_mlp": gain((Ld, D_MODEL)),
        "mlp_w1": nrm((Ld, D_MODEL, D_FF), D_MODEL ** -0.5),
        "mlp_w2": nrm((Ld, D_FF, D_MODEL), D_FF ** -0.5),
    }

def second_block(x, mem, ln_mix, w_in, attn_qnorm, attn_knorm, hy_conv, hy_w1, hy_b1, hy_w2, hy_b2,
              hy_w3, hy_b3, hy_freq, hy_skip, gla_w_lr, gla_b_lr, gla_onorm, w_br_attn, w_br_hyena,
              w_br_gla, w_out, ln_x, ln_mem, x_wq, x_wk, x_wv, x_wo, x_qnorm, x_knorm, ln_mlp,
              mlp_w1, mlp_w2):
    B, L, _ = x.shape
    cos, sin = axial_rope_angles(L)
    z_pos, window = hyena_pos_features(L)
    h = x
    for i in range(DEPTH):
        hn = rmsnorm(h, ln_mix[i])
        (aq, ak, av, hy, gq, gk, gv, go, glr, gates) = split_cols(hn @ w_in[i], IN_SPLITS_2)
        y_a = attention_mixer(aq, ak, av, attn_qnorm[i], attn_knorm[i], cos, sin) @ w_br_attn[i]
        spec = hyena_filter_spectra(z_pos, window, hy_w1[i], hy_b1[i], hy_w2[i], hy_b2[i],
                                    hy_w3[i], hy_b3[i], hy_freq[i])
        y_b = hyena_mixer(hy, hy_conv[i], spec, hy_skip[i]) @ w_br_hyena[i]
        y_c = gla_mixer(gq, gk, gv, go, glr, gla_w_lr[i], gla_b_lr[i], gla_onorm[i]) @ w_br_gla[i]
        gate = jax.nn.sigmoid(gates.reshape(B, L, N_BRANCH, D_MODEL))
        mixed = gate[:, :, 0] * y_a + gate[:, :, 1] * y_b + gate[:, :, 2] * y_c
        h = h + mixed @ w_out[i]
        h = h + memory_cross_attention(rmsnorm(h, ln_x[i]), rmsnorm(mem, ln_mem[i]),
                                       x_wq[i], x_wk[i], x_wv[i], x_wo[i], x_qnorm[i], x_knorm[i])
        hn = rmsnorm(h, ln_mlp[i])
        h = h + jnp.square(jax.nn.relu(hn @ mlp_w1[i])) @ mlp_w2[i]
    return h


def setup_inputs(seed=0):
    out = dict(first_inputs(seed))
    for name, value in second_inputs(seed + 1).items():
        if name != "x":
            out[name + "_2"] = value
    return out


def reference(
    x, norm_g, w_in, conv_w, w_out_conv, q_norm_g, k_norm_g, w_out_attn, pool_w, pool_scale,
    w_out_pool, w_o, mem_2, ln_mix_2, w_in_2, attn_qnorm_2, attn_knorm_2, hy_conv_2, hy_w1_2,
    hy_b1_2, hy_w2_2, hy_b2_2, hy_w3_2, hy_b3_2, hy_freq_2, hy_skip_2, gla_w_lr_2, gla_b_lr_2,
    gla_onorm_2, w_br_attn_2, w_br_hyena_2, w_br_gla_2, w_out_2, ln_x_2, ln_mem_2, x_wq_2,
    x_wk_2, x_wv_2, x_wo_2, x_qnorm_2, x_knorm_2, ln_mlp_2, mlp_w1_2, mlp_w2_2,
):
    x = first_block(
        x, norm_g, w_in, conv_w, w_out_conv, q_norm_g, k_norm_g, w_out_attn, pool_w, pool_scale,
        w_out_pool, w_o,
    )
    return second_block(
        x, mem_2, ln_mix_2, w_in_2, attn_qnorm_2, attn_knorm_2, hy_conv_2, hy_w1_2, hy_b1_2,
        hy_w2_2, hy_b2_2, hy_w3_2, hy_b3_2, hy_freq_2, hy_skip_2, gla_w_lr_2, gla_b_lr_2,
        gla_onorm_2, w_br_attn_2, w_br_hyena_2, w_br_gla_2, w_out_2, ln_x_2, ln_mem_2, x_wq_2,
        x_wk_2, x_wv_2, x_wo_2, x_qnorm_2, x_knorm_2, ln_mlp_2, mlp_w1_2, mlp_w2_2,
    )


_drawn_inputs = setup_inputs


def setup_inputs(seed=0):
    import zlib

    import numpy as np

    out = dict(_drawn_inputs(seed))
    spreads = {}
    factors = {'q_norm_g': 4.753,
     'k_norm_g': 5.339,
     'ln_mix_2': 3.471,
     'attn_qnorm_2': 8.0,
     'attn_knorm_2': 8.0,
     'hy_b1_2': 8.0,
     'hy_b2_2': 6.286,
     'hy_b3_2': 5.17,
     'hy_freq_2': 8.0,
     'gla_b_lr_2': 3.3,
     'gla_onorm_2': 7.817,
     'ln_x_2': 8.0,
     'ln_mem_2': 8.0,
     'x_qnorm_2': 8.0,
     'x_knorm_2': 8.0,
     'ln_mlp_2': 5.617}
    for name, (base, spread) in spreads.items():
        noise = np.random.default_rng([zlib.crc32(name.encode()), seed]).standard_normal(out[name].shape)
        drawn = base * np.exp(spread * noise) if base else spread * noise
        out[name] = __import__('jax').numpy.asarray(drawn.astype(out[name].dtype))
    for name, factor in factors.items():
        out[name] = (out[name] * factor).astype(out[name].dtype)
    return out
```

```python
import numpy as np
import concourse.bass as bass
from concourse import mybir
from contextlib import ExitStack

SEQ = 512
DM = 1024
EPS = 1e-6
NEG = -1e30
GONE = -3e38
BIG = 3e38
MAGIC = 12582912.0

NF = 26
NRT = 56
NRAW = 3
NSP = 3
PB_COLS = 64 + 2 * 26 + 2 * 84


def program(nc, ins, place, out, steps=8):
    fp32 = mybir.dt.float32
    fp32r = mybir.dt.float32r
    ALU = mybir.AluOpType
    ACT = mybir.ActivationFunctionType
    AX = mybir.AxisListType

    ctx = ExitStack()
    with ctx:
        def sb(name, shape, dt=fp32):
            return ctx.enter_context(nc.sbuf_tensor(name, shape, dt))

        FT = sb("FT", [128, NF, 512])
        RT = sb("RT", [128, NRT, 512], fp32r)
        WRAW = sb("WRAW", [128, NRAW, 1024])
        WSP = sb("WSP", [128, NSP, 2, 1024], fp32r)
        CST = sb("CST", [128, 8, 128])
        PAR = sb("PAR", [128, PB_COLS])
        SM = sb("SM", [128, 16, 16])
        banks = [ctx.enter_context(nc.psum_tensor(f"B{i}", [128, 512], fp32)) for i in range(8)]
        xs = [nc.dram_tensor(f"xs{i}", [8, 128, 512], fp32, kind="Internal").ap() for i in range(2)]

        eye, ones, pair = CST[:, 0, :], CST[:, 1, :], CST[:, 2, :]
        rotA, rotB, causal = CST[:, 3, :], CST[:, 4, :], CST[:, 5, :]
        maskf, maskb = CST[:, 6, :], CST[:, 7, :]

        class Tok:
            __slots__ = ("sem", "val")

            def __init__(self, sem, val):
                self.sem, self.val = sem, val

        class Queue:

            def __init__(self, sem):
                self.sem, self.n, self.q, self.seen = sem, 0, [], {}

            def wait(self, w):
                if w is None:
                    return
                if isinstance(w, Tok):
                    if self.seen.get(w.sem, 0) < w.val:
                        self.seen[w.sem] = w.val
                        self.q.append(("w", w.sem, w.val))
                    return
                for x in w:
                    self.wait(x)

            def put(self, fn, w, inc=True):
                best = {}

                def flat(t):
                    if t is None:
                        return
                    if isinstance(t, Tok):
                        if best.get(t.sem, 0) < t.val:
                            best[t.sem] = t.val
                        return
                    for x in t:
                        flat(x)
                flat(w)
                for s, v in best.items():
                    self.wait(Tok(s, v))
                if not inc:
                    self.q.append(("i", fn, None, 0))
                    return None
                self.n += 1
                self.q.append(("i", fn, self.sem, 1))
                return Tok(self.sem, self.n)

            def play(self, e):
                for it in self.q:
                    if it[0] == "w":
                        e.wait_ge(it[1], it[2])
                    else:
                        r = it[1](e)
                        if it[2] is not None:
                            r.then_inc(it[2], it[3])

        sems = [ctx.enter_context(nc.semaphore(f"s_{n}")) for n in ("pe", "dve", "act", "pool", "sp")]
        s_raw = [ctx.enter_context(nc.semaphore(f"s_raw{i}")) for i in range(NRAW)]
        s_misc = [ctx.enter_context(nc.semaphore(f"s_misc{i}")) for i in range(24)]
        s_out = ctx.enter_context(nc.semaphore("s_out"))

        class Tile:
            __slots__ = ("ap", "free", "t", "kind")

            def __init__(self, ap, kind):
                self.ap, self.free, self.t, self.kind = ap, None, None, kind

        def emit(order):
            M, V, A, G, S = (Queue(s) for s in sems)
            pools = {
                "F": [Tile(FT[:, i, :], "F") for i in range(NF)],
                "R": [Tile(RT[:, i, :], "R") for i in range(NRT)],
                "P": [Tile(b[:, :], "P") for b in banks],
                "S": [Tile(SM[:, i, :], "S") for i in range(16)],
            }

            def get(kind="F"):
                assert pools[kind], "no tile left: " + kind
                old = pools[kind].pop(0)
                new = Tile(old.ap, kind)
                new.free = old.free
                return new

            def drop(tile, *toks):
                tile.free = [x for x in toks]
                pools[tile.kind].append(tile)

            def tt(E, o, a, b, op, *w):
                return E.put(lambda e: e.tensor_tensor(o, a, b, op), w)

            def ts(E, o, a, s1, s2, op0, op1, *w):
                if s2 is None:
                    return E.put(lambda e: e.tensor_scalar(o, a, s1, None, op0), w)
                return E.put(lambda e: e.tensor_scalar(o, a, s1, s2, op0, op1), w)

            def stt(o, a, s, b, op0, op1, *w):
                return V.put(lambda e: e.scalar_tensor_tensor(o, a, s, b, op0, op1), w)

            def cp(E, o, a, *w):
                if E is A:
                    return A.put(lambda e: e.activation(o, a, ACT.Copy), w)
                return E.put(lambda e: e.tensor_copy(o, a), w)

            def act(o, a, f, *w, **k):
                return A.put(lambda e: e.activation(o, a, f, **k), w)

            def recip(o, a, *w):
                return V.put(lambda e: e.reciprocal(o, a), w)

            def memset(E, o, v, *w):
                return E.put(lambda e: e.memset(o, v), w)

            def mm(o, l, r, start, stop, *w, inc=False):
                return M.put(lambda e: e.matmul(o, l, r, start=start, stop=stop), w, inc)

            def tp(o, a, *w, inc=False):
                return M.put(lambda e: e.transpose(o, a, eye[0:a.shape[0], 0:a.shape[0]]), (w, cst), inc)

            misc = [0]
            mcount = [0] * len(s_misc)

            def dma(o, a, *w):
                i = misc[0] % len(s_misc)
                misc[0] += 1
                S.wait(Tok(s_misc[i], mcount[i] * 16))
                S.put(lambda e: e.dma_start(o, a).then_inc(s_misc[i], 16), w, inc=False)
                mcount[i] += 1
                return Tok(s_misc[i], mcount[i] * 16)

            asked = []
            raw_free = [None] * NRAW
            sp_free = [None] * NSP
            state = {"issued": 0, "used": 0}
            ready = {}

            def issue(i):
                arr, off, n, cols = place[order[i]]
                r, s = i % NRAW, i % NSP
                m = n * cols
                src = ins[arr][off:off + 128 * m].rearrange("(p m) -> p m", p=128)
                dst = WRAW[:, r, 0:m]
                S.put(lambda e: e.dma_start(dst, src).then_inc(s_raw[r], 16), raw_free[r], inc=False)
                t = Tok(s_raw[r], 16 * (i // NRAW + 1))
                hi, lo = WSP[:, s, 0, 0:m], WSP[:, s, 1, 0:m]
                a = A.put(lambda e: e.activation(hi, dst, ACT.Copy), (t, sp_free[s]))
                E = G if i % 3 == 1 else V
                b = E.put(lambda e: e.tensor_tensor(lo, dst, hi.bitcast(fp32), ALU.subtract), (t, a, sp_free[s]))
                raw_free[r] = (a, b)
                ready[i] = (hi.rearrange("p (n c) -> p n c", n=n), lo.rearrange("p (n c) -> p n c", n=n), (a, b))

            def weight(key):
                i = state["used"]
                state["used"] += 1
                asked.append(key)
                if order is None:
                    arr, off, n, cols = place[key]
                    z = WSP[:, 0, 0, 0:n * cols].rearrange("p (n c) -> p n c", n=n)
                    return z, z, None
                assert order[i] == key
                while state["issued"] < min(i + NSP, len(order)):
                    issue(state["issued"])
                    state["issued"] += 1
                return ready.pop(i)

            def weight_done(tok):
                sp_free[(state["used"] - 1) % NSP] = tok

            def mm3(o, L, R, first, last, *w, inc=False):
                mm(o, L[0], R[0], first, False, w)
                mm(o, L[0], R[1], False, False)
                return mm(o, L[1], R[0], False, last, inc=inc)

            def split(src, *w):
                hi, lo = get("R"), get("R")
                a = A.put(lambda e: e.activation(hi.ap, src, ACT.Copy), (w, hi.free))
                b = V.put(lambda e: e.tensor_tensor(lo.ap, src, hi.ap.bitcast(fp32), ALU.subtract), (w, a, lo.free))
                hi.t = (a, b)
                return hi, lo, (a, b)

            def drop_pair(x, *toks):
                drop(x[0], *toks)
                drop(x[1], *toks)

            def cols(x, sl):
                return x[0].ap[:, sl], x[1].ap[:, sl]

            FULL = slice(0, 512)

            def project(key, h, groups=1, n=512, bank=None, first=True, last=True, cuts=None):
                wh, wl, wt = weight(key)
                k = len(h)
                if bank is None:
                    bank = get("P")
                for i in range(k):
                    sl = FULL if cuts is None else cuts[i]
                    t = mm3(bank.ap[:, 0:n], (wh[:, i, :], wl[:, i, :]), cols(h[i], sl),
                            first and i == 0, last and i == k - 1, wt, bank.free, h[i][2], inc=(i == k - 1))
                weight_done(t)
                bank.t = t
                return bank

            def project_tok(key, h, width=512, ntok=4, cuts=None):
                bs = [get("P") for _ in range(ntok)]
                for j in range(4):
                    wh, wl, wt = weight(key + (j,))
                    for tq in range(ntok):
                        for kk in range(2):
                            k = 2 * j + kk
                            base = 0 if cuts is None else cuts[k].start
                            sl = slice(base + 128 * tq, base + 128 * tq + 128)
                            t = mm3(bs[tq].ap[:, 0:512], cols(h[k], sl),
                                    (wh[:, 4 * kk:4 * kk + 4, :].rearrange("p a c -> p (a c)"),
                                     wl[:, 4 * kk:4 * kk + 4, :].rearrange("p a c -> p (a c)")),
                                    k == 0, k == 7, wt, bs[tq].free, h[k][2], inc=(kk == 1))
                        bs[tq].t = t
                    weight_done(t)
                return bs

            cst = [dma(CST[:, :, :], ins["cst"]), dma(PAR[:, :], ins["par"])]

            def par(name, i=0, rows=128):
                c = place["par", name] + i
                return PAR[0:rows, c:c + 1]

            def rstd(bank, scale, o, n=512, *w):
                a = ts(V, o, bank.ap[:, 0:n], scale, EPS, ALU.mult, ALU.add, bank.t, w)
                drop(bank, a)
                b = act(o, o, ACT.Sqrt, a)
                return recip(o, o, b)

            class State:
                x = None
                xd = None
                h = None

            st = State()
            xcount = [0]

            def norm_x(gname):
                acc = get()
                sq = None
                for c in range(8):
                    x = st.x[c]
                    if c == 0:
                        ta = act(acc.ap, x.ap, ACT.Square, x.t, acc.free)
                    else:
                        sq = get()
                        t = act(sq.ap, x.ap, ACT.Square, x.t, sq.free)
                        ta = tt(V, acc.ap, acc.ap, sq.ap, ALU.add, t, ta)
                        drop(sq, ta)
                bank = get("P")
                bank.t = mm(bank.ap, ones, acc.ap, True, True, bank.free, ta, cst, inc=True)
                drop(acc, bank.t)
                r = get()
                tr = rstd(bank, 1.0 / DM, r.ap, 512, r.free)
                h = []
                dst = xs[xcount[0] % 2]
                xcount[0] += 1
                st.xd = []
                for c in range(8):
                    x = st.x[c]
                    hf = get()
                    t = stt(hf.ap, x.ap, par(gname, c), r.ap, ALU.mult, ALU.mult, x.t, tr, hf.free, cst)
                    h.append(split(hf.ap, t))
                    drop(hf, h[-1][2])
                    d = dma(dst[c], x.ap, x.t)
                    st.xd.append((dst[c], d))
                    drop(x, t, d)
                drop(r, t)
                st.x = None
                return h

            def load_x(c):
                x = get()
                src, d = st.xd[c]
                x.t = dma(x.ap, src, x.free, d)
                return x

            def drop_h(h, *toks):
                for p in h:
                    drop_pair(p, *toks)

            def add_out(bank, x, *w):
                x.t = tt(V, x.ap, bank.ap, x.ap, ALU.add, bank.t, x.t, w)
                drop(bank, x.t)
                return x

            def run(*gens):
                live = list(gens)
                while live:
                    for g in list(live):
                        try:
                            next(g)
                        except StopIteration:
                            live.remove(g)

            def short_conv(src, st_tok, o, w3, shift):
                mid = shift
                t = ts(V, o, src, w3[mid], None, ALU.mult, None, st_tok, cst)
                for j in range(3):
                    d = j - shift
                    if d == 0:
                        continue
                    if d < 0:
                        t = stt(o[:, -d:512], src[:, 0:512 + d], w3[j], o[:, -d:512], ALU.mult, ALU.add, t)
                    else:
                        t = stt(o[:, 0:512 - d], src[:, d:512], w3[j], o[:, 0:512 - d], ALU.mult, ALU.add, t)
                return t

            def conv_branch(l, h, y):
                for c in range(4):
                    bc = project(("a", l, "cc", c), h)
                    cc = get()
                    t = cp(A, cc.ap, bc.ap, bc.t, cc.free)
                    drop(bc, t)
                    yield
                    bx = project(("a", l, "cx", c), h)
                    tz = tt(V, cc.ap, bx.ap, cc.ap, ALU.mult, bx.t, t)
                    drop(bx, tz)
                    yc = get()
                    V.wait(yc.free)
                    ty = short_conv(cc.ap, tz, yc.ap, [par(f"conv{l}", 4 * j + c) for j in range(3)], 2)
                    drop(cc, ty)
                    yield
                    bg = project(("a", l, "cgate", c), h)
                    sg = get()
                    tg = act(sg.ap, bg.ap, ACT.Silu, bg.t, sg.free)
                    drop(bg, tg)
                    ty = tt(V, yc.ap, yc.ap, sg.ap, ALU.mult, tg, ty)
                    drop(sg, ty)
                    yield
                    bb = project(("a", l, "cb", c), h)
                    ty = tt(V, yc.ap, bb.ap, yc.ap, ALU.mult, bb.t, ty)
                    drop(bb, ty)
                    y.append(split(yc.ap, ty))
                    drop(yc, y[-1][2])
                    yield

            def pool_branch(l, h, y):
                pwt = get()
                pwt.t = dma(pwt.ap, ins["poolw"][l], pwt.free)
                ict = get()
                ict.t = dma(ict.ap[:, 0:64], ins["cnt"], ict.free)
                for g in range(4):
                    w = 2 << g
                    bu = project(("a", l, "pu", g), h)
                    u = get()
                    tu = cp(A, u.ap, bu.ap, bu.t, u.free)
                    drop(bu, tu)
                    src, tsrc = u, tu
                    k = 1
                    while k < w:
                        o = get()
                        a = tt(V, o.ap[:, k:512], src.ap[:, k:512], src.ap[:, 0:512 - k], ALU.add, tsrc, o.free)
                        b = cp(V, o.ap[:, 0:k], src.ap[:, 0:k])
                        if src is not u:
                            drop(src, b)
                        src, tsrc = o, b
                        k *= 2
                    p = get()
                    a = stt(p.ap, src.ap, 1.0 / w, u.ap, ALU.mult, ALU.subtract, tsrc, tu, p.free)
                    b = tt(V, p.ap[:, 0:16], src.ap[:, 0:16], ict.ap[:, 16 * g:16 * g + 16], ALU.mult, a, ict.t)
                    c = tt(V, p.ap[:, 0:16], p.ap[:, 0:16], u.ap[:, 0:16], ALU.subtract, b)
                    drop(src, b)
                    drop(u, c)
                    yield
                    bm = get("P")
                    tm = mm(bm.ap, pwt.ap[:, 128 * g:128 * g + 128], p.ap, True, True, bm.free, c, pwt.t, inc=True)
                    drop(p, tm)
                    bg = project(("a", l, "pgate", g), h)
                    sg = get()
                    tg = act(sg.ap, bg.ap, ACT.Silu, bg.t, sg.free)
                    drop(bg, tg)
                    ty = stt(sg.ap, bm.ap, par(f"pscale{l}", g), sg.ap, ALU.mult, ALU.mult, tm, tg, cst)
                    drop(bm, ty)
                    y.append(split(sg.ap, ty))
                    drop(sg, y[-1][2])
                    yield
                drop(pwt, tm)
                drop(ict, b)

            def rope(bank, cos, sin, rot, g=None, o=None):
                x = get()
                if g is None:
                    t0 = cp(A, x.ap, bank.ap, bank.t, x.free)
                    drop(bank, t0)
                else:
                    sq = get()
                    tsq = act(sq.ap, bank.ap, ACT.Square, bank.t, sq.free)
                    t0 = act(x.ap, bank.ap, ACT.Copy, bank.t, x.free, cst, scale=g)
                    drop(bank, tsq, t0)
                    ss = get("P")
                    ss.t = mm(ss.ap, pair, sq.ap, True, True, ss.free, tsq, cst, inc=True)
                br = get("P")
                tr = mm(br.ap, rot, x.ap, True, True, br.free, t0, cst, inc=True)
                if o is None:
                    o = get()
                t1 = tt(V, o.ap, br.ap, sin.ap, ALU.mult, tr, sin.t, o.free)
                drop(br, t1)
                t2 = tt(V, x.ap, x.ap, cos.ap, ALU.mult, t0, tr, cos.t)
                t3 = tt(V, o.ap, o.ap, x.ap, ALU.add, t1, t2)
                drop(x, t3)
                if g is not None:
                    tn = rstd(ss, 1.0 / 64, sq.ap, 512, ss.t)
                    t3 = tt(V, o.ap, o.ap, sq.ap, ALU.mult, t3, tn)
                    drop(sq, t3)
                o.t = t3
                return o

            def tables(which):
                cos, sin = get(), get()
                cos.t = dma(cos.ap, ins["rope"][which, 0], cos.free)
                sin.t = dma(sin.ap, ins["rope"][which, 1], sin.free)
                return cos, sin

            def head_pair(q, ks, v, vcol, causal_bias, finish):
                ob = get("P")
                sums = get("S")
                first = [True]
                todo = []
                gone = []

                def scores(i, hh):
                    n = 128 * (i + 1) if causal_bias is not None else 512
                    half = slice(64 * hh, 64 * hh + 64)
                    b = get("P")
                    t = mm(b.ap[:, 0:n], q.ap[half, 128 * i:128 * i + 128], ks[hh].ap[half, 0:n], True, True,
                           b.free, q.t, ks[hh].t, inc=True)
                    p = get()
                    m = get("S")
                    if causal_bias is not None:
                        bias, tb = causal_bias[i]
                        t = stt(p.ap[:, 0:n], b.ap[:, 0:n], 0.125, bias, ALU.mult, ALU.add, t, tb, p.free)
                        drop(b, t)
                        tm = V.put(lambda e: e.reduce_max(m.ap[:, 0:1], p.ap[:, 0:n], AX.X, negate=True), (t, m.free))
                        te = act(p.ap[:, 0:n], p.ap[:, 0:n], ACT.Exp, tm, sums.free, bias=m.ap[:, 0:1],
                                 accum_out=sums.ap[:, 2 * i + hh:2 * i + hh + 1])
                    else:
                        tm = V.put(lambda e: e.reduce_max(m.ap[:, 1:2], b.ap[:, 0:n], AX.X, negate=True), (t, m.free))
                        tm = ts(V, m.ap[:, 0:1], m.ap[:, 1:2], 0.125, None, ALU.mult, None, tm)
                        te = act(p.ap[:, 0:n], b.ap[:, 0:n], ACT.Exp, tm, sums.free, p.free, bias=m.ap[:, 0:1],
                                 scale=0.125, accum_out=sums.ap[:, 2 * i + hh:2 * i + hh + 1])
                        drop(b, te)
                    drop(m, te)
                    return i, hh, n, p, te

                def values(i, hh, n, p, te):
                    b = get("P")
                    for k in range(n // 128):
                        t = tp(b.ap[:, 128 * k:128 * k + 128], p.ap[:, 128 * k:128 * k + 128], te, b.free,
                               inc=(k == n // 128 - 1))
                    drop(p, t)
                    pt = get()
                    tc = cp(V if hh else A, pt.ap[:, 0:n], b.ap[:, 0:n], t, pt.free)
                    drop(b, tc)
                    dst = ob.ap[:, 64 * (2 * i + hh):64 * (2 * i + hh) + 64]
                    for k in range(n // 128):
                        t = mm(dst, pt.ap[:, 128 * k:128 * k + 128], v[k].ap[:, vcol[hh]:vcol[hh] + 64],
                               k == 0, k == n // 128 - 1, tc, ob.free, v[k].t, inc=(k == n // 128 - 1))
                    drop(pt, t)
                    ob.t = t
                    gone.append(te)

                units = [(i, hh) for i in range(4) for hh in range(2)]
                for u in units:
                    todo.append(scores(*u))
                    if len(todo) > 2:
                        values(*todo.pop(0))
                    yield
                for u in todo:
                    values(*u)
                    yield
                rs = get("S")
                t = recip(rs.ap[:, 0:8], sums.ap[:, 0:8], gone[-1], rs.free)
                drop(sums, t)
                on = get()
                t = tt(V, on.ap.rearrange("p (u d) -> p u d", d=64), ob.ap.rearrange("p (u d) -> p u d", d=64),
                       rs.ap[:, 0:8].unsqueeze(2).to_broadcast([128, 8, 64]), ALU.mult, t, ob.t, on.free)
                drop(ob, t)
                drop(rs, t)
                b = get("P")
                for i in range(4):
                    tb = tp(b.ap[:, 128 * i:128 * i + 128], on.ap[:, 128 * i:128 * i + 128], t, b.free, inc=(i == 3))
                drop(on, tb)
                b.t = tb
                finish(b, q, ks)
                yield

            def select_keys(l, h, bias):
                cos, sin = tables(0)
                bk = project(("a", l, "ik", 0), h)
                ik = rope(bk, cos, sin, rotA)
                yield
                iw = get("S")
                iw2 = get("S")
                bw = get("P")
                wh, wl, wt = weight(("a", l, "iw", 0))
                for tq in range(4):
                    for k in range(8):
                        sl = slice(128 * tq, 128 * tq + 128)
                        t = mm3(bw.ap[:, 8 * tq:8 * tq + 8], cols(h[k], sl), (wh[:, k, :], wl[:, k, :]),
                                k == 0, k == 7, wt, bw.free, h[k][2], inc=(k == 7))
                weight_done(t)
                sc8 = 8.0 ** -0.5
                a = ts(V, iw.ap[:, 0:16], bw.ap[:, 0:16], sc8, None, ALU.mult, None, t, iw.free)
                b = ts(V, iw2.ap[:, 0:16], bw.ap[:, 16:32], sc8, None, ALU.mult, None, t, iw2.free)
                drop(bw, b)
                tiw = b
                acc = [get() for _ in range(3)]
                yield
                for c in range(4):
                    iq = rope(project(("a", l, "iq", c), h), cos, sin, rotA)
                    yield
                    for hh in range(2):
                        hd = 2 * c + hh
                        half = slice(64 * hh, 64 * hh + 64)
                        for i in range(1, 4):
                            n = 128 * (i + 1)
                            bs = get("P")
                            t = mm(bs.ap[:, 0:n], iq.ap[half, 128 * i:128 * i + 128], ik.ap[half, 0:n], True, True,
                                   bs.free, iq.t, ik.t, inc=True)
                            r = get()
                            tr = act(r.ap[:, 0:n], bs.ap[:, 0:n], ACT.Relu, t, r.free, scale=0.125)
                            drop(bs, tr)
                            z = acc[i - 1]
                            src = (iw if i < 2 else iw2).ap
                            wcol = src[:, 8 * (i % 2) + hd:8 * (i % 2) + hd + 1]
                            if hd == 0:
                                z.t = ts(V, z.ap[:, 0:n], r.ap[:, 0:n], wcol, None, ALU.mult, None, tr, z.free, tiw)
                            else:
                                z.t = stt(z.ap[:, 0:n], r.ap[:, 0:n], wcol, z.ap[:, 0:n], ALU.mult, ALU.add, tr, z.t)
                            drop(r, z.t)
                            yield
                    drop(iq, t)
                drop(ik, t)
                drop(cos, iq.t)
                drop(sin, iq.t)
                m8 = get("S")
                for i in range(1, 4):
                    z = acc[i - 1]
                    n = 128 * (i + 1)
                    za = z.ap[:, 0:n]
                    t = tt(V, z.ap[:, 128 * i:n], z.ap[:, 128 * i:n], causal, ALU.add, z.t, cst)
                    for _ in range(16):
                        t = V.put(lambda e, za=za: e.max(m8.ap[:, 0:8], za), (t, m8.free))
                        t = V.put(lambda e, za=za: e.match_replace(za, m8.ap[:, 0:8], za, GONE), (t,))
                        if _ % 4 == 3:
                            yield
                    t = ts(V, za, za, GONE, NEG, ALU.not_equal, ALU.mult, t)
                    bias[i] = (za, t)
                drop(m8, t)
                drop(iw, z.t)
                drop(iw2, z.t)
                bias["tiles"] = acc

            def attend_first(l, h, y):
                bias = {0: (causal, cst)}
                yield from select_keys(l, h, bias)
                cos, sin = tables(0)
                vb = project_tok(("a", l, "v"), h)
                v = []
                for b in vb:
                    x = get()
                    x.t = cp(A, x.ap, b.ap, b.t, x.free)
                    drop(b, x.t)
                    v.append(x)
                yield

                def qk(c):
                    q = rope(project(("a", l, "q", c), h), cos, sin, rotA, par(f"qg{l}"))
                    k = rope(project(("a", l, "k", c), h), cos, sin, rotA, par(f"kg{l}"))
                    return q, k

                last = []
                nxt = qk(0)
                for c in range(4):
                    q, k = nxt

                    def finish(b, q, ks, c=c):
                        bg = project(("a", l, "agate", c), h)
                        sg = get()
                        tg = act(sg.ap, bg.ap, ACT.Silu, bg.t, sg.free)
                        drop(bg, tg)
                        ty = tt(V, sg.ap, b.ap, sg.ap, ALU.mult, b.t, tg)
                        drop(b, ty)
                        y.append(split(sg.ap, ty))
                        drop(sg, y[-1][2])
                        drop(q, b.t)
                        drop(ks[0], b.t)
                        last.append(b.t)
                        last.append(ty)

                    g = head_pair(q, (k, k), v, (128 * c, 128 * c + 64), bias, finish)
                    step = 0
                    for _ in g:
                        step += 1
                        if step == 4 and c < 3:
                            nxt = qk(c + 1)
                        yield
                for x in v:
                    drop(x, last)
                drop(cos, nxt[1].t)
                drop(sin, nxt[1].t)
                for x in bias["tiles"]:
                    drop(x, last)

            def merge(kind, l, h, ys):
                mg = []
                for c in range(8):
                    m = None
                    for br in range(3):
                        bg = project((kind, l, "gate", 8 * br + c), h)
                        sg = get()
                        tg = act(sg.ap, bg.ap, ACT.Sigmoid, bg.t, sg.free)
                        drop(bg, tg)
                        by = project((kind, l, "br", br, c), ys[br])
                        t = tt(V, sg.ap, by.ap, sg.ap, ALU.mult, by.t, tg)
                        drop(by, t)
                        if m is None:
                            m, tm = sg, t
                        else:
                            tm = tt(G, m.ap, m.ap, sg.ap, ALU.add, tm, t)
                            drop(sg, tm)
                    mg.append(split(m.ap, tm))
                    drop(m, mg[-1][2])
                last = by.t
                drop_h(h, last)
                for y in ys:
                    drop_h(y, last)
                out_product((kind, l, "wo"), mg)

            def out_product(key, y):
                st.x = []
                nxt = load_x(0)
                for c in range(8):
                    x = nxt
                    if c < 7:
                        nxt = load_x(c + 1)
                    b = project(key + (c,), y)
                    st.x.append(add_out(b, x))
                drop_h(y, b.t)

            def block_one(l):
                h = norm_x(f"ng{l}")
                ya, yb, yc = [], [], []
                side = [conv_branch(l, h, ya), pool_branch(l, h, yc)]

                def sides():
                    for g in side:
                        yield from g
                run(attend_first(l, h, yb), slow(sides(), 4))
                merge("a", l, h, (ya, yb, yc))

            def slow(g, k):
                for _ in g:
                    for _ in range(k):
                        yield

            def filters(l, o, hid, R):
                w3 = []
                for d in range(2):
                    w = get()
                    w.t = dma(w.ap[0:65, :], ins["w3"][l, 2 * o + d], w.free)
                    w3.append(w)
                acc = get()
                for tq in range(4):
                    win = get()
                    win.t = dma(win.ap, ins["win"][tq], win.free)
                    fs = []
                    for d in range(2):
                        b = get("P")
                        t = mm(b.ap, hid.ap[0:65, 128 * tq:128 * tq + 128], w3[d].ap[0:65, :], True, True, b.free,
                               hid.t, w3[d].t, inc=True)
                        f = get()
                        f.t = tt(V, f.ap, b.ap, win.ap, ALU.mult, t, win.t, f.free)
                        drop(b, f.t)
                        if d == 1 and tq == 0:
                            f.t = memset(V, f.ap[0:1, :], 0.0, f.t)
                        fs.append(f)
                    drop(win, fs[1].t, fs[0].t)
                    for w in w3:
                        w.free = t
                    s, df = get(), get()
                    ta = tt(V, s.ap, fs[0].ap, fs[1].ap, ALU.add, fs[0].t, fs[1].t, s.free)
                    td = tt(G, df.ap, fs[0].ap, fs[1].ap, ALU.subtract, fs[0].t, fs[1].t, df.free)
                    R[0].append(split(s.ap, ta))
                    drop(s, R[0][-1][2])
                    R[1].append(split(df.ap, td))
                    drop(df, R[1][-1][2])
                    for d in range(2):
                        f = fs[d]
                        if tq == 0 and d == 0:
                            tacc = act(acc.ap, f.ap, ACT.Abs, f.t, acc.free)
                            drop(f, tacc, ta, td)
                        else:
                            t1 = act(f.ap, f.ap, ACT.Abs, f.t, ta, td)
                            tacc = tt(G, acc.ap, acc.ap, f.ap, ALU.add, t1, tacc)
                            drop(f, tacc)
                for w in w3:
                    drop(w, t)
                b = get("P")
                t = mm(b.ap, ones, acc.ap, True, True, b.free, tacc, cst, inc=True)
                t = ts(V, acc.ap, b.ap, EPS, None, ALU.add, None, t)
                drop(b, t)
                t = recip(acc.ap, acc.ap, t)
                acc.t = ts(V, acc.ap, acc.ap, 2.0 / 1024, None, ALU.mult, None, t)
                return acc

            def sine(bank, rows, b1, fr, o, ow):
                n, x = get(), get()
                t = ts(V, x.ap[0:rows], bank.ap[0:rows], b1, fr, ALU.add, ALU.mult, bank.t, x.free, cst)
                drop(bank, t)
                tn = ts(V, n.ap[0:rows], x.ap[0:rows], 1.0 / (2 * np.pi), MAGIC, ALU.mult, ALU.add, t, n.free)
                tn = ts(V, n.ap[0:rows], n.ap[0:rows], MAGIC, None, ALU.subtract, None, tn)
                c1 = 6.28125
                c2 = float(np.float32(2 * np.pi - c1))
                c2 = float(np.frombuffer((np.array([c2], np.float32).view(np.uint32) & np.uint32(0xFFFFF000)).tobytes(), np.float32)[0])
                c3 = float(2 * np.pi - c1 - c2)
                for c in (c1, c2, c3):
                    t = stt(x.ap[0:rows], n.ap[0:rows], -c, x.ap[0:rows], ALU.mult, ALU.add, tn, t)
                t = ts(V, x.ap[0:rows], x.ap[0:rows], 3.1415925, -3.1415925, ALU.min, ALU.max, t)
                t = act(o.ap[0:rows], x.ap[0:rows], ACT.Sin, t, ow)
                drop(x, t)
                drop(n, t)
                return t

            def filter_mlp(l):
                w = get()
                tw = dma(w.ap[0:64, 0:128], ins["w12"][l], w.free)
                z = get()
                tz = dma(z.ap[0:33, :], ins["zpos"], z.free)
                b = get("P")
                b.t = mm(b.ap[0:64, :], w.ap[0:33, 0:64], z.ap[0:33, :], True, True, b.free, tw, tz, inc=True)
                drop(z, b.t)
                h1 = get()
                t = sine(b, 64, par(f"hb1{l}", 0, 64), par(f"hf1{l}", 0, 64), h1, h1.free)
                b = get("P")
                b.t = mm(b.ap[0:64, :], w.ap[0:64, 64:128], h1.ap[0:64, :], True, True, b.free, t, inc=True)
                drop(w, b.t)
                drop(h1, b.t)
                hid = get()
                t1 = memset(V, hid.ap[64:65, :], 1.0, hid.free)
                t2 = sine(b, 64, par(f"hb2{l}", 0, 64), par(f"hf2{l}", 0, 64), hid, hid.free)
                hid.t = (t1, t2)
                return hid

            def conv_chunk(l, part, c, h):
                b = project(("b", l, "hy", 4 * part + c), h)
                s = get()
                t = cp(A, s.ap, b.ap, b.t, s.free)
                drop(b, t)
                o = get()
                V.wait(o.free)
                o.t = short_conv(s.ap, t, o.ap, [par(f"hconv{l}", 12 * j + 4 * part + c) for j in range(3)], 1)
                drop(s, o.t)
                return o

            def to_tokens(fm):
                tm = []
                for i in range(4):
                    b = get("P")
                    for c in range(4):
                        t = tp(b.ap[:, 128 * c:128 * c + 128], fm[c].ap[:, 128 * i:128 * i + 128], fm[c].t, b.free,
                               inc=(c == 3))
                    o = get()
                    o.t = cp(A if i % 2 else V, o.ap, b.ap, t, o.free)
                    drop(b, o.t)
                    tm.append(o)
                for x in fm:
                    drop(x, t)
                return tm

            def spectra(l, o, R, u):
                ur, us = [], []
                for j in range(4):
                    wh, wl, wt = weight(("dft", "f", j, l, o))
                    bk = [get("P") for _ in range(4)]
                    jobs = [(0, u, 0), (1, u, 4), (2, R[0], 0), (3, R[1], 4)]
                    for bi, src, k0 in jobs:
                        for k in range(4):
                            t = mm3(bk[bi].ap, (wh[:, k0 + k, :], wl[:, k0 + k, :]), cols(src[k], FULL), k == 0, k == 3,
                                    wt, bk[bi].free, src[k][2], inc=(k == 3))
                        bk[bi].t = t
                    weight_done(t)
                    fr, fi = get(), get()
                    tr = cp(A, fr.ap, bk[2].ap, bk[2].t, fr.free)
                    ti = cp(A, fi.ap, bk[3].ap, bk[3].t, fi.free)
                    drop(bk[2], tr)
                    drop(bk[3], ti)
                    a, b, c = get(), get(), get()
                    t1 = tt(V, a.ap, bk[0].ap, fr.ap, ALU.mult, bk[0].t, tr, a.free)
                    t2 = tt(V, b.ap, bk[1].ap, fi.ap, ALU.mult, bk[1].t, ti, b.free)
                    t3 = tt(V, c.ap, bk[0].ap, fi.ap, ALU.mult, bk[0].t, ti, c.free)
                    t4 = tt(V, fr.ap, bk[1].ap, fr.ap, ALU.mult, bk[1].t, t1)
                    drop(bk[0], t3)
                    drop(bk[1], t4)
                    drop(fi, t3)
                    t5 = tt(G, a.ap, a.ap, b.ap, ALU.subtract, t1, t2)
                    t6 = tt(G, c.ap, c.ap, fr.ap, ALU.add, t3, t4)
                    drop(b, t5)
                    drop(fr, t6)
                    ur.append(split(a.ap, t5))
                    us.append(split(c.ap, t6))
                    drop(a, ur[-1][2])
                    drop(c, us[-1][2])
                for x in R[0] + R[1] + u:
                    drop_pair(x, t)
                return ur + us

            def hyena(l, h, y):
                hid = filter_mlp(l)
                skb = [get(), get()]
                for i in range(2):
                    skb[i].t = dma(skb[i].ap, ins["skip"][l, i], skb[i].free)
                R = ([], [])
                rn = filters(l, 0, hid, R)
                v = to_tokens([conv_chunk(l, 0, c, h) for c in range(4)])
                vs = [split(x.ap, x.t) for x in v]
                Y = spectra(l, 0, R, vs)
                x1 = to_tokens([conv_chunk(l, 1, c, h) for c in range(4)])
                zs = []
                for j in range(4):
                    b = project(("dft", "i", j, l, 0), Y)
                    t1 = tt(V, b.ap, b.ap, rn.ap, ALU.mult, b.t, rn.t)
                    t2 = tt(G, v[j].ap, v[j].ap, skb[0].ap, ALU.mult, v[j].t, vs[j][2], skb[0].t)
                    t3 = tt(V, v[j].ap, b.ap, v[j].ap, ALU.add, t1, t2)
                    drop(b, t3)
                    t4 = tt(V, v[j].ap, v[j].ap, x1[j].ap, ALU.mult, t3, x1[j].t)
                    v[j].t = t4
                    drop(x1[j], t4)
                for p in Y:
                    drop_pair(p, b.t)
                drop(rn, t3)
                drop(skb[0], t2)
                R = ([], [])
                rn = filters(l, 1, hid, R)
                drop(hid, b.t, R[0][-1][2], hid.t)
                zs = [split(x.ap, x.t) for x in v]
                Y = spectra(l, 1, R, zs)
                for j in range(4):
                    b = project(("dft", "i", j, l, 1), Y)
                    t1 = tt(V, b.ap, b.ap, rn.ap, ALU.mult, b.t, rn.t)
                    t2 = tt(G, v[j].ap, v[j].ap, skb[1].ap, ALU.mult, v[j].t, zs[j][2], skb[1].t)
                    v[j].t = tt(V, v[j].ap, b.ap, v[j].ap, ALU.add, t1, t2)
                    drop(b, v[j].t)
                for p in Y:
                    drop_pair(p, b.t)
                drop(rn, v[3].t)
                drop(skb[1], t2)
                for c in range(4):
                    x2 = conv_chunk(l, 2, c, h)
                    b = get("P")
                    for i in range(4):
                        t = tp(b.ap[:, 128 * i:128 * i + 128], v[i].ap[:, 128 * c:128 * c + 128], v[i].t, b.free,
                               inc=(i == 3))
                    t = tt(V, x2.ap, b.ap, x2.ap, ALU.mult, t, x2.t)
                    drop(b, t)
                    y.append(split(x2.ap, t))
                    drop(x2, y[-1][2])
                for x in v:
                    drop(x, t)

            def attend_second(l, h, y):
                cos, sin = tables(1)
                ks = [rope(project(("b", l, "k", g), h), cos, sin, rotB, par(f"akn{l}")) for g in range(2)]
                wh, wl, wt = weight(("b", l, "v", 0))
                vb = get("P")
                for tq in range(4):
                    for k in range(8):
                        t = mm3(vb.ap[:, 128 * tq:128 * tq + 128], cols(h[k], slice(128 * tq, 128 * tq + 128)),
                                (wh[:, k, :], wl[:, k, :]), k == 0, k == 7, wt, vb.free, h[k][2], inc=(k == 7))
                weight_done(t)
                va = get()
                va.t = cp(A, va.ap, vb.ap, t, va.free)
                drop(vb, va.t)
                v = []
                for tq in range(4):
                    x = Tile(va.ap[:, 128 * tq:128 * tq + 128], "F")
                    x.t = va.t
                    v.append(x)
                yield

                def qc(c):
                    return rope(project(("b", l, "q", c), h), cos, sin, rotB, par(f"aqn{l}"))

                nxt = qc(0)
                last = []
                for c in range(4):
                    q = nxt

                    def finish(b, q, kk):
                        f = get()
                        t = cp(V, f.ap, b.ap, b.t, f.free)
                        drop(b, t)
                        y.append(split(f.ap, t))
                        drop(f, y[-1][2])
                        drop(q, b.t)
                        last.append(b.t)

                    g = c // 2
                    step = 0
                    for _ in head_pair(q, (ks[g], ks[g]), v, (64 * g, 64 * g), None, finish):
                        step += 1
                        if step == 4 and c < 3:
                            nxt = qc(c + 1)
                        yield
                drop(va, last)
                for k in ks:
                    drop(k, last)
                drop(cos, nxt.t)
                drop(sin, nxt.t)

            def gla(l, h, y):
                wl_ = get()
                ta = memset(V, wl_.ap[0:32, :], 0.0, wl_.free)
                t1 = dma(wl_.ap[0:16, 0:256], ins["wlr"][l, 0], ta)
                t2 = dma(wl_.ap[16:32, 256:512], ins["wlr"][l, 1], ta)
                wl_.t = (t1, t2)
                blr = project(("b", l, "lr", 0), h)
                lr = get()
                lr.t = cp(A, lr.ap[0:32, :], blr.ap[0:32, :], blr.t, lr.free)
                drop(blr, lr.t)
                rst = get()
                tm0 = memset(V, rst.ap, 1.0, rst.free)
                rst.t = memset(V, rst.ap.rearrange("p (n c) -> p n c", c=64)[:, :, 0:1], 0.0, tm0)
                yield
                v = []
                for b in project_tok(("b", l, "gv"), h):
                    x = get()
                    x.t = cp(A, x.ap, b.ap, b.t, x.free)
                    drop(b, x.t)
                    v.append(x)
                yield
                for hp in range(2):
                    bq = project(("b", l, "gq", hp), h)
                    q = get()
                    q.t = act(q.ap, bq.ap, ACT.Copy, bq.t, q.free, scale=0.125)
                    drop(bq, q.t)
                    bk = project(("b", l, "gk", hp), h)
                    k = get()
                    k.t = cp(A, k.ap, bk.ap, bk.t, k.free)
                    drop(bk, k.t)
                    yield
                    qd, kinv, sp = [], [], []
                    for d in range(2):
                        b = get("P")
                        t = mm(b.ap, wl_.ap[0:32, 256 * d + 128 * hp:256 * d + 128 * hp + 128], lr.ap[0:32, :],
                               True, True, b.free, wl_.t, lr.t, inc=True)
                        lg, e = get(), get()
                        t = ts(V, lg.ap, b.ap, par(f"glab{l}", 2 * d + hp), None, ALU.add, None, t, lg.free, cst)
                        drop(b, t)
                        te = act(e.ap, lg.ap, ACT.Abs, t, e.free)
                        te = act(e.ap, e.ap, ACT.Exp, te, scale=-1.0)
                        te = act(e.ap, e.ap, ACT.Ln, te, bias=1.0)
                        t = ts(V, lg.ap, lg.ap, 0.0, None, ALU.min, None, t, te)
                        t = tt(V, lg.ap, lg.ap, e.ap, ALU.subtract, t)
                        B = e
                        src, dst = (lg.ap, B.ap) if d == 0 else (lg.ap[:, ::-1], B.ap[:, ::-1])
                        t = V.put(lambda e_, src=src, dst=dst: e_.tensor_tensor_scan(dst, rst.ap, src, 0.0, ALU.mult, ALU.add),
                                  (t, rst.t))
                        B3 = B.ap.rearrange("p (n c) -> p n c", c=64)
                        Bl = B3[:, :, 63:64] if d == 0 else B3[:, :, 0:1]
                        x = get()
                        tx = act(x.ap, B.ap, ACT.Exp, t, x.free, scale=1.0 / 16)
                        x.t = tt(V, x.ap, x.ap, q.ap, ALU.mult, tx, q.t)
                        qd.append(x)
                        x = get()
                        tx = act(x.ap, B.ap, ACT.Exp, t, x.free, scale=-1.0 / 16)
                        x.t = tt(V, x.ap, x.ap, k.ap, ALU.mult, tx, k.t)
                        kinv.append(x)
                        t5 = tt(V, lg.ap.rearrange("p (n c) -> p n c", c=64), Bl.to_broadcast([128, 8, 64]), B3,
                                ALU.subtract, t)
                        t5 = act(lg.ap, lg.ap, ACT.Exp, t5, scale=1.0 / 16)
                        t5 = tt(V, lg.ap, lg.ap, k.ap, ALU.mult, t5)
                        dec = get("S")
                        tdec = act(dec.ap[:, 0:8], Bl.rearrange("p n c -> p (n c)"), ACT.Exp, t, dec.free, scale=1.0 / 16)
                        b = get("P")
                        for i in range(4):
                            t = tp(b.ap[:, 128 * i:128 * i + 128], lg.ap[:, 128 * i:128 * i + 128], t5, b.free, inc=(i == 3))
                        kd = B
                        tk = cp(V, kd.ap, b.ap, t, tdec, qd[-1].t, kinv[-1].t)
                        drop(b, tk)
                        drop(lg, t)
                        bs = [get("P"), get("P")]
                        for n in range(8):
                            rows = slice(64 * (n % 2), 64 * (n % 2) + 64)
                            for hh in range(2):
                                t = mm(bs[n % 2].ap[64 * hh:64 * hh + 64, 128 * (n // 2):128 * (n // 2) + 128],
                                       kd.ap[rows, 128 * (n // 2) + 64 * hh:128 * (n // 2) + 64 * hh + 64],
                                       v[n // 2].ap[rows, 256 * hp + 128 * hh:256 * hp + 128 * hh + 128], True, True,
                                       tk, bs[n % 2].free, v[n // 2].t, inc=(n == 7 and hh == 1))
                        drop(kd, t)
                        sA, sB = get(), get()
                        SS = [(sA if n < 4 else sB).ap[:, 128 * (n % 4):128 * (n % 4) + 128] for n in range(8)]
                        V.wait([sA.free, sB.free])
                        seq = list(range(7)) if d == 0 else list(range(7, 0, -1))
                        ts_ = t
                        for j, n in enumerate(seq):
                            nx = n + 1 if d == 0 else n - 1
                            ds = bs[n % 2].ap[:, 128 * (n // 2):128 * (n // 2) + 128]
                            if j == 0:
                                ts_ = cp(V, SS[nx], ds, ts_)
                            else:
                                ts_ = stt(SS[nx], SS[n], dec.ap[:, n:n + 1], ds, ALU.mult, ALU.add, ts_, tdec)
                        drop(bs[0], ts_)
                        drop(bs[1], ts_)
                        drop(dec, ts_)
                        sp.append((SS, ts_, sA, sB))
                        yield
                    drop(q, qd[1].t)
                    drop(k, t5)
                    for hh in range(2):
                        half = slice(64 * hh, 64 * hh + 64)
                        am = []
                        for d in range(2):
                            b = get("P")
                            for i in range(4):
                                sl = slice(128 * i, 128 * i + 128)
                                t = mm(b.ap[:, sl], kinv[d].ap[half, sl], qd[d].ap[half, sl], True, True, b.free,
                                       kinv[d].t, qd[d].t, inc=(i == 3))
                            x = get()
                            t = ts(V, x.ap, b.ap, BIG, -BIG, ALU.min, ALU.max, t, x.free)
                            drop(b, t)
                            mk = (maskf if d == 0 else maskb).unsqueeze(1).to_broadcast([128, 4, 128])
                            x.t = tt(G, x.ap.rearrange("p (i c) -> p i c", c=128), x.ap.rearrange("p (i c) -> p i c", c=128),
                                     mk, ALU.mult, t, cst)
                            am.append(x)
                        t = tt(G, am[0].ap, am[0].ap, am[1].ap, ALU.add, am[0].t, am[1].t)
                        drop(am[1], t)
                        ob = get("P")
                        e0 = 256 * hp + 128 * hh
                        for i in range(4):
                            tl = mm(ob.ap[:, 128 * i:128 * i + 128], v[i].ap[:, e0:e0 + 128],
                                    am[0].ap[:, 128 * i:128 * i + 128], True, False, t, ob.free, v[i].t)
                            jobs = [(n, d) for n in (2 * i, 2 * i + 1) for d in range(2) if (n, d) not in ((0, 0), (7, 1))]
                            for n, d in jobs:
                                SS, tS = sp[d][0], sp[d][1]
                                tl = mm(ob.ap[:, 64 * n:64 * n + 64], SS[n][half, :], qd[d].ap[half, 64 * n:64 * n + 64],
                                        False, (n, d) == jobs[-1], tS, qd[d].t, inc=(n, d) == jobs[-1])
                        drop(am[0], tl)
                        sq = get()
                        t = act(sq.ap, ob.ap, ACT.Square, tl, sq.free)
                        ss = get("P")
                        ss.t = mm(ss.ap, ones, sq.ap, True, True, ss.free, t, cst, inc=True)
                        tr = rstd(ss, 1.0 / 128, sq.ap, 512, ss.t)
                        ty = stt(sq.ap, ob.ap, par(f"onorm{l}"), sq.ap, ALU.mult, ALU.mult, tr, tl, cst)
                        drop(ob, ty)
                        bg = project(("b", l, "go", 2 * hp + hh), h)
                        sg = get()
                        tg = act(sg.ap, bg.ap, ACT.Silu, bg.t, sg.free)
                        drop(bg, tg)
                        ty = tt(V, sq.ap, sq.ap, sg.ap, ALU.mult, ty, tg)
                        drop(sg, ty)
                        y.append(split(sq.ap, ty))
                        drop(sq, y[-1][2])
                        yield
                    for x in qd + kinv:
                        drop(x, tl)
                    for x in sp:
                        drop(x[2], tl)
                        drop(x[3], tl)
                for x in v + [lr, wl_]:
                    drop(x, tl)
                drop(rst, ts_)

            def memory_side(l):
                mt = []
                acc = get()
                for j in range(4):
                    x = get()
                    x.t = dma(x.ap, ins["mem"][j], x.free)
                    mt.append(x)
                for j in range(4):
                    x = mt[j]
                    if j == 0:
                        ta = act(acc.ap, x.ap, ACT.Square, x.t, acc.free)
                    else:
                        sq = get()
                        t = act(sq.ap, x.ap, ACT.Square, x.t, sq.free)
                        ta = tt(V, acc.ap, acc.ap, sq.ap, ALU.add, t, ta)
                        drop(sq, ta)
                b = get("P")
                mm(b.ap[:, 0:256], ones, acc.ap[:, 0:256], True, False, b.free, ta, cst)
                b.t = mm(b.ap[:, 0:256], ones, acc.ap[:, 256:512], False, True, inc=True)
                tr = rstd(b, 1.0 / DM, acc.ap[:, 0:256], 256, b.t)
                mn, cuts = [], []
                for j in range(4):
                    x = mt[j]
                    for kk in range(2):
                        sl = slice(256 * kk, 256 * kk + 256)
                        t = stt(x.ap[:, sl], x.ap[:, sl], par(f"lnm{l}", 2 * j + kk), acc.ap[:, 0:256], ALU.mult, ALU.mult,
                                tr, x.t, cst)
                    p = split(x.ap, t)
                    drop(x, p[2])
                    mn += [p, p]
                    cuts += [slice(0, 256), slice(256, 512)]
                drop(acc, t)
                yield
                km = []
                for hd in range(4):
                    kt = get()
                    ss = get("P")
                    for kk in range(2):
                        b = project(("b", l, "xk", 2 * hd + kk), mn, n=256, cuts=cuts)
                        sq = get()
                        t = act(sq.ap[:, 0:256], b.ap[:, 0:256], ACT.Square, b.t, sq.free)
                        tk = act(kt.ap[:, 256 * kk:256 * kk + 256], b.ap[:, 0:256], ACT.Copy, b.t, kt.free, cst,
                                 scale=par(f"xkn{l}", kk))
                        drop(b, t, tk)
                        ss.t = mm(ss.ap[:, 0:256], ones, sq.ap[:, 0:256], kk == 0, kk == 1, t, ss.free, cst, inc=True)
                        if kk == 0:
                            drop(sq, ss.t)
                    tr = rstd(ss, 1.0 / 256, sq.ap[:, 0:256], 256, ss.t)
                    for kk in range(2):
                        kt.t = tt(V, kt.ap[:, 256 * kk:256 * kk + 256], kt.ap[:, 256 * kk:256 * kk + 256],
                                  sq.ap[:, 0:256], ALU.mult, tr, tk)
                    drop(sq, kt.t)
                    km.append(kt)
                    yield
                vm = [[None, None], [None, None]]
                for half in range(2):
                    bs = project_tok(("b", l, "xv", half), mn, ntok=2, cuts=cuts)
                    for tq in range(2):
                        x = get()
                        x.t = cp(A, x.ap, bs[tq].ap, bs[tq].t, x.free)
                        drop(bs[tq], x.t)
                        vm[tq][half] = x
                    yield
                for p in mn[::2]:
                    drop_pair(p, bs[1].t)
                st.km, st.vm = km, vm

            def cross(l):
                for _ in memory_side(l):
                    pass
                h = norm_x(f"lnx{l}")
                km, vm = st.km, st.vm
                y = []

                def queries(hd):
                    qs = []
                    ss = get("P")
                    for kk in range(2):
                        b = project(("b", l, "xq", 2 * hd + kk), h)
                        sq = get()
                        t = act(sq.ap, b.ap, ACT.Square, b.t, sq.free)
                        q = get()
                        q.t = act(q.ap, b.ap, ACT.Copy, b.t, q.free, cst, scale=par(f"xqn{l}", kk))
                        drop(b, t, q.t)
                        qs.append(q)
                        ss.t = mm(ss.ap, ones, sq.ap, kk == 0, kk == 1, t, ss.free, cst, inc=True)
                        if kk == 0:
                            drop(sq, ss.t)
                    tr = rstd(ss, 1.0 / 256, sq.ap, 512, ss.t)
                    for q in qs:
                        q.t = tt(V, q.ap, q.ap, sq.ap, ALU.mult, tr, q.t)
                    drop(sq, qs[1].t)
                    return qs

                def score(qs, hd, i):
                    b = get("P")
                    for kk in range(2):
                        t = mm(b.ap[:, 0:256], qs[kk].ap[:, 128 * i:128 * i + 128],
                               km[hd].ap[:, 256 * kk:256 * kk + 256], kk == 0, kk == 1, b.free, qs[kk].t, km[hd].t,
                               inc=(kk == 1))
                    m, p = get("S"), get()
                    tm = V.put(lambda e: e.reduce_max(m.ap[:, 1:2], b.ap[:, 0:256], AX.X, negate=True), (t, m.free))
                    tm = ts(V, m.ap[:, 0:1], m.ap[:, 1:2], 1.0 / 16, None, ALU.mult, None, tm)
                    te = act(p.ap[:, 0:256], b.ap[:, 0:256], ACT.Exp, tm, p.free, bias=m.ap[:, 0:1], scale=1.0 / 16,
                             accum_out=m.ap[:, 2:3])
                    drop(b, te)
                    tr = recip(m.ap[:, 3:4], m.ap[:, 2:3], te)
                    tp_ = ts(V, p.ap[:, 0:256], p.ap[:, 0:256], m.ap[:, 3:4], None, ALU.mult, None, tr, te)
                    drop(m, tp_)
                    p.t = tp_
                    return p

                nxt = queries(0)
                for hd in range(4):
                    qs = nxt
                    ps = [score(qs, hd, i) for i in range(4)]
                    if hd < 3:
                        nxt = queries(hd + 1)
                    bt = [get("P"), get("P")]
                    for kk in range(2):
                        for i in range(4):
                            t = tp(bt[kk].ap[:, 128 * i:128 * i + 128], ps[i].ap[:, 128 * kk:128 * kk + 128], ps[i].t,
                                   bt[kk].free, inc=(i == 3))
                        bt[kk].t = t
                    for p in ps:
                        drop(p, t)
                    for q in qs:
                        drop(q, t)
                    pt = []
                    for kk in range(2):
                        x = get()
                        x.t = cp((V, A)[kk], x.ap, bt[kk].ap, bt[kk].t, x.free)
                        drop(bt[kk], x.t)
                        pt.append(x)
                    for dc in range(2):
                        f = 256 * hd + 128 * dc
                        b = get("P")
                        for kk in range(2):
                            vv = vm[kk][f // 512]
                            t = mm(b.ap, vv.ap[:, f % 512:f % 512 + 128], pt[kk].ap, kk == 0, kk == 1, b.free, vv.t,
                                   pt[kk].t, inc=(kk == 1))
                        o = get()
                        to = cp(V, o.ap, b.ap, t, o.free)
                        drop(b, to)
                        y.append(split(o.ap, to))
                        drop(o, y[-1][2])
                    for x in pt:
                        drop(x, t)
                for x in km + vm[0] + vm[1]:
                    drop(x, t)
                drop_h(h, t)
                out_product(("b", l, "xo"), y)

            def mlp(l):
                h = norm_x(f"lnp{l}")
                xn = []
                for half in range(2):
                    y = []
                    for c in range(16):
                        b = project(("b", l, "w1", 16 * half + c), h)
                        r = get()
                        t = act(r.ap, b.ap, ACT.Relu, b.t, r.free)
                        drop(b, t)
                        t = tt(G, r.ap, r.ap, r.ap, ALU.mult, t)
                        y.append(split(r.ap, t))
                        drop(r, y[-1][2])
                    if half == 1:
                        drop_h(h, b.t)
                    if half == 0:
                        nxt = load_x(0)
                    for c in range(8):
                        if half == 0:
                            x = nxt
                            if c < 7:
                                nxt = load_x(c + 1)
                        else:
                            x = xn[c]
                        b = project(("b", l, "w2", c, 2 * half), y[0:8], last=False)
                        b = project(("b", l, "w2", c, 2 * half + 1), y[8:16], bank=b, first=False)
                        add_out(b, x)
                        if half == 0:
                            xn.append(x)
                    drop_h(y, b.t)
                st.x = xn

            def mix_second(l):
                h = norm_x(f"lnmix{l}")
                ya, yb, yc = [], [], []
                hyena(l, h, yb)
                for _ in attend_second(l, h, ya):
                    pass
                for _ in gla(l, h, yc):
                    pass
                merge("b", l, h, (ya, yb, yc))

            st.x = []
            for c in range(8):
                x = get()
                x.t = dma(x.ap, ins["x"][c], x.free)
                st.x.append(x)
            todo = [lambda l=l: block_one(l) for l in range(2)]
            for l in range(2):
                todo += [lambda l=l: mix_second(l), lambda l=l: cross(l), lambda l=l: mlp(l)]
            for f in todo[:steps]:
                f()
            for c in range(8):
                x = st.x[c]
                S.put(lambda e, c=c, x=x: e.dma_start(out[c], x.ap).then_inc(s_out, 16), x.t, inc=False)
            S.wait(Tok(s_out, 128))
            for i in range(len(s_misc)):
                S.wait(Tok(s_misc[i], 16 * mcount[i]))
            assert len(pools["F"]) == NF - 8 and len(pools["R"]) == NRT and len(pools["P"]) == 8, \
                {k: len(p) for k, p in pools.items()}
            return asked, (M, V, A, G, S)

        order, _ = emit(None)
        _, (M, V, A, G, S) = emit(order)

        block = ctx.enter_context(nc.Block())

        @block.tensor
        def _(e):
            M.play(e)

        @block.vector
        def _(e):
            V.play(e)

        @block.scalar
        def _(e):
            A.play(e)

        @block.gpsimd
        def _(e):
            G.play(e)

        @block.sync
        def _(e):
            S.play(e)


def tables():
    f = np.float32
    k = {}
    cst = np.zeros((128, 8, 128), f)
    p = np.arange(128)
    cst[:, 0] = np.eye(128)
    cst[:, 1] = 1
    cst[:, 2] = (p[:, None] // 64) == (p[None, :] // 64)
    for m in range(128):
        if m % 64 < 32:
            cst[m + 32, 3, m] = -1
        else:
            cst[m - 32, 3, m] = 1
        if m % 32 < 16:
            cst[m + 16, 4, m] = -1
        else:
            cst[m - 16, 4, m] = 1
    cst[:, 5] = np.where(p[None, :] <= p[:, None], 0, NEG)
    same = (p[:, None] // 64) == (p[None, :] // 64)
    cst[:, 6] = same & (p[:, None] <= p[None, :])
    cst[:, 7] = same & (p[:, None] > p[None, :])
    k["cst"] = cst
    rope = np.zeros((2, 2, 128, 512), f)
    inv = (f(1.0) / (f(10000.0) ** (np.arange(0, 64, 2, dtype=f) / f(64)))).astype(f)
    ang = np.arange(512, dtype=f)[:, None] * inv[None, :]
    rope[0, 0] = np.cos(ang).T[(p % 64) % 32]
    rope[0, 1] = np.sin(ang).T[(p % 64) % 32]
    inv = (f(10000.0) ** (-np.arange(16, dtype=f) / f(16))).astype(f)
    t = np.arange(512)
    pos = np.stack([t // 64, t % 64], 1).astype(f)
    ang = (pos[:, :, None] * inv).astype(f)
    q = p % 64
    rope[1, 0] = np.cos(ang)[:, q // 32, q % 16].T
    rope[1, 1] = np.sin(ang)[:, q // 32, q % 16].T
    k["rope"] = rope
    cnt = np.zeros((4, 16), f)
    for g in range(4):
        cnt[g] = f(1) / np.minimum(np.arange(16) + 1, 2 << g).astype(f)
    k["cnt"] = np.broadcast_to(cnt.reshape(1, 64), (128, 64)).copy()
    L = 512
    tn = np.arange(L, dtype=f) / f(L - 1)
    w = (f(2.0 * np.pi) * np.arange(L, dtype=f) / f(L)).astype(f)
    fr = np.linspace(1e-4, 15, 16, dtype=f)
    fw = w[:, None] * fr
    k["zpos"] = np.concatenate([tn[:, None], np.cos(fw), -np.sin(fw)], -1).T.astype(f).copy()
    deltas = np.abs(np.linspace(np.log(1e-2) / 0.3, np.log(1e-2) / 1.5, 512, dtype=f))
    k["win"] = np.exp(-tn[:, None] * deltas).astype(f).reshape(4, 128, 512)
    om = 2 * np.pi * (np.arange(512) + 0.5) / 1024
    a = np.arange(512)[:, None] * om[None, :]
    k["C"], k["Sn"] = np.cos(a).astype(f), np.sin(a).astype(f)
    return k


def layout(x):
    k = tables()
    place = {}
    ins = {n: k[n] for n in ("cst", "rope", "cnt", "zpos", "win")}
    flat = {}

    def fm(w):
        n = w.shape[0] // 128
        return w.reshape(n, 128, w.shape[1]).transpose(1, 0, 2)

    def add(arr, key, w):
        lst = flat.setdefault(arr, [0, []])
        n, cols = w.shape[1], w.shape[2]
        place[key] = (arr, lst[0], n, cols)
        lst[0] += w.size
        lst[1].append(np.ascontiguousarray(w).reshape(-1))

    def chunks(arr, l, name, w, c0=0):
        for c in range(w.shape[1] // 128):
            add(arr, (arr[1], l, name, c0 + c), fm(w[:, 128 * c:128 * c + 128]))

    def tok(arr, key, w):
        for j in range(4):
            v = w[256 * j:256 * j + 256].reshape(2, 128, 512).transpose(1, 0, 2).reshape(128, 8, 128)
            add(arr, key + (j,), v)

    for l in range(2):
        w = x["w_in"][l]
        arr = f"wa{l}"
        names = ["cb", "cc", "cx", "cgate", "q", "k", "v", "agate"]
        for i, n in enumerate(names):
            s = w[:, 512 * i:512 * i + 512]
            if n == "v":
                tok(arr, ("a", l, "v"), s)
            else:
                chunks(arr, l, n, s)
        chunks(arr, l, "iq", w[:, 4096:4608])
        ik = w[:, 4608:4672]
        add(arr, ("a", l, "ik", 0), fm(np.concatenate([ik, ik], 1)))
        add(arr, ("a", l, "iw", 0), fm(w[:, 4672:4680]))
        chunks(arr, l, "pu", w[:, 4680:5192])
        chunks(arr, l, "pgate", w[:, 5192:5704])
        chunks(arr, l, "gate", w[:, 5704:8776])
        for br, n in enumerate(("w_out_conv", "w_out_attn", "w_out_pool")):
            for c in range(8):
                add(arr, ("a", l, "br", br, c), fm(x[n][l][:, 128 * c:128 * c + 128]))
        chunks(arr, l, "wo", x["w_o"][l])
        w = x["w_in_2"][l]
        arr = f"wb{l}"
        chunks(arr, l, "q", w[:, 0:512])
        for g in range(2):
            kk = w[:, 512 + 64 * g:576 + 64 * g]
            add(arr, ("b", l, "k", g), fm(np.concatenate([kk, kk], 1)))
        add(arr, ("b", l, "v", 0), fm(w[:, 640:768]))
        chunks(arr, l, "hy", w[:, 768:2304])
        chunks(arr, l, "gq", w[:, 2304:2560])
        chunks(arr, l, "gk", w[:, 2560:2816])
        tok(arr, ("b", l, "gv"), w[:, 2816:3328])
        chunks(arr, l, "go", w[:, 3328:3840])
        lr = w[:, 3840:3872]
        add(arr, ("b", l, "lr", 0), fm(np.concatenate([lr] * 4, 1)))
        chunks(arr, l, "gate", w[:, 3872:6944])
        for br, n in enumerate(("w_br_attn_2", "w_br_hyena_2", "w_br_gla_2")):
            for c in range(8):
                add(arr, ("b", l, "br", br, c), fm(x[n][l][:, 128 * c:128 * c + 128]))
        chunks(arr, l, "wo", x["w_out_2"][l])
        chunks(arr, l, "xq", x["x_wq_2"][l])
        chunks(arr, l, "xk", x["x_wk_2"][l])
        for half in range(2):
            tok(arr, ("b", l, "xv", half), x["x_wv_2"][l][:, 512 * half:512 * half + 512])
        chunks(arr, l, "xo", x["x_wo_2"][l])
        chunks(arr, l, "w1", x["mlp_w1_2"][l])
        for c in range(8):
            for g in range(4):
                add(arr, ("b", l, "w2", c, g), fm(x["mlp_w2_2"][l][1024 * g:1024 * g + 1024, 128 * c:128 * c + 128]))
    for j in range(4):
        sl = slice(128 * j, 128 * j + 128)
        add("wd", ("dft", "f", j), np.concatenate([fm(k["C"][:, sl]), fm(k["Sn"][:, sl])], 1))
        add("wd", ("dft", "i", j), np.concatenate([fm(k["C"].T[:, sl]), fm(k["Sn"].T[:, sl])], 1))
        for d in "fi":
            for l in range(2):
                for o in range(2):
                    place["dft", d, j, l, o] = place["dft", d, j]
    for arr, (_, lst) in flat.items():
        ins[arr] = np.concatenate(lst)
    par = []

    def col(name, a):
        place["par", name] = sum(q.shape[1] for q in par)
        b = np.zeros((128, a.shape[1]), np.float32)
        b[0:a.shape[0]] = a
        par.append(b)

    def vec(name, a):
        col(name, a.reshape(-1, 128).T)

    for l in range(2):
        vec(f"ng{l}", x["norm_g"][l])
        vec(f"conv{l}", x["conv_w"][l])
        col(f"qg{l}", np.concatenate([x["q_norm_g"][l]] * 2)[:, None])
        col(f"kg{l}", np.concatenate([x["k_norm_g"][l]] * 2)[:, None])
        vec(f"pscale{l}", x["pool_scale"][l])
        vec(f"lnmix{l}", x["ln_mix_2"][l])
        col(f"aqn{l}", np.concatenate([x["attn_qnorm_2"][l]] * 2)[:, None])
        col(f"akn{l}", np.concatenate([x["attn_knorm_2"][l]] * 2)[:, None])
        vec(f"hconv{l}", x["hy_conv_2"][l])
        col(f"hb1{l}", x["hy_b1_2"][l][:, None])
        col(f"hb2{l}", x["hy_b2_2"][l][:, None])
        col(f"hf1{l}", x["hy_freq_2"][l, 0][:, None])
        col(f"hf2{l}", x["hy_freq_2"][l, 1][:, None])
        vec(f"glab{l}", x["gla_b_lr_2"][l])
        vec(f"onorm{l}", x["gla_onorm_2"][l])
        vec(f"lnx{l}", x["ln_x_2"][l])
        vec(f"lnm{l}", x["ln_mem_2"][l])
        vec(f"xqn{l}", x["x_qnorm_2"][l])
        vec(f"xkn{l}", x["x_knorm_2"][l])
        vec(f"lnp{l}", x["ln_mlp_2"][l])
    n = sum(q.shape[1] for q in par)
    par.append(np.zeros((128, PB_COLS - n), np.float32))
    ins["par"] = np.concatenate(par, 1)
    ins["poolw"] = x["pool_w"].transpose(0, 2, 1, 3).reshape(2, 128, 512)
    ins["skip"] = np.broadcast_to(x["hy_skip_2"][:, :, None, :], (2, 2, 128, 512))
    w12 = np.zeros((2, 64, 128), np.float32)
    w12[:, 0:33, 0:64] = x["hy_w1_2"]
    w12[:, :, 64:128] = x["hy_w2_2"]
    ins["w12"] = w12
    w3 = np.concatenate([x["hy_w3_2"], x["hy_b3_2"][:, None, :]], 1)
    ins["w3"] = w3.reshape(2, 65, 4, 512).transpose(0, 2, 1, 3)
    ins["wlr"] = x["gla_w_lr_2"]
    ins["mem"] = x["mem_2"][0].T.reshape(4, 2, 128, 256).transpose(0, 2, 1, 3).reshape(4, 128, 512)
    ins["x"] = x["x"][0].T.reshape(8, 128, 512)
    return {n: np.ascontiguousarray(a) for n, a in ins.items()}, place


def kernel(**inputs):
    import concourse.bacc as _bacc
    from concourse.bass_utils import run_bass_kernel_spmd as _run

    arrays, place = layout({n: np.asarray(a) for n, a in inputs.items()})
    nc = _bacc.Bacc("TRN2", target_bir_lowering=False, num_devices=1)
    aps = {n: nc.dram_tensor(f"in_{n}", a.shape, mybir.dt.from_np(a.dtype), kind="ExternalInput").ap()
           for n, a in arrays.items()}
    out = nc.dram_tensor("out_x", [8, 128, 512], mybir.dt.float32, kind="ExternalOutput").ap()
    program(nc, aps, place, out)
    r = _run(nc, [{f"in_{n}": a for n, a in arrays.items()}], core_ids=[0])
    o = np.asarray(r.results[0]["out_x"])
    return np.ascontiguousarray(o.reshape(1024, 512).T).reshape(1, 512, 1024)
```

```python
import numpy as np
import concourse.bass as bass
from concourse import mybir
from contextlib import ExitStack

SEQ = 512
DM = 1024
EPS = 1e-6
NEG = -1e30
GONE = -3e38
BIG = 3e38
MAGIC = 12582912.0

NF = 26
NRT = 56
NRAW = 3
NSP = 3
PB_COLS = 64 + 2 * 26 + 2 * 84


def program(nc, ins, place, out, steps=8):
    fp32 = mybir.dt.float32
    fp32r = mybir.dt.float32r
    ALU = mybir.AluOpType
    ACT = mybir.ActivationFunctionType
    AX = mybir.AxisListType

    ctx = ExitStack()
    with ctx:
        def sb(name, shape, dt=fp32):
            return ctx.enter_context(nc.sbuf_tensor(name, shape, dt))

        FT = sb("FT", [128, NF, 512])
        RT = sb("RT", [128, NRT, 512], fp32r)
        WRAW = sb("WRAW", [128, NRAW, 1024])
        WSP = sb("WSP", [128, NSP, 2, 1024], fp32r)
        CST = sb("CST", [128, 8, 128])
        PAR = sb("PAR", [128, PB_COLS])
        EPSC = sb("EPSC", [128, 2])
        SM = sb("SM", [128, 16, 16])
        banks = [ctx.enter_context(nc.psum_tensor(f"B{i}", [128, 512], fp32)) for i in range(8)]
        xs = [nc.dram_tensor(f"xs{i}", [8, 128, 512], fp32, kind="Internal").ap() for i in range(2)]

        eye, ones, pair = CST[:, 0, :], CST[:, 1, :], CST[:, 2, :]
        rotA, rotB, causal = CST[:, 3, :], CST[:, 4, :], CST[:, 5, :]
        maskf, maskb = CST[:, 6, :], CST[:, 7, :]

        class Tok:
            __slots__ = ("sem", "val")

            def __init__(self, sem, val):
                self.sem, self.val = sem, val

        class Queue:

            def __init__(self, sem):
                self.sem, self.n, self.q, self.seen = sem, 0, [], {}

            def wait(self, w):
                if w is None:
                    return
                if isinstance(w, Tok):
                    if self.seen.get(w.sem, 0) < w.val:
                        self.seen[w.sem] = w.val
                        self.q.append(("w", w.sem, w.val))
                    return
                for x in w:
                    self.wait(x)

            def put(self, fn, w, inc=True):
                best = {}

                def flat(t):
                    if t is None:
                        return
                    if isinstance(t, Tok):
                        if best.get(t.sem, 0) < t.val:
                            best[t.sem] = t.val
                        return
                    for x in t:
                        flat(x)
                flat(w)
                for s, v in best.items():
                    self.wait(Tok(s, v))
                if not inc:
                    self.q.append(("i", fn, None, 0))
                    return None
                self.n += 1
                self.q.append(("i", fn, self.sem, 1))
                return Tok(self.sem, self.n)

            def play(self, e):
                for it in self.q:
                    if it[0] == "w":
                        e.wait_ge(it[1], it[2])
                    else:
                        r = it[1](e)
                        if it[2] is not None:
                            r.then_inc(it[2], it[3])

        sems = [ctx.enter_context(nc.semaphore(f"s_{n}")) for n in ("pe", "dve", "act", "pool", "sp")]
        s_raw = [ctx.enter_context(nc.semaphore(f"s_raw{i}")) for i in range(NRAW)]
        s_misc = [ctx.enter_context(nc.semaphore(f"s_misc{i}")) for i in range(24)]
        s_out = ctx.enter_context(nc.semaphore("s_out"))

        class Tile:
            __slots__ = ("ap", "free", "t", "kind", "last")

            def __init__(self, ap, kind):
                self.ap, self.free, self.t, self.kind = ap, None, None, kind

        def emit(order, plan):
            rates = []
            M, V, A, G, S = (Queue(s) for s in sems)
            pools = {
                "F": [Tile(FT[:, i, :], "F") for i in range(NF)],
                "R": [Tile(RT[:, i, :], "R") for i in range(NRT)],
                "P": [Tile(b[:, :], "P") for b in banks],
                "S": [Tile(SM[:, i, :], "S") for i in range(16)],
            }

            def get(kind="F"):
                assert pools[kind], "no tile left: " + kind
                old = pools[kind].pop(0)
                new = Tile(old.ap, kind)
                new.free = old.free
                return new

            def drop(tile, *toks):
                tile.free = [x for x in toks]
                pools[tile.kind].append(tile)

            def tt(E, o, a, b, op, *w):
                return E.put(lambda e: e.tensor_tensor(o, a, b, op), w)

            def ts(E, o, a, s1, s2, op0, op1, *w):
                if s2 is None:
                    return E.put(lambda e: e.tensor_scalar(o, a, s1, None, op0), w)
                return E.put(lambda e: e.tensor_scalar(o, a, s1, s2, op0, op1), w)

            def stt(o, a, s, b, op0, op1, *w):
                return V.put(lambda e: e.scalar_tensor_tensor(o, a, s, b, op0, op1), w)

            def cp(E, o, a, *w):
                if E is A:
                    return A.put(lambda e: e.activation(o, a, ACT.Copy), w)
                return E.put(lambda e: e.tensor_copy(o, a), w)

            def act(o, a, f, *w, **k):
                return A.put(lambda e: e.activation(o, a, f, **k), w)

            def recip(o, a, *w):
                return V.put(lambda e: e.reciprocal(o, a), w)

            def memset(E, o, v, *w):
                return E.put(lambda e: e.memset(o, v), w)

            work = [0.0]

            def mm(o, l, r, start, stop, *w, inc=False):
                work[0] += r.free_size() * (4 if r.dtype == fp32 else 1)
                return M.put(lambda e: e.matmul(o, l, r, start=start, stop=stop), w, inc)

            def tp(o, a, *w, inc=False):
                return M.put(lambda e: e.transpose(o, a, eye[0:a.shape[0], 0:a.shape[0]]), (w, cst), inc)

            misc = [0]
            mcount = [0] * len(s_misc)

            def dma(o, a, *w):
                i = misc[0] % len(s_misc)
                misc[0] += 1
                S.wait(Tok(s_misc[i], mcount[i] * 16))
                S.put(lambda e: e.dma_start(o, a).then_inc(s_misc[i], 16), w, inc=False)
                mcount[i] += 1
                return Tok(s_misc[i], mcount[i] * 16)

            asked = []
            raw_free = [None] * NRAW
            sp_free = [None] * NSP
            state = {"issued": 0, "used": 0}
            ready = {}

            def issue(i):
                arr, off, n, cols = place[order[i]]
                r, s = i % NRAW, i % NSP
                m = n * cols
                src = ins[arr][off:off + 128 * m].rearrange("(p m) -> p m", p=128)
                dst = WRAW[:, r, 0:m]
                S.put(lambda e: e.dma_start(dst, src).then_inc(s_raw[r], 16), raw_free[r], inc=False)
                t = Tok(s_raw[r], 16 * (i // NRAW + 1))
                hi, lo = WSP[:, s, 0, 0:m], WSP[:, s, 1, 0:m]
                a = A.put(lambda e: e.activation(hi, dst, ACT.Copy), (t, sp_free[s]))
                E = G if i % 3 == 1 else V
                b = E.put(lambda e: e.tensor_tensor(lo, dst, hi.bitcast(fp32), ALU.subtract), (t, a, sp_free[s]))
                raw_free[r] = (a, b)
                ready[i] = (hi.rearrange("p (n c) -> p n c", n=n), lo.rearrange("p (n c) -> p n c", n=n), (a, b))

            def weight(key):
                i = state["used"]
                state["used"] += 1
                asked.append(key)
                if order is None:
                    arr, off, n, cols = place[key]
                    z = WSP[:, 0, 0, 0:n * cols].rearrange("p (n c) -> p n c", n=n)
                    return z, z, None
                assert order[i] == key
                while state["issued"] < min(i + NSP, len(order)):
                    issue(state["issued"])
                    state["issued"] += 1
                return ready.pop(i)

            def weight_done(tok):
                sp_free[(state["used"] - 1) % NSP] = tok

            def mm3(o, L, R, first, last, *w, inc=False):
                mm(o, L[0], R[0], first, False, w)
                mm(o, L[0], R[1], False, False)
                return mm(o, L[1], R[0], False, last, inc=inc)

            def split(src, *w, E=None):
                hi, lo = get("R"), get("R")
                a = A.put(lambda e: e.activation(hi.ap, src, ACT.Copy), (w, hi.free))
                b = (E or V).put(lambda e: e.tensor_tensor(lo.ap, src, hi.ap.bitcast(fp32), ALU.subtract), (w, a, lo.free))
                hi.t = (a, b)
                return hi, lo, (a, b)

            def drop_pair(x, *toks):
                drop(x[0], *toks)
                drop(x[1], *toks)

            def cols(x, sl):
                return x[0].ap[:, sl], x[1].ap[:, sl]

            FULL = slice(0, 512)

            def project(key, h, groups=1, n=512, bank=None, first=True, last=True, cuts=None):
                wh, wl, wt = weight(key)
                k = len(h)
                if bank is None:
                    bank = get("P")
                ta, tb = wt or (None, None)
                for part in range(3):
                    for i in range(k):
                        sl = FULL if cuts is None else cuts[i]
                        ha, hb = h[i][2]
                        w = ((ta, ha, bank.free), (tb, ha), (ta, hb))[part]
                        t = mm(bank.ap[:, 0:n], (wh, wl, wh)[part][:, i, :], h[i][part // 2].ap[:, sl],
                               first and part == 0 and i == 0, last and part == 2 and i == k - 1, w,
                               inc=(part == 2 and i == k - 1))
                weight_done(t)
                bank.t = t
                return bank

            def project_tok(key, h, width=512, ntok=4, cuts=None):
                bs = [get("P") for _ in range(ntok)]
                for j in range(4):
                    wh, wl, wt = weight(key + (j,))
                    for tq in range(ntok):
                        for kk in range(2):
                            k = 2 * j + kk
                            base = 0 if cuts is None else cuts[k].start
                            sl = slice(base + 128 * tq, base + 128 * tq + 128)
                            t = mm3(bs[tq].ap[:, 0:512], cols(h[k], sl),
                                    (wh[:, 4 * kk:4 * kk + 4, :].rearrange("p a c -> p (a c)"),
                                     wl[:, 4 * kk:4 * kk + 4, :].rearrange("p a c -> p (a c)")),
                                    k == 0, k == 7, wt, bs[tq].free, h[k][2], inc=(kk == 1))
                        bs[tq].t = t
                    weight_done(t)
                return bs

            cst = [dma(CST[:, :, :], ins["cst"]), dma(PAR[:, :], ins["par"])]

            eps, eps2 = EPSC[:, 0:1], EPSC[:, 1:2]
            teps = memset(V, eps, EPS)

            def par(name, i=0, rows=128):
                c = place["par", name] + i
                return PAR[0:rows, c:c + 1]

            def rstd(bank, scale, o, n=512, *w):
                b = act(o, bank.ap[:, 0:n], ACT.Sqrt, bank.t, w, teps, scale=scale, bias=eps)
                drop(bank, b)
                return recip(o, o, b)

            class State:
                x = None
                xd = None
                h = None

            st = State()
            xcount = [0]

            def norm_x(gname, fill=None):
                return norm_x_(gname, fill or Aux(None))

            def norm_x_(gname, fill):
                acc = get()
                sq = None
                for c in range(8):
                    x = st.x[c]
                    if c == 0:
                        ta = act(acc.ap, x.ap, ACT.Square, x.t, acc.free)
                    else:
                        sq = get()
                        if c == 7:
                            act(eps2, eps, ACT.Sqrt, teps)
                        t = act(sq.ap, x.ap, ACT.Square, x.t, sq.free)
                        ta = tt(V, acc.ap, acc.ap, sq.ap, ALU.add, t, ta)
                        drop(sq, ta)
                fill.step()
                bank = get("P")
                bank.t = mm(bank.ap, ones, acc.ap, True, True, bank.free, ta, cst, inc=True)
                drop(acc, bank.t)
                r = get()
                tr = rstd(bank, 1.0 / DM, r.ap, 512, r.free)
                h = []
                dst = xs[xcount[0] % 2]
                xcount[0] += 1
                st.xd = []
                for c in range(8):
                    x = st.x[c]
                    hf = get()
                    t = stt(hf.ap, x.ap, par(gname, c), r.ap, ALU.mult, ALU.mult, x.t, tr, hf.free, cst)
                    h.append(split(hf.ap, t, E=G if c % 2 else V))
                    drop(hf, h[-1][2])
                    d = dma(dst[c], x.ap, x.t)
                    st.xd.append((dst[c], d))
                    drop(x, t, d)
                drop(r, t)
                st.x = None
                return h

            def load_x(c):
                x = get()
                src, d = st.xd[c]
                x.t = dma(x.ap, src, x.free, d)
                return x

            def drop_h(h, *toks):
                for p in h:
                    drop_pair(p, *toks)

            def add_out(bank, x, *w):
                x.t = tt(V, x.ap, bank.ap, x.ap, ALU.add, bank.t, x.t, w)
                drop(bank, x.t)
                return x

            class Aux:

                def __init__(self, gen):
                    self.gen, self.done, self.val = gen, gen is None, None

                def step(self):
                    if not self.done:
                        try:
                            next(self.gen)
                        except StopIteration as e:
                            self.done, self.val = True, e.value

            def beside(main, side):
                i = len(rates)
                rates.append(None)
                rate = plan[i] if plan is not None else 0.0
                side = Aux(side)
                steps, credit, total = 0, 0.0, 0.0
                for room in main:
                    room = 1 if room is None else room
                    steps += room
                    credit += rate * room
                    while credit > 0 and not side.done:
                        w0 = work[0]
                        side.step()
                        credit -= work[0] - w0
                        total += work[0] - w0
                while not side.done:
                    w0 = work[0]
                    side.step()
                    total += work[0] - w0
                rates[i] = total / max(steps, 1)

            def short_conv(src, st_tok, o, w3, shift):
                mid = shift
                t = ts(V, o, src, w3[mid], None, ALU.mult, None, st_tok, cst)
                for j in range(3):
                    d = j - shift
                    if d == 0:
                        continue
                    if d < 0:
                        t = stt(o[:, -d:512], src[:, 0:512 + d], w3[j], o[:, -d:512], ALU.mult, ALU.add, t)
                    else:
                        t = stt(o[:, 0:512 - d], src[:, d:512], w3[j], o[:, 0:512 - d], ALU.mult, ALU.add, t)
                return t

            def conv_branch(l, h, y):
                for c in range(4):
                    bc = project(("a", l, "cc", c), h)
                    cc = get()
                    t = cp(A, cc.ap, bc.ap, bc.t, cc.free)
                    drop(bc, t)
                    yield
                    bx = project(("a", l, "cx", c), h)
                    tz = tt(V, cc.ap, bx.ap, cc.ap, ALU.mult, bx.t, t)
                    drop(bx, tz)
                    yc = get()
                    V.wait(yc.free)
                    ty = short_conv(cc.ap, tz, yc.ap, [par(f"conv{l}", 4 * j + c) for j in range(3)], 2)
                    drop(cc, ty)
                    yield
                    bg = project(("a", l, "cgate", c), h)
                    sg = get()
                    tg = act(sg.ap, bg.ap, ACT.Silu, bg.t, sg.free)
                    drop(bg, tg)
                    ty = tt(V, yc.ap, yc.ap, sg.ap, ALU.mult, tg, ty)
                    drop(sg, ty)
                    yield
                    bb = project(("a", l, "cb", c), h)
                    ty = tt(V, yc.ap, bb.ap, yc.ap, ALU.mult, bb.t, ty)
                    drop(bb, ty)
                    y.append(split(yc.ap, ty))
                    drop(yc, y[-1][2])
                    yield

            def pool_branch(l, h, y):
                pwt = get()
                pwt.t = dma(pwt.ap, ins["poolw"][l], pwt.free)
                ict = get()
                ict.t = dma(ict.ap[:, 0:64], ins["cnt"], ict.free)
                late = []

                def mixed(g, p, tp_, sg):
                    bm = get("P")
                    tm = mm(bm.ap, pwt.ap[:, 128 * g:128 * g + 128], p.ap, True, True, bm.free, tp_, pwt.t, inc=True)
                    drop(p, tm)
                    ty = stt(sg.ap, bm.ap, par(f"pscale{l}", g), sg.ap, ALU.mult, ALU.mult, tm, sg.t, cst)
                    drop(bm, ty)
                    y.append(split(sg.ap, ty))
                    drop(sg, y[-1][2])
                    return tm

                for g in range(4):
                    w = 2 << g
                    bu = project(("a", l, "pu", g), h)
                    u = get()
                    tu = cp(A, u.ap, bu.ap, bu.t, u.free)
                    drop(bu, tu)
                    src, tsrc = u, tu
                    k = 1
                    while k < w:
                        o = get()
                        a = tt(V, o.ap[:, k:512], src.ap[:, k:512], src.ap[:, 0:512 - k], ALU.add, tsrc, o.free)
                        b = cp(V, o.ap[:, 0:k], src.ap[:, 0:k])
                        if src is not u:
                            drop(src, b)
                        src, tsrc = o, b
                        k *= 2
                    p = get()
                    a = stt(p.ap, src.ap, 1.0 / w, u.ap, ALU.mult, ALU.subtract, tsrc, tu, p.free)
                    b = tt(V, p.ap[:, 0:16], src.ap[:, 0:16], ict.ap[:, 16 * g:16 * g + 16], ALU.mult, a, ict.t)
                    c = tt(V, p.ap[:, 0:16], p.ap[:, 0:16], u.ap[:, 0:16], ALU.subtract, b)
                    drop(src, b)
                    drop(u, c)
                    yield
                    bg = project(("a", l, "pgate", g), h)
                    sg = get()
                    sg.t = act(sg.ap, bg.ap, ACT.Silu, bg.t, sg.free)
                    drop(bg, sg.t)
                    yield
                    if late:
                        tm = mixed(*late.pop())
                    late.append((g, p, c, sg))
                tm = mixed(*late.pop())
                drop(pwt, tm)
                drop(ict, b)

            def rope(key, h, cos, sin, rot, g=None, pre=None):
                bank = project(key, h)
                x = get()
                if g is None:
                    t0 = cp(A, x.ap, bank.ap, bank.t, x.free)
                    drop(bank, t0)
                else:
                    sq = get()
                    tsq = act(sq.ap, bank.ap, ACT.Square, bank.t, sq.free)
                    t0 = act(x.ap, bank.ap, ACT.Copy, bank.t, x.free, cst, scale=g)
                    drop(bank, tsq, t0)
                yield
                if g is not None:
                    ss = get("P")
                    ss.t = mm(ss.ap, pair, sq.ap, True, True, ss.free, tsq, cst, inc=True)
                br = get("P")
                tr = mm(br.ap, rot, x.ap, True, True, br.free, t0, cst, inc=True)
                o = get()
                t1 = tt(V, o.ap, br.ap, sin.ap, ALU.mult, tr, sin.t, o.free)
                drop(br, t1)
                tpre = None if pre is None else pre(x, t0)
                t2 = tt(V, x.ap, x.ap, cos.ap, ALU.mult, t0, tr, cos.t, tpre)
                t3 = tt(V, o.ap, o.ap, x.ap, ALU.add, t1, t2)
                drop(x, t3)
                if g is not None:
                    tn = rstd(ss, 1.0 / 64, sq.ap, 512, ss.t)
                    t3 = tt(V, o.ap, o.ap, sq.ap, ALU.mult, t3, tn)
                    drop(sq, t3)
                o.t = t3
                yield
                return o

            def tables(which):
                cos, sin = get(), get()
                cos.t = dma(cos.ap, ins["rope"][which, 0], cos.free)
                sin.t = dma(sin.ap, ins["rope"][which, 1], sin.free)
                return cos, sin

            def head_pair(q, ks, v, vcol, causal_bias, finish, done_q):
                ob = get("P")
                sums = get("S")
                todo = []
                gone = []

                def scores(i, hh):
                    n = 128 * (i + 1) if causal_bias is not None else 512
                    half = slice(64 * hh, 64 * hh + 64)
                    b = get("P")
                    t = t0 = mm(b.ap[:, 0:n], q.ap[half, 128 * i:128 * i + 128], ks[hh].ap[half, 0:n], True, True,
                                b.free, q.t, ks[hh].t, inc=True)
                    p = get()
                    m = get("S")
                    if causal_bias is not None:
                        bias, tb = causal_bias[i]
                        t = V.put(lambda e: e.tensor_tensor_reduce(
                            out=p.ap[:, 0:n], in0=b.ap[:, 0:n], in1=bias, scale=0.125, scalar=NEG, op0=ALU.add,
                            op1=ALU.max, accum_out=m.ap[:, 1:2]), (t, tb, p.free, m.free))
                        drop(b, t)
                        tm = ts(V, m.ap[:, 0:1], m.ap[:, 1:2], -1.0, None, ALU.mult, None, t)
                        te = act(p.ap[:, 0:n], p.ap[:, 0:n], ACT.Exp, tm, sums.free, bias=m.ap[:, 0:1],
                                 accum_out=sums.ap[:, 2 * i + hh:2 * i + hh + 1])
                    else:
                        tm = V.put(lambda e: e.reduce_max(m.ap[:, 1:2], b.ap[:, 0:n], AX.X, negate=True), (t, m.free))
                        tm = ts(V, m.ap[:, 0:1], m.ap[:, 1:2], 0.125, None, ALU.mult, None, tm)
                        te = act(p.ap[:, 0:n], b.ap[:, 0:n], ACT.Exp, tm, sums.free, p.free, bias=m.ap[:, 0:1],
                                 scale=0.125, accum_out=sums.ap[:, 2 * i + hh:2 * i + hh + 1])
                        drop(b, te)
                    drop(m, te)
                    q.free = t0
                    return i, hh, n, p, te

                def turned(i, hh, n, p, te):
                    b = get("P")
                    for k in range(n // 128):
                        t = tp(b.ap[:, 128 * k:128 * k + 128], p.ap[:, 128 * k:128 * k + 128], te, b.free,
                               inc=(k == n // 128 - 1))
                    drop(p, t)
                    pt = get()
                    pt.t = cp(V if hh else A, pt.ap[:, 0:n], b.ap[:, 0:n], t, pt.free)
                    drop(b, pt.t)
                    gone.append(te)
                    return i, hh, n, pt

                def values(i, hh, n, pt):
                    dst = ob.ap[:, 64 * (2 * i + hh):64 * (2 * i + hh) + 64]
                    for k in range(n // 128):
                        t = mm(dst, pt.ap[:, 128 * k:128 * k + 128], v[k].ap[:, vcol[hh]:vcol[hh] + 64],
                               k == 0, k == n // 128 - 1, pt.t, ob.free, v[k].t, inc=(k == n // 128 - 1))
                    drop(pt, t)
                    ob.t = t

                def onward():
                    if todo:
                        ready_.append(turned(*todo.pop(0)))
                        if len(ready_) > 1:
                            values(*ready_.pop(0))
                    elif ready_:
                        values(*ready_.pop(0))

                def rest():
                    while todo or ready_:
                        onward()
                        yield
                    yield from normed(ob, sums, gone[-1], finish)

                ready_ = []
                units = [(i, hh) for i in range(4) for hh in range(2)]
                for u in units:
                    todo.append(scores(*u))
                    if len(todo) > 2:
                        onward()
                    yield
                done_q(q, ks, q.free)
                return rest()

            def normed(ob, sums, te, finish):
                rs = get("S")
                t = recip(rs.ap[:, 0:8], sums.ap[:, 0:8], te, rs.free)
                drop(sums, t)
                on = get()
                t = tt(V, on.ap.rearrange("p (u d) -> p u d", d=64), ob.ap.rearrange("p (u d) -> p u d", d=64),
                       rs.ap[:, 0:8].unsqueeze(2).to_broadcast([128, 8, 64]), ALU.mult, t, ob.t, on.free)
                drop(ob, t)
                drop(rs, t)
                yield
                b = get("P")
                for i in range(4):
                    tb = tp(b.ap[:, 128 * i:128 * i + 128], on.ap[:, 128 * i:128 * i + 128], t, b.free, inc=(i == 3))
                drop(on, tb)
                b.t = tb
                f = finish(b)
                yield
                return f

            def index_scores(l, h, cos, sin):
                iw = get("S")
                iw2 = get("S")
                sc8 = 8.0 ** -0.5

                def head_weights(x, t0):
                    bw = get("P")
                    for i in range(4):
                        t = M.put(lambda e, i=i: e.transpose(bw.ap[:, 8 * i:8 * i + 8], x.ap[64:72, 128 * i:128 * i + 128],
                                                             eye[64:72, 64:72]), (t0, bw.free, cst), i == 3)
                    a = ts(V, iw.ap[:, 0:16], bw.ap[:, 0:16], sc8, None, ALU.mult, None, t, iw.free)
                    b = ts(V, iw2.ap[:, 0:16], bw.ap[:, 16:32], sc8, None, ALU.mult, None, t, iw2.free)
                    drop(bw, b)
                    iw.t = b
                    return b

                ik = yield from rope(("a", l, "ik", 0), h, cos, sin, rotA, None, head_weights)
                tiw = iw.t
                ik.t = cp(A, ik.ap[64:128, :], ik.ap[0:64, :], ik.t)
                acc = [get() for _ in range(3)]
                yield
                nxt = Aux(rope(("a", l, "iq", 0), h, cos, sin, rotA))
                while not nxt.done:
                    nxt.step()
                    yield
                for c in range(4):
                    iq = nxt.val
                    nxt = Aux(rope(("a", l, "iq", c + 1), h, cos, sin, rotA) if c < 3 else None)
                    for hh in range(2):
                        hd = 2 * c + hh
                        half = slice(64 * hh, 64 * hh + 64)
                        for i in range(1, 4):
                            n = 128 * (i + 1)
                            bs = get("P")
                            t = mm(bs.ap[:, 0:n], iq.ap[half, 128 * i:128 * i + 128], ik.ap[half, 0:n], True, True,
                                   bs.free, iq.t, ik.t, inc=True)
                            r = get()
                            tr = act(r.ap[:, 0:n], bs.ap[:, 0:n], ACT.Relu, t, r.free, scale=0.125)
                            drop(bs, tr)
                            z = acc[i - 1]
                            src = (iw if i < 2 else iw2).ap
                            wcol = src[:, 8 * (i % 2) + hd:8 * (i % 2) + hd + 1]
                            if hd == 0:
                                z.t = ts(V, z.ap[:, 0:n], r.ap[:, 0:n], wcol, None, ALU.mult, None, tr, z.free, tiw)
                            else:
                                z.t = stt(z.ap[:, 0:n], r.ap[:, 0:n], wcol, z.ap[:, 0:n], ALU.mult, ALU.add, tr, z.t)
                            drop(r, z.t)
                            if i % 2:
                                nxt.step()
                                yield
                    drop(iq, t)
                drop(ik, t)
                drop(iw, acc[0].t, acc[2].t)
                drop(iw2, acc[1].t, acc[2].t)
                return acc

            def select_keys(acc, bias):
                m8 = get("S")
                for i in range(1, 4):
                    z = acc[i - 1]
                    n = 128 * (i + 1)
                    za = z.ap[:, 0:n]
                    t = tt(V, z.ap[:, 128 * i:n], z.ap[:, 128 * i:n], causal, ALU.add, z.t, cst)
                    for r in range(16):
                        t = V.put(lambda e, za=za: e.max(m8.ap[:, 0:8], za), (t, m8.free))
                        t = V.put(lambda e, za=za: e.match_replace(za, m8.ap[:, 0:8], za, GONE), (t,))
                        if r % 2:
                            yield
                    t = ts(V, za, za, GONE, NEG, ALU.not_equal, ALU.mult, t)
                    bias[i] = (za, t)
                drop(m8, t)

            def attend_first(l, h, y):
                bias = {0: (causal, cst)}
                cos, sin = tables(0)
                acc = yield from index_scores(l, h, cos, sin)
                sel = Aux(select_keys(acc, bias))

                def values_in():
                    v = []
                    for b in project_tok(("a", l, "v"), h):
                        x = get()
                        x.t = cp(A, x.ap, b.ap, b.t, x.free)
                        drop(b, x.t)
                        v.append(x)
                    yield
                    return v

                def qk(c):
                    q = yield from rope(("a", l, "q", c), h, cos, sin, rotA, par(f"qg{l}"))
                    k = yield from rope(("a", l, "k", c), h, cos, sin, rotA, par(f"kg{l}"))
                    return q, k

                sel.step()
                sel.step()
                va, nxt = Aux(values_in()), Aux(qk(0))
                while not (sel.done and va.done and nxt.done):
                    sel.step()
                    if not nxt.done:
                        nxt.step()
                    else:
                        va.step()
                    yield
                v = va.val
                last = []
                tail = Aux(None)
                for c in range(4):
                    while not nxt.done:
                        nxt.step()
                    q, k = nxt.val
                    nxt = Aux(qk(c + 1) if c < 3 else None)

                    def finish(b, c=c):
                        bg = project(("a", l, "agate", c), h)
                        sg = get()
                        tg = act(sg.ap, bg.ap, ACT.Silu, bg.t, sg.free)
                        drop(bg, tg)
                        ty = tt(V, sg.ap, b.ap, sg.ap, ALU.mult, b.t, tg)
                        drop(b, ty)
                        y.append(split(sg.ap, ty))
                        drop(sg, y[-1][2])
                        last.append(b.t)

                    def done_q(q, ks, t):
                        drop(q, t)
                        drop(ks[0], t)

                    g = Aux(head_pair(q, (k, k), v, (128 * c, 128 * c + 64), bias, finish, done_q))
                    while not g.done:
                        g.step()
                        tail.step()
                        nxt.step()
                        yield
                    tail = Aux(g.val)
                while not tail.done:
                    tail.step()
                    yield
                for x in v:
                    drop(x, last)
                drop(cos, k.t)
                drop(sin, k.t)
                for x in acc:
                    drop(x, last)

            def gated(kind, l, h, ys, m, keep):
                for c in range(8):
                    s = None
                    for br, y in ys:
                        bg = project((kind, l, "gate", 8 * br + c), h)
                        sg = get()
                        tg = act(sg.ap, bg.ap, ACT.Sigmoid, bg.t, sg.free)
                        drop(bg, tg)
                        yield
                        by = project((kind, l, "br", br, c), y)
                        t = tt(V, sg.ap, by.ap, sg.ap, ALU.mult, by.t, tg)
                        drop(by, t)
                        if s is None:
                            s, tm = sg, t
                        else:
                            tm = tt(G, s.ap, s.ap, sg.ap, ALU.add, tm, t)
                            drop(sg, tm)
                    if m[c] is not None:
                        for part in m[c][0:2]:
                            tm = tt(G, s.ap, s.ap, part.ap.bitcast(fp32), ALU.add, tm, m[c][2])
                        drop_pair(m[c], tm)
                    m[c] = split(s.ap, tm)
                    drop(s, m[c][2])
                    yield
                for br, y in ys:
                    drop_h(y, by.t)
                if not keep:
                    drop_h(h, by.t)

            def out_product(key, y, aux=None):
                st.x = []
                nxt = load_x(0)
                for c in range(8):
                    x = nxt
                    if c < 7:
                        nxt = load_x(c + 1)
                    b = project(key + (c,), y)
                    st.x.append(add_out(b, x))
                    if aux is not None:
                        aux.step()
                drop_h(y, b.t)

            def all_of(*gens):
                for g in gens:
                    yield from g

            def block_one(l, aux):
                h = norm_x(f"ng{l}")
                ya, yb, yc = [], [], []
                m = [None] * 8
                side = all_of(conv_branch(l, h, ya), pool_branch(l, h, yc),
                              gated("a", l, h, ((0, ya), (2, yc)), m, True))
                beside(attend_first(l, h, yb), side)
                for _ in gated("a", l, h, ((1, yb),), m, False):
                    pass
                out_product(("a", l, "wo"), m, aux)

            def filters(l, o, hid, R):
                w3 = []
                for d in range(2):
                    w = get()
                    w.t = dma(w.ap[0:65, :], ins["w3"][l, 2 * o + d], w.free)
                    w3.append(w)
                acc = get()
                for tq in range(4):
                    win = get()
                    win.t = dma(win.ap, ins["win"][tq], win.free)
                    fs = []
                    for d in range(2):
                        b = get("P")
                        t = mm(b.ap, hid.ap[0:65, 128 * tq:128 * tq + 128], w3[d].ap[0:65, :], True, True, b.free,
                               hid.t, w3[d].t, inc=True)
                        f = get()
                        f.t = tt(V, f.ap, b.ap, win.ap, ALU.mult, t, win.t, f.free)
                        drop(b, f.t)
                        if d == 1 and tq == 0:
                            f.t = memset(V, f.ap[0:1, :], 0.0, f.t)
                        fs.append(f)
                    drop(win, fs[1].t, fs[0].t)
                    hid.last = t
                    for w in w3:
                        w.free = t
                    s, df = get(), get()
                    ta = tt(V, s.ap, fs[0].ap, fs[1].ap, ALU.add, fs[0].t, fs[1].t, s.free)
                    td = tt(G, df.ap, fs[0].ap, fs[1].ap, ALU.subtract, fs[0].t, fs[1].t, df.free)
                    R[0].append(split(s.ap, ta))
                    drop(s, R[0][-1][2])
                    R[1].append(split(df.ap, td))
                    drop(df, R[1][-1][2])
                    yield
                    for d in range(2):
                        f = fs[d]
                        if tq == 0 and d == 0:
                            tacc = act(acc.ap, f.ap, ACT.Abs, f.t, acc.free)
                            drop(f, tacc, ta, td)
                        else:
                            t1 = act(f.ap, f.ap, ACT.Abs, f.t, ta, td)
                            tacc = tt(G, acc.ap, acc.ap, f.ap, ALU.add, t1, tacc)
                            drop(f, tacc)
                for w in w3:
                    drop(w, t)
                yield
                b = get("P")
                t = mm(b.ap, ones, acc.ap, True, True, b.free, tacc, cst, inc=True)
                t = ts(V, acc.ap, b.ap, EPS, None, ALU.add, None, t)
                drop(b, t)
                t = recip(acc.ap, acc.ap, t)
                acc.t = ts(V, acc.ap, acc.ap, 2.0 / 1024, None, ALU.mult, None, t)
                return acc

            def sine(bank, rows, b1, fr, o, ow):
                n, x = get(), get()
                t = ts(V, x.ap[0:rows], bank.ap[0:rows], b1, fr, ALU.add, ALU.mult, bank.t, x.free, cst)
                drop(bank, t)
                tn = ts(V, n.ap[0:rows], x.ap[0:rows], 1.0 / (2 * np.pi), MAGIC, ALU.mult, ALU.add, t, n.free)
                tn = ts(V, n.ap[0:rows], n.ap[0:rows], MAGIC, None, ALU.subtract, None, tn)
                c1 = 6.28125
                c2 = float(np.float32(2 * np.pi - c1))
                c2 = float(np.frombuffer((np.array([c2], np.float32).view(np.uint32) & np.uint32(0xFFFFF000)).tobytes(), np.float32)[0])
                c3 = float(2 * np.pi - c1 - c2)
                for c in (c1, c2, c3):
                    t = stt(x.ap[0:rows], n.ap[0:rows], -c, x.ap[0:rows], ALU.mult, ALU.add, tn, t)
                t = ts(V, x.ap[0:rows], x.ap[0:rows], 3.1415925, -3.1415925, ALU.min, ALU.max, t)
                t = act(o.ap[0:rows], x.ap[0:rows], ACT.Sin, t, ow)
                drop(x, t)
                drop(n, t)
                return t

            def filter_mlp(l):
                w = get()
                tw = dma(w.ap[0:64, 0:128], ins["w12"][l], w.free)
                z = get()
                tz = dma(z.ap[0:33, :], ins["zpos"], z.free)
                yield
                b = get("P")
                b.t = mm(b.ap[0:64, :], w.ap[0:33, 0:64], z.ap[0:33, :], True, True, b.free, tw, tz, inc=True)
                drop(z, b.t)
                h1 = get()
                t = sine(b, 64, par(f"hb1{l}", 0, 64), par(f"hf1{l}", 0, 64), h1, h1.free)
                yield
                yield
                b = get("P")
                b.t = mm(b.ap[0:64, :], w.ap[0:64, 64:128], h1.ap[0:64, :], True, True, b.free, t, inc=True)
                drop(w, b.t)
                drop(h1, b.t)
                hid = get()
                t1 = memset(V, hid.ap[64:65, :], 1.0, hid.free)
                t2 = sine(b, 64, par(f"hb2{l}", 0, 64), par(f"hf2{l}", 0, 64), hid, hid.free)
                hid.t = (t1, t2)
                return hid

            def conv_chunk(l, part, c, h):
                b = project(("b", l, "hy", 4 * part + c), h)
                s = get()
                t = cp(A, s.ap, b.ap, b.t, s.free)
                drop(b, t)
                o = get()
                V.wait(o.free)
                o.t = short_conv(s.ap, t, o.ap, [par(f"hconv{l}", 12 * j + 4 * part + c) for j in range(3)], 1)
                drop(s, o.t)
                return o

            def to_tokens(fm):
                tm = []
                for i in range(4):
                    b = get("P")
                    for c in range(4):
                        t = tp(b.ap[:, 128 * c:128 * c + 128], fm[c].ap[:, 128 * i:128 * i + 128], fm[c].t, b.free,
                               inc=(c == 3))
                    o = get()
                    o.t = cp(A if i % 2 else V, o.ap, b.ap, t, o.free)
                    drop(b, o.t)
                    tm.append(o)
                for x in fm:
                    drop(x, t)
                return tm

            def spectra(l, o, R, u, aux):
                ur, us = [], []
                for j in range(4):
                    wh, wl, wt = weight(("dft", "f", j, l, o))
                    bk = [get("P") for _ in range(4)]
                    jobs = [(0, u, 0), (1, u, 4), (2, R[0], 0), (3, R[1], 4)]
                    for bi, src, k0 in jobs:
                        for k in range(4):
                            t = mm3(bk[bi].ap, (wh[:, k0 + k, :], wl[:, k0 + k, :]), cols(src[k], FULL), k == 0, k == 3,
                                    wt, bk[bi].free, src[k][2], inc=(k == 3))
                        bk[bi].t = t
                    weight_done(t)
                    fr, fi = get(), get()
                    tr = cp(A, fr.ap, bk[2].ap, bk[2].t, fr.free)
                    ti = cp(A, fi.ap, bk[3].ap, bk[3].t, fi.free)
                    drop(bk[2], tr)
                    drop(bk[3], ti)
                    a, b, c = get(), get(), get()
                    t1 = tt(V, a.ap, bk[0].ap, fr.ap, ALU.mult, bk[0].t, tr, a.free)
                    t2 = tt(V, b.ap, bk[1].ap, fi.ap, ALU.mult, bk[1].t, ti, b.free)
                    t3 = tt(V, c.ap, bk[0].ap, fi.ap, ALU.mult, bk[0].t, ti, c.free)
                    t4 = tt(V, fr.ap, bk[1].ap, fr.ap, ALU.mult, bk[1].t, t1)
                    drop(bk[0], t3)
                    drop(bk[1], t4)
                    drop(fi, t3)
                    t5 = tt(G, a.ap, a.ap, b.ap, ALU.subtract, t1, t2)
                    t6 = tt(G, c.ap, c.ap, fr.ap, ALU.add, t3, t4)
                    drop(b, t5)
                    drop(fr, t6)
                    ur.append(split(a.ap, t5))
                    us.append(split(c.ap, t6))
                    aux.step()
                    drop(a, ur[-1][2])
                    drop(c, us[-1][2])
                for x in R[0] + R[1] + u:
                    drop_pair(x, t)
                return ur + us

            def hyena(l, h, y, hid):
                def signals():
                    fm = []
                    for part in range(2):
                        fm.append([])
                        for c in range(4):
                            fm[part].append(conv_chunk(l, part, c, h))
                            if part and c == 0:
                                v = to_tokens(fm[0])
                                vs = [split(x.ap, x.t) for x in v]
                            yield
                    x1 = to_tokens(fm[1])
                    got.append((v, vs, x1))

                got = []
                R = ([], [])
                f = Aux(filters(l, 0, hid, R))
                sg = Aux(signals())
                while not (len(R[1]) == 4 and sg.done):
                    sg.step()
                    if len(R[1]) < 4:
                        f.step()
                v, vs, x1 = got[0]
                Y = spectra(l, 0, R, vs, f)
                while not f.done:
                    f.step()
                rn = f.val
                R = ([], [])
                f = Aux(filters(l, 1, hid, R))
                skb = get()
                skb.t = dma(skb.ap, ins["skip"][l, 0], skb.free)
                for j in range(4):
                    b = project(("dft", "i", j, l, 0), Y)
                    t1 = tt(V, b.ap, b.ap, rn.ap, ALU.mult, b.t, rn.t)
                    t2 = tt(G, v[j].ap, v[j].ap, skb.ap, ALU.mult, v[j].t, vs[j][2], skb.t)
                    t3 = tt(V, v[j].ap, b.ap, v[j].ap, ALU.add, t1, t2)
                    drop(b, t3)
                    t4 = tt(V, v[j].ap, v[j].ap, x1[j].ap, ALU.mult, t3, x1[j].t)
                    v[j].t = t4
                    drop(x1[j], t4)
                    if len(R[1]) < 4:
                        f.step()
                for p in Y:
                    drop_pair(p, b.t)
                drop(rn, t3)
                zs = [split(x.ap, x.t) for x in v]
                while len(R[1]) < 4:
                    f.step()
                drop(hid, b.t, R[0][-1][2], hid.t, hid.last)
                t3 = dma(skb.ap, ins["skip"][l, 1], t2)
                skb.t = t3
                x2 = [conv_chunk(l, 2, c, h) for c in range(2)]
                Y = spectra(l, 1, R, zs, f)
                while not f.done:
                    f.step()
                rn = f.val
                for j in range(4):
                    b = project(("dft", "i", j, l, 1), Y)
                    t1 = tt(V, b.ap, b.ap, rn.ap, ALU.mult, b.t, rn.t)
                    t2 = tt(G, v[j].ap, v[j].ap, skb.ap, ALU.mult, v[j].t, zs[j][2], skb.t)
                    v[j].t = tt(V, v[j].ap, b.ap, v[j].ap, ALU.add, t1, t2)
                    drop(b, v[j].t)
                for p in Y:
                    drop_pair(p, b.t)
                drop(rn, v[3].t)
                drop(skb, t2)
                x2 += [conv_chunk(l, 2, c, h) for c in range(2, 4)]
                for c in range(4):
                    b = get("P")
                    for i in range(4):
                        t = tp(b.ap[:, 128 * i:128 * i + 128], v[i].ap[:, 128 * c:128 * c + 128], v[i].t, b.free,
                               inc=(i == 3))
                    x = x2[c]
                    t = tt(V, x.ap, b.ap, x.ap, ALU.mult, t, x.t)
                    drop(b, t)
                    y.append(split(x.ap, t))
                    drop(x, y[-1][2])
                for x in v:
                    drop(x, t)

            def attend_second(l, h, y):
                cos, sin = tables(1)
                ka = yield from rope(("b", l, "k", 0), h, cos, sin, rotB, par(f"akn{l}"))
                kb = get()
                t1 = cp(A, kb.ap[64:128, :], ka.ap[0:64, :], ka.t, kb.free)
                t2 = cp(V, kb.ap[0:64, :], ka.ap[64:128, :], ka.t, kb.free)
                kb.t = (t1, t2)
                ks = [ka, kb]
                wh, wl, wt = weight(("b", l, "v", 0))
                vb = get("P")
                for tq in range(4):
                    for k in range(8):
                        t = mm3(vb.ap[:, 128 * tq:128 * tq + 128], cols(h[k], slice(128 * tq, 128 * tq + 128)),
                                (wh[:, k, :], wl[:, k, :]), k == 0, k == 7, wt, vb.free, h[k][2], inc=(k == 7))
                weight_done(t)
                va = get()
                va.t = cp(A, va.ap, vb.ap, t, va.free)
                drop(vb, va.t)
                v = []
                for tq in range(4):
                    x = Tile(va.ap[:, 128 * tq:128 * tq + 128], "F")
                    x.t = va.t
                    v.append(x)
                yield

                def qc(c):
                    return rope(("b", l, "q", c), h, cos, sin, rotB, par(f"aqn{l}"))

                nxt, tail = Aux(qc(0)), Aux(None)
                last = []
                for c in range(4):
                    while not nxt.done:
                        nxt.step()
                        yield
                    q = nxt.val
                    nxt = Aux(qc(c + 1) if c < 3 else None)

                    def finish(b):
                        f = get()
                        t = cp(V, f.ap, b.ap, b.t, f.free)
                        drop(b, t)
                        y.append(split(f.ap, t))
                        drop(f, y[-1][2])
                        last.append(b.t)

                    def done_q(q, ks, t):
                        drop(q, t)

                    gi = c // 2
                    g = Aux(head_pair(q, (ks[gi], ks[1 - gi]), v, (64 * gi, 64 * gi), None, finish, done_q))
                    while not g.done:
                        g.step()
                        tail.step()
                        nxt.step()
                        yield
                    tail = Aux(g.val)
                while not tail.done:
                    tail.step()
                    yield
                drop(va, last)
                for k in ks:
                    drop(k, last)
                drop(cos, q.t)
                drop(sin, q.t)

            def gla(l, h, y):
                wl_ = get()
                ta = memset(V, wl_.ap[0:32, :], 0.0, wl_.free)
                t1 = dma(wl_.ap[0:16, 0:256], ins["wlr"][l, 0], ta)
                t2 = dma(wl_.ap[16:32, 256:512], ins["wlr"][l, 1], ta)
                wl_.t = (t1, t2)
                blr = project(("b", l, "lr", 0), h)
                lr = get()
                lr.t = cp(A, lr.ap[0:32, :], blr.ap[0:32, :], blr.t, lr.free)
                drop(blr, lr.t)
                rst = get()
                tm0 = memset(V, rst.ap, 1.0, rst.free)
                rst.t = memset(V, rst.ap.rearrange("p (n c) -> p n c", c=64)[:, :, 0:1], 0.0, tm0)
                yield

                def front(hp):
                    lgs, es, tt_ = [], [], []
                    for d in range(2):
                        b = get("P")
                        t = mm(b.ap, wl_.ap[0:32, 256 * d + 128 * hp:256 * d + 128 * hp + 128], lr.ap[0:32, :],
                               True, True, b.free, wl_.t, lr.t, inc=True)
                        lg, e = get(), get()
                        t = ts(V, lg.ap, b.ap, par(f"glab{l}", 2 * d + hp), None, ALU.add, None, t, lg.free, cst)
                        drop(b, t)
                        te = act(e.ap, lg.ap, ACT.Abs, t, e.free)
                        te = act(e.ap, e.ap, ACT.Exp, te, scale=-1.0)
                        lgs.append(lg)
                        es.append(e)
                        tt_.append((t, te))
                    for d in range(2):
                        t, te = tt_[d]
                        t1 = act(es[d].ap, es[d].ap, ACT.Ln, te, bias=1.0)
                        tt_[d] = (ts(V, lgs[d].ap, lgs[d].ap, 0.0, None, ALU.min, None, t, te), t1)
                    for d in range(2):
                        lg, B = lgs[d], es[d]
                        t = tt(V, lg.ap, lg.ap, B.ap, ALU.subtract, tt_[d])
                        src, dst = (lg.ap, B.ap) if d == 0 else (lg.ap[:, ::-1], B.ap[:, ::-1])
                        B.t = V.put(lambda e_, src=src, dst=dst: e_.tensor_tensor_scan(dst, rst.ap, src, 0.0, ALU.mult,
                                                                                     ALU.add), (t, rst.t))
                    return lgs, es

                nf = front(0)
                yield
                v = []
                for b in project_tok(("b", l, "gv"), h):
                    x = get()
                    x.t = cp(A, x.ap, b.ap, b.t, x.free)
                    drop(b, x.t)
                    v.append(x)
                yield
                for hp in range(2):
                    lgs, es = nf
                    bk = project(("b", l, "gk", hp), h)
                    k = get()
                    k.t = cp(A, k.ap, bk.ap, bk.t, k.free)
                    drop(bk, k.t)
                    bq = project(("b", l, "gq", hp), h)
                    q = get()
                    q.t = act(q.ap, bq.ap, ACT.Copy, bq.t, q.free, scale=0.125)
                    drop(bq, q.t)
                    yield
                    qd, kinv, sp, decs, t5s = [], [], [], [], []
                    for d in range(2):
                        lg, B = lgs[d], es[d]
                        t = B.t
                        B3 = B.ap.rearrange("p (n c) -> p n c", c=64)
                        Bl = B3[:, :, 63:64] if d == 0 else B3[:, :, 0:1]
                        t5 = tt(V, lg.ap.rearrange("p (n c) -> p n c", c=64), Bl.to_broadcast([128, 8, 64]), B3,
                                ALU.subtract, t)
                        t5 = act(lg.ap, lg.ap, ACT.Exp, t5, scale=1.0 / 16)
                        x = get()
                        tx = act(x.ap, B.ap, ACT.Exp, t, x.free, scale=-1.0 / 16)
                        x2 = get()
                        tx2 = act(x2.ap, B.ap, ACT.Exp, t, x2.free, scale=1.0 / 16)
                        dec = get("S")
                        tdec = act(dec.ap[:, 0:8], Bl.rearrange("p n c -> p (n c)"), ACT.Exp, t, dec.free, scale=1.0 / 16)
                        t5s.append(tt(V, lg.ap, lg.ap, k.ap, ALU.mult, t5, k.t))
                        x.t = tt(V, x.ap, x.ap, k.ap, ALU.mult, tx, k.t)
                        x2.t = tt(V, x2.ap, x2.ap, q.ap, ALU.mult, tx2, q.t)
                        kinv.append(x)
                        qd.append(x2)
                        decs.append((dec, tdec))
                        yield 2
                    kds = []
                    for d in range(2):
                        b = get("P")
                        for i in range(4):
                            t = tp(b.ap[:, 128 * i:128 * i + 128], lgs[d].ap[:, 128 * i:128 * i + 128], t5s[d], b.free,
                                   inc=(i == 3))
                        kd = es[d]
                        kd.t = cp(V if d else A, kd.ap, b.ap, t, decs[d][1], qd[d].t, kinv[d].t)
                        drop(b, kd.t)
                        drop(lgs[d], t)
                        kds.append(kd)
                    drop(q, qd[1].t)
                    drop(k, t5s[1], kinv[1].t)
                    yield 2
                    ams = [[], []]

                    def inside(hh):
                        half = slice(64 * hh, 64 * hh + 64)
                        for d in range(2):
                            b = get("P")
                            for i in range(4):
                                sl = slice(128 * i, 128 * i + 128)
                                t = mm(b.ap[:, sl], kinv[d].ap[half, sl], qd[d].ap[half, sl], True, True, b.free,
                                       kinv[d].t, qd[d].t, inc=(i == 3))
                            t_last = t
                            x = get()
                            t = ts(V, x.ap, b.ap, BIG, -BIG, ALU.min, ALU.max, t, x.free)
                            drop(b, t)
                            mk = (maskf if d == 0 else maskb).unsqueeze(1).to_broadcast([128, 4, 128])
                            x3 = x.ap.rearrange("p (i c) -> p i c", c=128)
                            x.t = tt(G, x3, x3, mk, ALU.mult, t, cst)
                            ams[hh].append(x)
                        kinv[0].last = t_last
                        a0, a1 = ams[hh]
                        a0.t = tt(G, a0.ap, a0.ap, a1.ap, ALU.add, a0.t, a1.t)
                        drop(a1, a0.t)

                    for d in range(2):
                        kd = kds[d]
                        dec, tdec = decs[d]
                        bs = [get("P"), get("P")]
                        for n in range(8):
                            rows = slice(64 * (n % 2), 64 * (n % 2) + 64)
                            for hh in range(2):
                                t = mm(bs[n % 2].ap[64 * hh:64 * hh + 64, 128 * (n // 2):128 * (n // 2) + 128],
                                       kd.ap[rows, 128 * (n // 2) + 64 * hh:128 * (n // 2) + 64 * hh + 64],
                                       v[n // 2].ap[rows, 256 * hp + 128 * hh:256 * hp + 128 * hh + 128], True, True,
                                       kd.t, bs[n % 2].free, v[n // 2].t, inc=(n == 7 and hh == 1))
                        drop(kd, t)
                        inside(d)
                        sA, sB = get(), get()
                        SS = [(sA if n < 4 else sB).ap[:, 128 * (n % 4):128 * (n % 4) + 128] for n in range(8)]
                        V.wait([sA.free, sB.free])
                        seq = list(range(7)) if d == 0 else list(range(7, 0, -1))
                        ts_ = t
                        for j, n in enumerate(seq):
                            nx = n + 1 if d == 0 else n - 1
                            ds = bs[n % 2].ap[:, 128 * (n // 2):128 * (n // 2) + 128]
                            if j == 0:
                                ts_ = cp(V, SS[nx], ds, ts_)
                            else:
                                ts_ = stt(SS[nx], SS[n], dec.ap[:, n:n + 1], ds, ALU.mult, ALU.add, ts_, tdec)
                        drop(bs[0], ts_)
                        drop(bs[1], ts_)
                        drop(dec, ts_)
                        sp.append((SS, ts_, sA, sB))
                        yield 2
                    for x in kinv:
                        drop(x, kinv[0].last)
                    if hp == 0:
                        nf = front(1)
                        yield
                    for hh in range(2):
                        half = slice(64 * hh, 64 * hh + 64)
                        am = ams[hh][0]
                        ob = get("P")
                        e0 = 256 * hp + 128 * hh
                        for i in range(4):
                            tl = mm(ob.ap[:, 128 * i:128 * i + 128], v[i].ap[:, e0:e0 + 128],
                                    am.ap[:, 128 * i:128 * i + 128], True, False, am.t, ob.free, v[i].t)
                            jobs = [(n, d) for n in (2 * i, 2 * i + 1) for d in range(2) if (n, d) not in ((0, 0), (7, 1))]
                            for n, d in jobs:
                                SS, tS = sp[d][0], sp[d][1]
                                tl = mm(ob.ap[:, 64 * n:64 * n + 64], SS[n][half, :], qd[d].ap[half, 64 * n:64 * n + 64],
                                        False, (n, d) == jobs[-1], tS, qd[d].t, inc=(n, d) == jobs[-1])
                        drop(am, tl)
                        sq = get()
                        t = act(sq.ap, ob.ap, ACT.Square, tl, sq.free)
                        bg = project(("b", l, "go", 2 * hp + hh), h)
                        sg = get()
                        tg = act(sg.ap, bg.ap, ACT.Silu, bg.t, sg.free)
                        drop(bg, tg)
                        ss = get("P")
                        ss.t = mm(ss.ap, ones, sq.ap, True, True, ss.free, t, cst, inc=True)
                        tr = rstd(ss, 1.0 / 128, sq.ap, 512, ss.t)
                        ty = stt(sq.ap, ob.ap, par(f"onorm{l}"), sq.ap, ALU.mult, ALU.mult, tr, tl, cst)
                        drop(ob, ty)
                        ty = tt(V, sq.ap, sq.ap, sg.ap, ALU.mult, ty, tg)
                        drop(sg, ty)
                        y.append(split(sq.ap, ty))
                        drop(sq, y[-1][2])
                        yield
                    for x in qd:
                        drop(x, tl)
                    for x in sp:
                        drop(x[2], tl)
                        drop(x[3], tl)
                for x in v + [lr, wl_]:
                    drop(x, tl)
                drop(rst, ts_)

            def memory_side(l):
                km, vm = [], [[None, None], [None, None]]
                mt = []
                acc = get()
                for j in range(4):
                    x = get()
                    x.t = dma(x.ap, ins["mem"][j], x.free)
                    mt.append(x)
                for j in range(4):
                    x = mt[j]
                    if j == 0:
                        ta = act(acc.ap, x.ap, ACT.Square, x.t, acc.free)
                    else:
                        sq = get()
                        t = act(sq.ap, x.ap, ACT.Square, x.t, sq.free)
                        ta = tt(V, acc.ap, acc.ap, sq.ap, ALU.add, t, ta)
                        drop(sq, ta)
                b = get("P")
                mm(b.ap[:, 0:256], ones, acc.ap[:, 0:256], True, False, b.free, ta, cst)
                b.t = mm(b.ap[:, 0:256], ones, acc.ap[:, 256:512], False, True, inc=True)
                tr = rstd(b, 1.0 / DM, acc.ap[:, 0:256], 256, b.t)
                mn, cuts = [], []
                for j in range(4):
                    x = mt[j]
                    for kk in range(2):
                        sl = slice(256 * kk, 256 * kk + 256)
                        t = stt(x.ap[:, sl], x.ap[:, sl], par(f"lnm{l}", 2 * j + kk), acc.ap[:, 0:256], ALU.mult, ALU.mult,
                                tr, x.t, cst)
                    p = split(x.ap, t)
                    drop(x, p[2])
                    mn += [p, p]
                    cuts += [slice(0, 256), slice(256, 512)]
                drop(acc, t)
                yield
                yield
                st.km, st.vm = km, vm
                for hd in range(4):
                    kt = get()
                    ss = get("P")
                    for kk in range(2):
                        b = project(("b", l, "xk", 2 * hd + kk), mn, n=256, cuts=cuts)
                        sq = get()
                        t = act(sq.ap[:, 0:256], b.ap[:, 0:256], ACT.Square, b.t, sq.free)
                        tk = act(kt.ap[:, 256 * kk:256 * kk + 256], b.ap[:, 0:256], ACT.Copy, b.t, kt.free, cst,
                                 scale=par(f"xkn{l}", kk))
                        drop(b, t, tk)
                        ss.t = mm(ss.ap[:, 0:256], ones, sq.ap[:, 0:256], kk == 0, kk == 1, t, ss.free, cst, inc=True)
                        if kk == 0:
                            drop(sq, ss.t)
                    tr = rstd(ss, 1.0 / 256, sq.ap[:, 0:256], 256, ss.t)
                    for kk in range(2):
                        kt.t = tt(V, kt.ap[:, 256 * kk:256 * kk + 256], kt.ap[:, 256 * kk:256 * kk + 256],
                                  sq.ap[:, 0:256], ALU.mult, tr, tk)
                    drop(sq, kt.t)
                    km.append(kt)
                    yield
                for half in range(2):
                    bs = project_tok(("b", l, "xv", half), mn, ntok=2, cuts=cuts)
                    for tq in range(2):
                        x = get()
                        x.t = cp(A, x.ap, bs[tq].ap, bs[tq].t, x.free)
                        drop(bs[tq], x.t)
                        vm[tq][half] = x
                    yield
                for p in mn[::2]:
                    drop_pair(p, bs[1].t)

            def cross(l, mem):
                mem.step()
                h = norm_x(f"lnx{l}", mem)
                while len(st.km) < 4:
                    mem.step()
                km, vm = st.km, st.vm
                y = []

                def queries(hd):
                    qs = []
                    sqs = []
                    for kk in range(2):
                        b = project(("b", l, "xq", 2 * hd + kk), h)
                        sq = get()
                        sq.t = act(sq.ap, b.ap, ACT.Square, b.t, sq.free)
                        q = get()
                        q.t = act(q.ap, b.ap, ACT.Copy, b.t, q.free, cst, scale=par(f"xqn{l}", kk))
                        drop(b, sq.t, q.t)
                        qs.append(q)
                        sqs.append(sq)
                        yield
                    ss = get("P")
                    for kk in range(2):
                        ss.t = mm(ss.ap, ones, sqs[kk].ap, kk == 0, kk == 1, sqs[kk].t, ss.free, cst, inc=True)
                    drop(sqs[0], ss.t)
                    sq = sqs[1]
                    tr = rstd(ss, 1.0 / 256, sq.ap, 512, ss.t)
                    for q in qs:
                        q.t = tt(V, q.ap, q.ap, sq.ap, ALU.mult, tr, q.t)
                    drop(sq, qs[1].t)
                    return qs

                def scores(qs, hd):
                    ps = []
                    for i in range(4):
                        b = get("P")
                        for kk in range(2):
                            t = mm(b.ap[:, 0:256], qs[kk].ap[:, 128 * i:128 * i + 128],
                                   km[hd].ap[:, 256 * kk:256 * kk + 256], kk == 0, kk == 1, b.free, qs[kk].t, km[hd].t,
                                   inc=(kk == 1))
                        m, p = get("S"), get()
                        tm = V.put(lambda e, m=m, b=b: e.reduce_max(m.ap[:, 1:2], b.ap[:, 0:256], AX.X, negate=True),
                                   (t, m.free))
                        tm = ts(V, m.ap[:, 0:1], m.ap[:, 1:2], 1.0 / 16, None, ALU.mult, None, tm)
                        te = act(p.ap[:, 0:256], b.ap[:, 0:256], ACT.Exp, tm, p.free, bias=m.ap[:, 0:1], scale=1.0 / 16,
                                 accum_out=m.ap[:, 2:3])
                        drop(b, te)
                        p.t = te
                        ps.append((p, m))
                    for q in qs:
                        drop(q, t)
                    for p, m in ps:
                        tr = recip(m.ap[:, 3:4], m.ap[:, 2:3], p.t)
                        p.t = ts(G, p.ap[:, 0:256], p.ap[:, 0:256], m.ap[:, 3:4], None, ALU.mult, None, tr, p.t)
                        drop(m, p.t)
                    return [p for p, _ in ps]

                def head(hd, qs):
                    ps = scores(qs, hd)
                    yield
                    bt = [get("P"), get("P")]
                    for kk in range(2):
                        for i in range(4):
                            t = tp(bt[kk].ap[:, 128 * i:128 * i + 128], ps[i].ap[:, 128 * kk:128 * kk + 128], ps[i].t,
                                   bt[kk].free, inc=(i == 3))
                        bt[kk].t = t
                    for p in ps:
                        drop(p, t)
                    pt = []
                    for kk in range(2):
                        x = get()
                        x.t = cp((V, A)[kk], x.ap, bt[kk].ap, bt[kk].t, x.free)
                        drop(bt[kk], x.t)
                        pt.append(x)
                    yield
                    for dc in range(2):
                        f = 256 * hd + 128 * dc
                        b = get("P")
                        for kk in range(2):
                            vv = vm[kk][f // 512]
                            t = mm(b.ap, vv.ap[:, f % 512:f % 512 + 128], pt[kk].ap, kk == 0, kk == 1, b.free, vv.t,
                                   pt[kk].t, inc=(kk == 1))
                        o = get()
                        to = cp(V, o.ap, b.ap, t, o.free)
                        drop(b, to)
                        y.append(split(o.ap, to))
                        drop(o, y[-1][2])
                    for x in pt:
                        drop(x, t)
                    last.append(t)

                last = []
                todo = [Aux(queries(0)), Aux(queries(1))]
                for q in todo:
                    while not q.done:
                        q.step()
                g = Aux(None)
                for hd in range(4):
                    qs = todo.pop(0).val
                    old, g = g, Aux(head(hd, qs))
                    nxt = Aux(queries(hd + 2) if hd < 2 else None)
                    todo.append(nxt)
                    old.step()
                    g.step()
                    if hd in (1, 2):
                        mem.step()
                    while not (nxt.done and old.done):
                        nxt.step()
                        old.step()
                while not (g.done and mem.done):
                    g.step()
                    mem.step()
                t = last[-1]
                for x in km + vm[0] + vm[1]:
                    drop(x, t)
                drop_h(h, t)
                out_product(("b", l, "xo"), y)

            def mlp(l, aux):
                h = norm_x(f"lnp{l}")
                xn = []
                for half in range(2):
                    y = []
                    for c in range(16):
                        b = project(("b", l, "w1", 16 * half + c), h)
                        r = get()
                        t = act(r.ap, b.ap, ACT.Relu, b.t, r.free)
                        drop(b, t)
                        t = tt(G, r.ap, r.ap, r.ap, ALU.mult, t)
                        y.append(split(r.ap, t))
                        drop(r, y[-1][2])
                    if half == 1:
                        drop_h(h, b.t)
                    if half == 0:
                        nxt = load_x(0)
                    for c in range(8):
                        if half == 0:
                            x = nxt
                            if c < 7:
                                nxt = load_x(c + 1)
                        else:
                            x = xn[c]
                        b = project(("b", l, "w2", c, 2 * half), y[0:8], last=False)
                        b = project(("b", l, "w2", c, 2 * half + 1), y[8:16], bank=b, first=False)
                        add_out(b, x)
                        if half == 0:
                            xn.append(x)
                        elif aux is not None:
                            aux.step()
                    drop_h(y, b.t)
                st.x = xn

            def mix_second(l, hid, mem):
                h = norm_x(f"lnmix{l}")
                ya, yb, yc = [], [], []
                m = [None] * 8
                while not hid.done:
                    hid.step()
                hyena(l, h, yb, hid.val)
                beside(attend_second(l, h, ya), gated("b", l, h, ((1, yb),), m, True))
                beside(gla(l, h, yc), gated("b", l, h, ((0, ya),), m, True))
                for _ in gated("b", l, h, ((2, yc),), m, False):
                    pass
                out_product(("b", l, "wo"), m, mem)

            st.x = []
            if order is not None:
                for i in range(NSP):
                    issue(i)
                state["issued"] = NSP
            for c in range(8):
                x = get()
                x.t = dma(x.ap, ins["x"][c], x.free)
                st.x.append(x)
            hid = [Aux(filter_mlp(l)) for l in range(2)]
            mem = [Aux(memory_side(l)) for l in range(2)]
            todo = [lambda: block_one(0, None), lambda: block_one(1, hid[0])]
            for l in range(2):
                todo += [lambda l=l: mix_second(l, hid[l], mem[l]), lambda l=l: cross(l, mem[l]),
                         lambda l=l: mlp(l, None if l else hid[1])]
            for f in todo[:steps]:
                f()
            for c in range(8):
                x = st.x[c]
                S.put(lambda e, c=c, x=x: e.dma_start(out[c], x.ap).then_inc(s_out, 16), x.t, inc=False)
            S.wait(Tok(s_out, 128))
            for i in range(len(s_misc)):
                S.wait(Tok(s_misc[i], 16 * mcount[i]))
            assert len(pools["F"]) == NF - 8 and len(pools["R"]) == NRT and len(pools["P"]) == 8, \
                {k: len(p) for k, p in pools.items()}
            return asked, rates, (M, V, A, G, S)

        _, plan, _ = emit(None, None)
        order, _, _ = emit(None, plan)
        _, _, (M, V, A, G, S) = emit(order, plan)

        block = ctx.enter_context(nc.Block())

        @block.tensor
        def _(e):
            M.play(e)

        @block.vector
        def _(e):
            V.play(e)

        @block.scalar
        def _(e):
            A.play(e)

        @block.gpsimd
        def _(e):
            G.play(e)

        @block.sync
        def _(e):
            S.play(e)


def tables():
    f = np.float32
    k = {}
    cst = np.zeros((128, 8, 128), f)
    p = np.arange(128)
    cst[:, 0] = np.eye(128)
    cst[:, 1] = 1
    cst[:, 2] = (p[:, None] // 64) == (p[None, :] // 64)
    for m in range(128):
        if m % 64 < 32:
            cst[m + 32, 3, m] = -1
        else:
            cst[m - 32, 3, m] = 1
        if m % 32 < 16:
            cst[m + 16, 4, m] = -1
        else:
            cst[m - 16, 4, m] = 1
    cst[:, 5] = np.where(p[None, :] <= p[:, None], 0, NEG)
    same = (p[:, None] // 64) == (p[None, :] // 64)
    cst[:, 6] = same & (p[:, None] <= p[None, :])
    cst[:, 7] = same & (p[:, None] > p[None, :])
    k["cst"] = cst
    rope = np.zeros((2, 2, 128, 512), f)
    inv = (f(1.0) / (f(10000.0) ** (np.arange(0, 64, 2, dtype=f) / f(64)))).astype(f)
    ang = np.arange(512, dtype=f)[:, None] * inv[None, :]
    rope[0, 0] = np.cos(ang).T[(p % 64) % 32]
    rope[0, 1] = np.sin(ang).T[(p % 64) % 32]
    inv = (f(10000.0) ** (-np.arange(16, dtype=f) / f(16))).astype(f)
    t = np.arange(512)
    pos = np.stack([t // 64, t % 64], 1).astype(f)
    ang = (pos[:, :, None] * inv).astype(f)
    q = p % 64
    rope[1, 0] = np.cos(ang)[:, q // 32, q % 16].T
    rope[1, 1] = np.sin(ang)[:, q // 32, q % 16].T
    k["rope"] = rope
    cnt = np.zeros((4, 16), f)
    for g in range(4):
        cnt[g] = f(1) / np.minimum(np.arange(16) + 1, 2 << g).astype(f)
    k["cnt"] = np.broadcast_to(cnt.reshape(1, 64), (128, 64)).copy()
    L = 512
    tn = np.arange(L, dtype=f) / f(L - 1)
    w = (f(2.0 * np.pi) * np.arange(L, dtype=f) / f(L)).astype(f)
    fr = np.linspace(1e-4, 15, 16, dtype=f)
    fw = w[:, None] * fr
    k["zpos"] = np.concatenate([tn[:, None], np.cos(fw), -np.sin(fw)], -1).T.astype(f).copy()
    deltas = np.abs(np.linspace(np.log(1e-2) / 0.3, np.log(1e-2) / 1.5, 512, dtype=f))
    k["win"] = np.exp(-tn[:, None] * deltas).astype(f).reshape(4, 128, 512)
    om = 2 * np.pi * (np.arange(512) + 0.5) / 1024
    a = np.arange(512)[:, None] * om[None, :]
    k["C"], k["Sn"] = np.cos(a).astype(f), np.sin(a).astype(f)
    return k


def layout(x):
    k = tables()
    place = {}
    ins = {n: k[n] for n in ("cst", "rope", "cnt", "zpos", "win")}
    flat = {}

    def fm(w):
        n = w.shape[0] // 128
        return w.reshape(n, 128, w.shape[1]).transpose(1, 0, 2)

    def add(arr, key, w):
        lst = flat.setdefault(arr, [0, []])
        n, cols = w.shape[1], w.shape[2]
        place[key] = (arr, lst[0], n, cols)
        lst[0] += w.size
        lst[1].append(np.ascontiguousarray(w).reshape(-1))

    def chunks(arr, l, name, w, c0=0):
        for c in range(w.shape[1] // 128):
            add(arr, (arr[1], l, name, c0 + c), fm(w[:, 128 * c:128 * c + 128]))

    def tok(arr, key, w):
        for j in range(4):
            v = w[256 * j:256 * j + 256].reshape(2, 128, 512).transpose(1, 0, 2).reshape(128, 8, 128)
            add(arr, key + (j,), v)

    for l in range(2):
        w = x["w_in"][l]
        arr = f"wa{l}"
        names = ["cb", "cc", "cx", "cgate", "q", "k", "v", "agate"]
        for i, n in enumerate(names):
            s = w[:, 512 * i:512 * i + 512]
            if n == "v":
                tok(arr, ("a", l, "v"), s)
            else:
                chunks(arr, l, n, s)
        chunks(arr, l, "iq", w[:, 4096:4608])
        add(arr, ("a", l, "ik", 0), fm(np.concatenate([w[:, 4608:4672]] + [w[:, 4672:4680]] * 8, 1)))
        chunks(arr, l, "pu", w[:, 4680:5192])
        chunks(arr, l, "pgate", w[:, 5192:5704])
        chunks(arr, l, "gate", w[:, 5704:8776])
        for br, n in enumerate(("w_out_conv", "w_out_attn", "w_out_pool")):
            for c in range(8):
                add(arr, ("a", l, "br", br, c), fm(x[n][l][:, 128 * c:128 * c + 128]))
        chunks(arr, l, "wo", x["w_o"][l])
        w = x["w_in_2"][l]
        arr = f"wb{l}"
        chunks(arr, l, "q", w[:, 0:512])
        add(arr, ("b", l, "k", 0), fm(w[:, 512:640]))
        add(arr, ("b", l, "v", 0), fm(w[:, 640:768]))
        chunks(arr, l, "hy", w[:, 768:2304])
        chunks(arr, l, "gq", w[:, 2304:2560])
        chunks(arr, l, "gk", w[:, 2560:2816])
        tok(arr, ("b", l, "gv"), w[:, 2816:3328])
        chunks(arr, l, "go", w[:, 3328:3840])
        lr = w[:, 3840:3872]
        add(arr, ("b", l, "lr", 0), fm(np.concatenate([lr] * 4, 1)))
        chunks(arr, l, "gate", w[:, 3872:6944])
        for br, n in enumerate(("w_br_attn_2", "w_br_hyena_2", "w_br_gla_2")):
            for c in range(8):
                add(arr, ("b", l, "br", br, c), fm(x[n][l][:, 128 * c:128 * c + 128]))
        chunks(arr, l, "wo", x["w_out_2"][l])
        chunks(arr, l, "xq", x["x_wq_2"][l])
        chunks(arr, l, "xk", x["x_wk_2"][l])
        for half in range(2):
            tok(arr, ("b", l, "xv", half), x["x_wv_2"][l][:, 512 * half:512 * half + 512])
        chunks(arr, l, "xo", x["x_wo_2"][l])
        chunks(arr, l, "w1", x["mlp_w1_2"][l])
        for c in range(8):
            for g in range(4):
                add(arr, ("b", l, "w2", c, g), fm(x["mlp_w2_2"][l][1024 * g:1024 * g + 1024, 128 * c:128 * c + 128]))
    for j in range(4):
        sl = slice(128 * j, 128 * j + 128)
        add("wd", ("dft", "f", j), np.concatenate([fm(k["C"][:, sl]), fm(k["Sn"][:, sl])], 1))
        add("wd", ("dft", "i", j), np.concatenate([fm(k["C"].T[:, sl]), fm(k["Sn"].T[:, sl])], 1))
        for d in "fi":
            for l in range(2):
                for o in range(2):
                    place["dft", d, j, l, o] = place["dft", d, j]
    for arr, (_, lst) in flat.items():
        ins[arr] = np.concatenate(lst)
    par = []

    def col(name, a):
        place["par", name] = sum(q.shape[1] for q in par)
        b = np.zeros((128, a.shape[1]), np.float32)
        b[0:a.shape[0]] = a
        par.append(b)

    def vec(name, a):
        col(name, a.reshape(-1, 128).T)

    for l in range(2):
        vec(f"ng{l}", x["norm_g"][l])
        vec(f"conv{l}", x["conv_w"][l])
        col(f"qg{l}", np.concatenate([x["q_norm_g"][l]] * 2)[:, None])
        col(f"kg{l}", np.concatenate([x["k_norm_g"][l]] * 2)[:, None])
        vec(f"pscale{l}", x["pool_scale"][l])
        vec(f"lnmix{l}", x["ln_mix_2"][l])
        col(f"aqn{l}", np.concatenate([x["attn_qnorm_2"][l]] * 2)[:, None])
        col(f"akn{l}", np.concatenate([x["attn_knorm_2"][l]] * 2)[:, None])
        vec(f"hconv{l}", x["hy_conv_2"][l])
        col(f"hb1{l}", x["hy_b1_2"][l][:, None])
        col(f"hb2{l}", x["hy_b2_2"][l][:, None])
        col(f"hf1{l}", x["hy_freq_2"][l, 0][:, None])
        col(f"hf2{l}", x["hy_freq_2"][l, 1][:, None])
        vec(f"glab{l}", x["gla_b_lr_2"][l])
        vec(f"onorm{l}", x["gla_onorm_2"][l])
        vec(f"lnx{l}", x["ln_x_2"][l])
        vec(f"lnm{l}", x["ln_mem_2"][l])
        vec(f"xqn{l}", x["x_qnorm_2"][l])
        vec(f"xkn{l}", x["x_knorm_2"][l])
        vec(f"lnp{l}", x["ln_mlp_2"][l])
    n = sum(q.shape[1] for q in par)
    par.append(np.zeros((128, PB_COLS - n), np.float32))
    ins["par"] = np.concatenate(par, 1)
    ins["poolw"] = x["pool_w"].transpose(0, 2, 1, 3).reshape(2, 128, 512)
    ins["skip"] = np.broadcast_to(x["hy_skip_2"][:, :, None, :], (2, 2, 128, 512))
    w12 = np.zeros((2, 64, 128), np.float32)
    w12[:, 0:33, 0:64] = x["hy_w1_2"]
    w12[:, :, 64:128] = x["hy_w2_2"]
    ins["w12"] = w12
    w3 = np.concatenate([x["hy_w3_2"], x["hy_b3_2"][:, None, :]], 1)
    ins["w3"] = w3.reshape(2, 65, 4, 512).transpose(0, 2, 1, 3)
    ins["wlr"] = x["gla_w_lr_2"]
    ins["mem"] = x["mem_2"][0].T.reshape(4, 2, 128, 256).transpose(0, 2, 1, 3).reshape(4, 128, 512)
    ins["x"] = x["x"][0].T.reshape(8, 128, 512)
    return {n: np.ascontiguousarray(a) for n, a in ins.items()}, place


def kernel(**inputs):
    import concourse.bacc as _bacc
    from concourse.bass_utils import run_bass_kernel_spmd as _run

    arrays, place = layout({n: np.asarray(a) for n, a in inputs.items()})
    nc = _bacc.Bacc("TRN2", target_bir_lowering=False, num_devices=1)
    aps = {n: nc.dram_tensor(f"in_{n}", a.shape, mybir.dt.from_np(a.dtype), kind="ExternalInput").ap()
           for n, a in arrays.items()}
    out = nc.dram_tensor("out_x", [8, 128, 512], mybir.dt.float32, kind="ExternalOutput").ap()
    program(nc, aps, place, out)
    r = _run(nc, [{f"in_{n}": a for n, a in arrays.items()}], core_ids=[0])
    o = np.asarray(r.results[0]["out_x"])
    return np.ascontiguousarray(o.reshape(1024, 512).T).reshape(1, 512, 1024)
```

```python
import numpy as np
import concourse.bass as bass
from concourse import mybir
from contextlib import ExitStack

SEQ = 512
DM = 1024
EPS = 1e-6
NEG = -1e30
GONE = -3e38
BIG = 3e38
MAGIC = 12582912.0

NF = 26
NRT = 56
NRAW = 3
NSP = 3
PB_COLS = 64 + 2 * 26 + 2 * 84


def program(nc, ins, place, out, steps=8):
    fp32 = mybir.dt.float32
    fp32r = mybir.dt.float32r
    ALU = mybir.AluOpType
    ACT = mybir.ActivationFunctionType
    AX = mybir.AxisListType

    ctx = ExitStack()
    with ctx:
        def sb(name, shape, dt=fp32):
            return ctx.enter_context(nc.sbuf_tensor(name, shape, dt))

        FT = sb("FT", [128, NF, 512])
        RT = sb("RT", [128, NRT, 512], fp32r)
        WRAW = sb("WRAW", [128, NRAW, 1024])
        WSP = sb("WSP", [128, NSP, 2, 1024], fp32r)
        CST = sb("CST", [128, 8, 128])
        PAR = sb("PAR", [128, PB_COLS])
        EPSC = sb("EPSC", [128, 2])
        SM = sb("SM", [128, 16, 16])
        banks = [ctx.enter_context(nc.psum_tensor(f"B{i}", [128, 512], fp32)) for i in range(8)]
        xs = [nc.dram_tensor(f"xs{i}", [8, 128, 512], fp32, kind="Internal").ap() for i in range(2)]

        eye, ones, pair = CST[:, 0, :], CST[:, 1, :], CST[:, 2, :]
        rotA, rotB, causal = CST[:, 3, :], CST[:, 4, :], CST[:, 5, :]
        maskf, maskb = CST[:, 6, :], CST[:, 7, :]

        class Tok:
            __slots__ = ("sem", "val")

            def __init__(self, sem, val):
                self.sem, self.val = sem, val

        class Queue:

            def __init__(self, sem):
                self.sem, self.n, self.q, self.seen = sem, 0, [], {}

            def wait(self, w):
                if w is None:
                    return
                if isinstance(w, Tok):
                    if self.seen.get(w.sem, 0) < w.val:
                        self.seen[w.sem] = w.val
                        self.q.append(("w", w.sem, w.val))
                    return
                for x in w:
                    self.wait(x)

            def put(self, fn, w, inc=True):
                best = {}

                def flat(t):
                    if t is None:
                        return
                    if isinstance(t, Tok):
                        if best.get(t.sem, 0) < t.val:
                            best[t.sem] = t.val
                        return
                    for x in t:
                        flat(x)
                flat(w)
                for s, v in best.items():
                    self.wait(Tok(s, v))
                if not inc:
                    self.q.append(("i", fn, None, 0))
                    return None
                self.n += 1
                self.q.append(("i", fn, self.sem, 1))
                return Tok(self.sem, self.n)

            def play(self, e):
                for it in self.q:
                    if it[0] == "w":
                        e.wait_ge(it[1], it[2])
                    else:
                        r = it[1](e)
                        if it[2] is not None:
                            r.then_inc(it[2], it[3])

        sems = [ctx.enter_context(nc.semaphore(f"s_{n}")) for n in ("pe", "dve", "act", "pool", "sp")]
        s_raw = [ctx.enter_context(nc.semaphore(f"s_raw{i}")) for i in range(NRAW)]
        s_misc = [ctx.enter_context(nc.semaphore(f"s_misc{i}")) for i in range(24)]
        s_out = ctx.enter_context(nc.semaphore("s_out"))

        class Tile:
            __slots__ = ("ap", "free", "t", "kind", "last", "used", "r")

            def __init__(self, ap, kind):
                self.ap, self.free, self.t, self.kind = ap, None, None, kind

        def emit(order, plan):
            rates = []
            M, V, A, G, S = (Queue(s) for s in sems)
            pools = {
                "F": [Tile(FT[:, i, :], "F") for i in range(NF)],
                "R": [Tile(RT[:, i, :], "R") for i in range(NRT)],
                "P": [Tile(b[:, :], "P") for b in banks],
                "S": [Tile(SM[:, i, :], "S") for i in range(16)],
            }

            def get(kind="F"):
                assert pools[kind], "no tile left: " + kind
                old = pools[kind].pop(0)
                new = Tile(old.ap, kind)
                new.free = old.free
                return new

            def drop(tile, *toks):
                tile.free = [x for x in toks]
                pools[tile.kind].append(tile)

            def tt(E, o, a, b, op, *w):
                return E.put(lambda e: e.tensor_tensor(o, a, b, op), w)

            def ts(E, o, a, s1, s2, op0, op1, *w):
                if s2 is None:
                    return E.put(lambda e: e.tensor_scalar(o, a, s1, None, op0), w)
                return E.put(lambda e: e.tensor_scalar(o, a, s1, s2, op0, op1), w)

            def stt(o, a, s, b, op0, op1, *w):
                return V.put(lambda e: e.scalar_tensor_tensor(o, a, s, b, op0, op1), w)

            def cp(E, o, a, *w):
                if E is A:
                    return A.put(lambda e: e.activation(o, a, ACT.Copy), w)
                return E.put(lambda e: e.tensor_copy(o, a), w)

            def act(o, a, f, *w, **k):
                return A.put(lambda e: e.activation(o, a, f, **k), w)

            def recip(o, a, *w):
                return V.put(lambda e: e.reciprocal(o, a), w)

            def memset(E, o, v, *w):
                return E.put(lambda e: e.memset(o, v), w)

            work = [0.0]

            def mm(o, l, r, start, stop, *w, inc=False):
                work[0] += r.free_size() * (4 if r.dtype == fp32 else 1)
                return M.put(lambda e: e.matmul(o, l, r, start=start, stop=stop), w, inc)

            def tp(o, a, *w, inc=False):
                return M.put(lambda e: e.transpose(o, a, eye[0:a.shape[0], 0:a.shape[0]]), (w, cst), inc)

            misc = [0]
            mcount = [0] * len(s_misc)

            def dma(o, a, *w):
                i = misc[0] % len(s_misc)
                misc[0] += 1
                S.wait(Tok(s_misc[i], mcount[i] * 16))
                S.put(lambda e: e.dma_start(o, a).then_inc(s_misc[i], 16), w, inc=False)
                mcount[i] += 1
                return Tok(s_misc[i], mcount[i] * 16)

            asked = []
            raw_free = [None] * NRAW
            sp_free = [None] * NSP
            state = {"issued": 0, "used": 0}
            ready = {}

            def issue(i):
                arr, off, n, cols = place[order[i]]
                r, s = i % NRAW, i % NSP
                m = n * cols
                src = ins[arr][off:off + 128 * m].rearrange("(p m) -> p m", p=128)
                dst = WRAW[:, r, 0:m]
                S.put(lambda e: e.dma_start(dst, src).then_inc(s_raw[r], 16), raw_free[r], inc=False)
                t = Tok(s_raw[r], 16 * (i // NRAW + 1))
                hi, lo = WSP[:, s, 0, 0:m], WSP[:, s, 1, 0:m]
                a = A.put(lambda e: e.activation(hi, dst, ACT.Copy), (t, sp_free[s]))
                E = G if i % 2 else V
                b = E.put(lambda e: e.tensor_tensor(lo, dst, hi.bitcast(fp32), ALU.subtract), (t, a, sp_free[s]))
                raw_free[r] = (a, b)
                ready[i] = (hi.rearrange("p (n c) -> p n c", n=n), lo.rearrange("p (n c) -> p n c", n=n), (a, b))

            def weight(key):
                i = state["used"]
                state["used"] += 1
                asked.append(key)
                if order is None:
                    arr, off, n, cols = place[key]
                    z = WSP[:, 0, 0, 0:n * cols].rearrange("p (n c) -> p n c", n=n)
                    return z, z, None
                assert order[i] == key
                while state["issued"] < min(i + NSP, len(order)):
                    issue(state["issued"])
                    state["issued"] += 1
                return ready.pop(i)

            def weight_done(tok):
                sp_free[(state["used"] - 1) % NSP] = tok

            def mm3(o, L, R, first, last, *w, inc=False):
                mm(o, L[0], R[0], first, False, w)
                mm(o, L[0], R[1], False, False)
                return mm(o, L[1], R[0], False, last, inc=inc)

            def split(src, *w, E=None):
                hi, lo = get("R"), get("R")
                a = A.put(lambda e: e.activation(hi.ap, src, ACT.Copy), (w, hi.free))
                b = (E or V).put(lambda e: e.tensor_tensor(lo.ap, src, hi.ap.bitcast(fp32), ALU.subtract), (w, a, lo.free))
                hi.t = (a, b)
                return hi, lo, (a, b)

            def drop_pair(x, *toks):
                drop(x[0], *toks)
                drop(x[1], *toks)

            def cols(x, sl):
                return x[0].ap[:, sl], x[1].ap[:, sl]

            FULL = slice(0, 512)

            def project(key, h, n=512, bank=None, first=True, last=True, cuts=None, raw=False):
                wh, wl, wt = weight(key)
                k = len(h)
                if bank is None:
                    bank = get("P")
                for i in range(k):
                    sl = FULL if cuts is None else cuts[i]
                    t = mm3(bank.ap[:, 0:n], (wh[:, i, :], wl[:, i, :]), cols(h[i], sl), first and i == 0,
                            last and i == k - 1, wt, bank.free, h[i][2], inc=(i == k - 1))
                weight_done(t)
                bank.t = t
                if isinstance(h, Normed):
                    r = h.factor()
                    if not raw:
                        bank.t = h.used(tt(V, bank.ap, bank.ap, r.ap, ALU.mult, t, r.t))
                return bank

            def scaled(key, h, rows=128):
                b = project(key, h, raw=True)
                r = h.factor()
                x = get()
                x.t = h.used(tt(V, x.ap[0:rows], b.ap[0:rows], r.ap[0:rows], ALU.mult, b.t, r.t, x.free))
                drop(b, x.t)
                return x

            def project_tok(key, h, width=512, ntok=4, cuts=None):
                bs = [get("P") for _ in range(ntok)]
                for j in range(4):
                    wh, wl, wt = weight(key + (j,))
                    for tq in range(ntok):
                        for kk in range(2):
                            k = 2 * j + kk
                            base = 0 if cuts is None else cuts[k].start
                            sl = slice(base + 128 * tq, base + 128 * tq + 128)
                            t = mm3(bs[tq].ap[:, 0:512], cols(h[k], sl),
                                    (wh[:, 4 * kk:4 * kk + 4, :].rearrange("p a c -> p (a c)"),
                                     wl[:, 4 * kk:4 * kk + 4, :].rearrange("p a c -> p (a c)")),
                                    k == 0, k == 7, wt, bs[tq].free, h[k][2], inc=(kk == 1))
                        bs[tq].t = t
                    weight_done(t)
                return bs

            cst = [dma(CST[:, :, :], ins["cst"]), dma(PAR[:, :], ins["par"])]

            eps, eps2 = EPSC[:, 0:1], EPSC[:, 1:2]
            teps = memset(V, eps, EPS)

            def par(name, i=0, rows=128):
                c = place["par", name] + i
                return PAR[0:rows, c:c + 1]

            def rstd(bank, scale, o, n=512, *w):
                b = act(o, bank.ap[:, 0:n], ACT.Sqrt, bank.t, w, teps, scale=scale, bias=eps)
                drop(bank, b)
                return recip(o, o, b)

            class State:
                x = None
                xd = None
                h = None

            st = State()
            xcount = [0]

            class Normed(list):

                def __init__(self, gname):
                    super().__init__()
                    self.gname = gname
                    self.acc = get()
                    self.dst = xs[xcount[0] % 2]
                    xcount[0] += 1
                    self.xd = []
                    self.r = self.rt = None
                    self.last = {}

                def used(self, t):
                    self.last[id(t.sem)] = t
                    return t

                def add(self, x):
                    c = len(self)
                    g = par(self.gname, c)
                    hi, lo = get("R"), get("R")
                    a = act(hi.ap, x.ap, ACT.Copy, x.t, hi.free, cst, scale=g)
                    b = stt(lo.ap, x.ap, g, hi.ap.bitcast(fp32), ALU.mult, ALU.subtract, x.t, a, lo.free, cst)
                    self.append((hi, lo, (a, b)))
                    acc = self.acc
                    if c == 0:
                        t = acc.t = act(acc.ap, x.ap, ACT.Square, x.t, acc.free)
                    else:
                        sq = get()
                        t = act(sq.ap, x.ap, ACT.Square, x.t, sq.free)
                        if c == 7:
                            act(eps2, eps, ACT.Sqrt, teps)
                        acc.t = tt(V if c > 5 else G, acc.ap, acc.ap, sq.ap, ALU.add, t, acc.t)
                        drop(sq, acc.t)
                    d = dma(self.dst[c], x.ap, x.t)
                    self.xd.append((self.dst[c], d))
                    drop(x, a, b, t, d)

                def factor(self):
                    if self.r is None:
                        acc = self.acc
                        bank = get("P")
                        bank.t = mm(bank.ap, ones, acc.ap, True, True, bank.free, acc.t, cst, inc=True)
                        acc.t = rstd(bank, 1.0 / DM, acc.ap, 512, bank.t)
                        self.r = acc
                    return self.r

                def by_token(self):
                    if self.rt is None:
                        r = self.factor()
                        b = get("P")
                        for i in range(4):
                            t = mm(b.ap[:, i:i + 1], r.ap[:, 128 * i:128 * i + 128], eye[:, 0:1], True, True, b.free,
                                   r.t, cst, inc=(i == 3))
                        self.used(t)
                        self.rt = get("S")
                        self.rt.t = cp(V, self.rt.ap[:, 0:4], b.ap[:, 0:4], t, self.rt.free)
                        drop(b, self.rt.t)
                    return self.rt

            def start_norm():
                names = ["ng0", "ng1", "lnmix0", "lnx0", "lnp0", "lnmix1", "lnx1", "lnp1"]
                i = xcount[0]
                st.h = Normed(names[i]) if i < min(steps, 8) else None
                return st.h

            def take_norm():
                st.xd = st.h.xd
                return st.h

            def load_x(c):
                x = get()
                src, d = st.xd[c]
                x.t = dma(x.ap, src, x.free, d)
                return x

            def drop_h(h, *toks):
                for p in h:
                    drop_pair(p, *toks)
                if isinstance(h, Normed):
                    drop(h.r, *h.last.values())
                    if h.rt is not None:
                        drop(h.rt, *h.last.values())

            def add_out(bank, x, *w):
                x.t = tt(V, x.ap, bank.ap, x.ap, ALU.add, bank.t, x.t, w)
                drop(bank, x.t)
                return x

            class Aux:

                def __init__(self, gen):
                    self.gen, self.done, self.val = gen, gen is None, None

                def step(self):
                    if not self.done:
                        try:
                            next(self.gen)
                        except StopIteration as e:
                            self.done, self.val = True, e.value

            def beside(main, side):
                i = len(rates)
                rates.append(None)
                rate = plan[i] if plan is not None else 0.0
                side = Aux(side)
                steps, credit, total = 0, 0.0, 0.0
                for room in main:
                    room = 1 if room is None else room
                    steps += room
                    credit += rate * room
                    while credit > 0 and not side.done:
                        w0 = work[0]
                        side.step()
                        credit -= work[0] - w0
                        total += work[0] - w0
                while not side.done:
                    w0 = work[0]
                    side.step()
                    total += work[0] - w0
                rates[i] = total / max(steps, 1)

            def short_conv(src, st_tok, o, w3, shift):
                mid = shift
                t = ts(V, o, src, w3[mid], None, ALU.mult, None, st_tok, cst)
                for j in range(3):
                    d = j - shift
                    if d == 0:
                        continue
                    if d < 0:
                        t = stt(o[:, -d:512], src[:, 0:512 + d], w3[j], o[:, -d:512], ALU.mult, ALU.add, t)
                    else:
                        t = stt(o[:, 0:512 - d], src[:, d:512], w3[j], o[:, 0:512 - d], ALU.mult, ALU.add, t)
                return t

            def conv_branch(l, h, y):
                for c in range(4):
                    cc = scaled(("a", l, "cc", c), h)
                    t = h.used(tt(G, cc.ap, cc.ap, h.r.ap, ALU.mult, cc.t, h.r.t))
                    yield
                    bx = project(("a", l, "cx", c), h, raw=True)
                    tz = tt(V, cc.ap, bx.ap, cc.ap, ALU.mult, bx.t, t)
                    drop(bx, tz)
                    yc = get()
                    V.wait(yc.free)
                    ty = short_conv(cc.ap, tz, yc.ap, [par(f"conv{l}", 4 * j + c) for j in range(3)], 2)
                    drop(cc, ty)
                    yield
                    bg = project(("a", l, "cgate", c), h)
                    sg = get()
                    tg = act(sg.ap, bg.ap, ACT.Silu, bg.t, sg.free)
                    drop(bg, tg)
                    ty = tt(V, yc.ap, yc.ap, sg.ap, ALU.mult, tg, ty)
                    drop(sg, ty)
                    yield
                    ty = h.used(tt(G, yc.ap, yc.ap, h.r.ap, ALU.mult, ty, h.r.t))
                    bb = project(("a", l, "cb", c), h, raw=True)
                    ty = tt(V, yc.ap, bb.ap, yc.ap, ALU.mult, bb.t, ty)
                    drop(bb, ty)
                    y.append(split(yc.ap, ty))
                    drop(yc, y[-1][2])
                    yield

            def pool_branch(l, h, y):
                pwt = get()
                pwt.t = dma(pwt.ap, ins["poolw"][l], pwt.free)
                ict = get()
                ict.t = dma(ict.ap[:, 0:64], ins["cnt"], ict.free)
                late = []

                def mixed(g, p, tp_, sg):
                    bm = get("P")
                    tm = mm(bm.ap, pwt.ap[:, 128 * g:128 * g + 128], p.ap, True, True, bm.free, tp_, pwt.t, inc=True)
                    drop(p, tm)
                    ty = stt(sg.ap, bm.ap, par(f"pscale{l}", g), sg.ap, ALU.mult, ALU.mult, tm, sg.t, cst)
                    drop(bm, ty)
                    y.append(split(sg.ap, ty))
                    drop(sg, y[-1][2])
                    return tm

                for g in range(4):
                    w = 2 << g
                    u = scaled(("a", l, "pu", g), h)
                    tu = u.t
                    src, tsrc = u, tu
                    k = 1
                    while k < w:
                        o = get()
                        a = tt(G, o.ap[:, k:512], src.ap[:, k:512], src.ap[:, 0:512 - k], ALU.add, tsrc, o.free)
                        b = cp(G, o.ap[:, 0:k], src.ap[:, 0:k], tsrc, o.free)
                        if src is not u:
                            drop(src, b)
                        src, tsrc = o, b
                        k *= 2
                    p = get()
                    a = stt(p.ap, src.ap, 1.0 / w, u.ap, ALU.mult, ALU.subtract, tsrc, tu, p.free)
                    b = tt(V, p.ap[:, 0:16], src.ap[:, 0:16], ict.ap[:, 16 * g:16 * g + 16], ALU.mult, a, ict.t)
                    c = tt(V, p.ap[:, 0:16], p.ap[:, 0:16], u.ap[:, 0:16], ALU.subtract, b)
                    drop(src, b)
                    drop(u, c)
                    yield
                    bg = project(("a", l, "pgate", g), h)
                    sg = get()
                    sg.t = act(sg.ap, bg.ap, ACT.Silu, bg.t, sg.free)
                    drop(bg, sg.t)
                    yield
                    if late:
                        tm = mixed(*late.pop())
                    late.append((g, p, c, sg))
                yield
                tm = mixed(*late.pop())
                drop(pwt, tm)
                drop(ict, b)

            def rope(key, h, cos, sin, rot, g=None, pre=None, query=False):
                if g is None:
                    x = scaled(key, h)
                    t0 = x.t
                else:
                    bank = project(key, h)
                    x = get()
                    sq = get()
                    tsq = act(sq.ap, bank.ap, ACT.Square, bank.t, sq.free)
                    t0 = act(x.ap, bank.ap, ACT.Copy, bank.t, x.free, cst, scale=g)
                    drop(bank, tsq, t0)
                yield
                if query:
                    ss = get("P")
                    for i in range(4):
                        t = mm(ss.ap[:, 2 * i:2 * i + 2], sq.ap[:, 128 * i:128 * i + 128], pair[:, ::64], True, True,
                               ss.free, tsq, cst, inc=(i == 3))
                    drop(sq, t)
                    ss.t = t
                elif g is not None:
                    ss = get("P")
                    ss.t = mm(ss.ap, pair, sq.ap, True, True, ss.free, tsq, cst, inc=True)
                br = get("P")
                tr = mm(br.ap, rot, x.ap, True, True, br.free, t0, cst, inc=True)
                o = get()
                t1 = tt(V, o.ap, br.ap, sin.ap, ALU.mult, tr, sin.t, o.free)
                drop(br, t1)
                tpre = None if pre is None else pre(x, t0)
                t2 = tt(G, x.ap, x.ap, cos.ap, ALU.mult, t0, tr, cos.t, tpre)
                t3 = tt(V, o.ap, o.ap, x.ap, ALU.add, t1, t2)
                drop(x, t3)
                if query:
                    o.r = get("S")
                    tn = rstd(ss, 1.0 / 64, o.r.ap[:, 0:8], 8, o.r.free)
                    o.r.t = ts(V, o.r.ap[:, 0:8], o.r.ap[:, 0:8], 0.125, None, ALU.mult, None, tn)
                elif g is not None:
                    tn = rstd(ss, 1.0 / 64, sq.ap, 512, ss.t)
                    t3 = tt(V, o.ap, o.ap, sq.ap, ALU.mult, t3, tn)
                    drop(sq, t3)
                o.t = t3
                yield
                return o

            def tables(which):
                cos, sin = get(), get()
                cos.t = dma(cos.ap, ins["rope"][which, 0], cos.free)
                sin.t = dma(sin.ap, ins["rope"][which, 1], sin.free)
                return cos, sin

            def head_pair(q, ks, v, vcol, causal_bias, finish, done_q):
                ob = get("P")
                sums = get("S")
                todo = []
                gone = []

                def scores(i, hh):
                    n = 128 * (i + 1) if causal_bias is not None else 512
                    half = slice(64 * hh, 64 * hh + 64)
                    b = get("P")
                    t = t0 = mm(b.ap[:, 0:n], q.ap[half, 128 * i:128 * i + 128], ks[hh].ap[half, 0:n], True, True,
                                b.free, q.t, ks[hh].t, inc=True)
                    p = get()
                    m = get("S")
                    r = q.r.ap[:, 2 * i + hh:2 * i + hh + 1]
                    if causal_bias is not None:
                        bias, tb = causal_bias[i]
                        t = V.put(lambda e: e.tensor_tensor_reduce(
                            out=p.ap[:, 0:n], in0=b.ap[:, 0:n], in1=bias, scale=1.0, scalar=NEG, op0=ALU.add,
                            op1=ALU.max, accum_out=m.ap[:, 1:2]), (t, tb, p.free, m.free))
                        drop(b, t)
                        tm = ts(V, m.ap[:, 0:1], m.ap[:, 1:2], -1.0, r, ALU.mult, ALU.mult, t, q.r.t)
                        te = act(p.ap[:, 0:n], p.ap[:, 0:n], ACT.Exp, tm, sums.free, bias=m.ap[:, 0:1], scale=r,
                                 accum_out=sums.ap[:, 2 * i + hh:2 * i + hh + 1])
                    else:
                        tm = V.put(lambda e: e.reduce_max(m.ap[:, 1:2], b.ap[:, 0:n], AX.X, negate=True), (t, m.free))
                        tm = ts(V, m.ap[:, 0:1], m.ap[:, 1:2], r, None, ALU.mult, None, tm, q.r.t)
                        te = act(p.ap[:, 0:n], b.ap[:, 0:n], ACT.Exp, tm, sums.free, p.free, bias=m.ap[:, 0:1],
                                 scale=r, accum_out=sums.ap[:, 2 * i + hh:2 * i + hh + 1])
                        drop(b, te)
                    drop(m, te)
                    q.free = t0
                    q.r.used = te
                    return i, hh, n, p, te

                def turned(i, hh, n, p, te):
                    b = get("P")
                    for k in range(n // 128):
                        t = tp(b.ap[:, 128 * k:128 * k + 128], p.ap[:, 128 * k:128 * k + 128], te, b.free,
                               inc=(k == n // 128 - 1))
                    drop(p, t)
                    pt = get()
                    pt.t = cp(V if hh else A, pt.ap[:, 0:n], b.ap[:, 0:n], t, pt.free)
                    drop(b, pt.t)
                    gone.append(te)
                    return i, hh, n, pt

                def values(i, hh, n, pt):
                    dst = ob.ap[:, 64 * (2 * i + hh):64 * (2 * i + hh) + 64]
                    for k in range(n // 128):
                        t = mm(dst, pt.ap[:, 128 * k:128 * k + 128], v[k].ap[:, vcol[hh]:vcol[hh] + 64],
                               k == 0, k == n // 128 - 1, pt.t, ob.free, v[k].t, inc=(k == n // 128 - 1))
                    drop(pt, t)
                    ob.t = t

                def onward():
                    if todo:
                        ready_.append(turned(*todo.pop(0)))
                        if len(ready_) > 2:
                            values(*ready_.pop(0))
                    elif ready_:
                        values(*ready_.pop(0))

                def rest():
                    while todo or ready_:
                        onward()
                        yield
                    yield from normed(ob, sums, gone[-1], finish)

                ready_ = []
                units = [(i, hh) for i in range(4) for hh in range(2)]
                for u in units:
                    todo.append(scores(*u))
                    if len(todo) > 3:
                        onward()
                    yield
                drop(q.r, q.r.used)
                done_q(q, ks, q.free)
                return rest()

            def normed(ob, sums, te, finish):
                rs = get("S")
                t = recip(rs.ap[:, 0:8], sums.ap[:, 0:8], te, rs.free)
                drop(sums, t)
                on = get()
                t = tt(V, on.ap.rearrange("p (u d) -> p u d", d=64), ob.ap.rearrange("p (u d) -> p u d", d=64),
                       rs.ap[:, 0:8].unsqueeze(2).to_broadcast([128, 8, 64]), ALU.mult, t, ob.t, on.free)
                drop(ob, t)
                drop(rs, t)
                yield
                b = get("P")
                for i in range(4):
                    tb = tp(b.ap[:, 128 * i:128 * i + 128], on.ap[:, 128 * i:128 * i + 128], t, b.free, inc=(i == 3))
                drop(on, tb)
                b.t = tb
                f = finish(b)
                yield
                return f

            def index_scores(l, h, cos, sin):
                iw = get("S")
                iw2 = get("S")
                sc8 = 8.0 ** -0.5

                def head_weights(x, t0):
                    bw = get("P")
                    for i in range(4):
                        t = M.put(lambda e, i=i: e.transpose(bw.ap[:, 8 * i:8 * i + 8], x.ap[64:72, 128 * i:128 * i + 128],
                                                             eye[64:72, 64:72]), (t0, bw.free, cst), i == 3)
                    a = ts(V, iw.ap[:, 0:16], bw.ap[:, 0:16], sc8, None, ALU.mult, None, t, iw.free)
                    b = ts(V, iw2.ap[:, 0:16], bw.ap[:, 16:32], sc8, None, ALU.mult, None, t, iw2.free)
                    drop(bw, b)
                    iw.t = b
                    return b

                ik = yield from rope(("a", l, "ik", 0), h, cos, sin, rotA, None, head_weights)
                tiw = iw.t
                ik.t = cp(A, ik.ap[64:128, :], ik.ap[0:64, :], ik.t)
                acc = [get() for _ in range(3)]
                yield
                nxt = Aux(rope(("a", l, "iq", 0), h, cos, sin, rotA))
                while not nxt.done:
                    nxt.step()
                    yield
                for c in range(4):
                    iq = nxt.val
                    nxt = Aux(rope(("a", l, "iq", c + 1), h, cos, sin, rotA) if c < 3 else None)
                    for hh in range(2):
                        hd = 2 * c + hh
                        half = slice(64 * hh, 64 * hh + 64)
                        for i in range(1, 4):
                            n = 128 * (i + 1)
                            bs = get("P")
                            t = mm(bs.ap[:, 0:n], iq.ap[half, 128 * i:128 * i + 128], ik.ap[half, 0:n], True, True,
                                   bs.free, iq.t, ik.t, inc=True)
                            r = get()
                            tr = act(r.ap[:, 0:n], bs.ap[:, 0:n], ACT.Relu, t, r.free, scale=0.125)
                            drop(bs, tr)
                            z = acc[i - 1]
                            src = (iw if i < 2 else iw2).ap
                            wcol = src[:, 8 * (i % 2) + hd:8 * (i % 2) + hd + 1]
                            if hd == 0:
                                z.t = ts(V, z.ap[:, 0:n], r.ap[:, 0:n], wcol, None, ALU.mult, None, tr, z.free, tiw)
                            else:
                                z.t = stt(z.ap[:, 0:n], r.ap[:, 0:n], wcol, z.ap[:, 0:n], ALU.mult, ALU.add, tr, z.t)
                            drop(r, z.t)
                            if i % 2:
                                nxt.step()
                                yield
                    drop(iq, t)
                drop(ik, t)
                drop(iw, acc[0].t, acc[2].t)
                drop(iw2, acc[1].t, acc[2].t)
                return acc

            def select_keys(acc, bias):
                m8 = get("S")
                for i in range(1, 4):
                    z = acc[i - 1]
                    n = 128 * (i + 1)
                    za = z.ap[:, 0:n]
                    t = tt(V, z.ap[:, 128 * i:n], z.ap[:, 128 * i:n], causal, ALU.add, z.t, cst)
                    for r in range(16):
                        t = V.put(lambda e, za=za: e.max(m8.ap[:, 0:8], za), (t, m8.free))
                        t = V.put(lambda e, za=za: e.match_replace(za, m8.ap[:, 0:8], za, GONE), (t,))
                        yield
                    t = ts(V, za, za, GONE, NEG, ALU.not_equal, ALU.mult, t)
                    bias[i] = (za, t)
                drop(m8, t)

            def attend_first(l, h, y):
                bias = {0: (causal, cst)}
                cos, sin = tables(0)
                acc = yield from index_scores(l, h, cos, sin)
                sel = Aux(select_keys(acc, bias))

                def values_in():
                    v = []
                    for i, b in enumerate(project_tok(("a", l, "v"), h)):
                        x = get()
                        rt = h.by_token()
                        x.t = h.used(act(x.ap, b.ap, ACT.Copy, b.t, x.free, rt.t, scale=rt.ap[:, i:i + 1]))
                        drop(b, x.t)
                        v.append(x)
                    yield
                    return v

                def qk(c):
                    q = yield from rope(("a", l, "q", c), h, cos, sin, rotA, par(f"qg{l}"), query=True)
                    k = yield from rope(("a", l, "k", c), h, cos, sin, rotA, par(f"kg{l}"))
                    return q, k

                sel.step()
                sel.step()
                va, nxt = Aux(values_in()), Aux(qk(0))
                while not (sel.done and va.done and nxt.done):
                    sel.step()
                    if not nxt.done:
                        nxt.step()
                    else:
                        va.step()
                    yield 2
                v = va.val
                last = []
                tail = Aux(None)
                for c in range(4):
                    while not nxt.done:
                        nxt.step()
                    q, k = nxt.val
                    nxt = Aux(qk(c + 1) if c < 3 else None)

                    def finish(b, c=c):
                        bg = project(("a", l, "agate", c), h)
                        sg = get()
                        tg = act(sg.ap, bg.ap, ACT.Silu, bg.t, sg.free)
                        drop(bg, tg)
                        ty = tt(V, sg.ap, b.ap, sg.ap, ALU.mult, b.t, tg)
                        drop(b, ty)
                        y.append(split(sg.ap, ty))
                        drop(sg, y[-1][2])
                        last.append(b.t)

                    def done_q(q, ks, t):
                        drop(q, t)
                        drop(ks[0], t)

                    g = Aux(head_pair(q, (k, k), v, (128 * c, 128 * c + 64), bias, finish, done_q))
                    while not g.done:
                        g.step()
                        tail.step()
                        nxt.step()
                        yield
                    tail = Aux(g.val)
                while not tail.done:
                    tail.step()
                    yield
                for x in v:
                    drop(x, last)
                drop(cos, k.t)
                drop(sin, k.t)
                for x in acc:
                    drop(x, last)

            def gated(kind, l, h, ys, m, keep):
                late = []

                def parts():
                    for c, s, t in late:
                        m[c] = split(s.ap, t)
                        drop(s, m[c][2])
                    late.clear()

                for c in range(8):
                    s = None
                    for br, y in ys:
                        bg = project((kind, l, "gate", 8 * br + c), h)
                        sg = get()
                        tg = act(sg.ap, bg.ap, ACT.Sigmoid, bg.t, sg.free)
                        drop(bg, tg)
                        yield
                        by = project((kind, l, "br", br, c), y)
                        parts()
                        t = tt(V, sg.ap, by.ap, sg.ap, ALU.mult, by.t, tg)
                        drop(by, t)
                        if s is None:
                            s, tm = sg, t
                        else:
                            tm = tt(G, s.ap, s.ap, sg.ap, ALU.add, tm, t)
                            drop(sg, tm)
                    if m[c] is not None:
                        for part in m[c][0:2]:
                            tm = tt(G, s.ap, s.ap, part.ap.bitcast(fp32), ALU.add, tm, m[c][2])
                        drop_pair(m[c], tm)
                    late.append((c, s, tm))
                    yield
                parts()
                for br, y in ys:
                    drop_h(y, by.t)
                if not keep:
                    drop_h(h, by.t)

            def out_product(key, y, aux=None):
                st.x = []
                nm = start_norm()
                nxt = load_x(0)
                for c in range(8):
                    x = nxt
                    if c < 7:
                        nxt = load_x(c + 1)
                    b = project(key + (c,), y)
                    st.x.append(add_out(b, x))
                    if nm is not None and c:
                        nm.add(st.x[c - 1])
                    if aux is not None:
                        aux.step()
                if nm is not None:
                    nm.add(x)
                drop_h(y, b.t)

            def all_of(*gens):
                for g in gens:
                    yield from g

            def block_one(l, aux):
                h = take_norm()
                ya, yb, yc = [], [], []
                m = [None] * 8
                side = all_of(conv_branch(l, h, ya), pool_branch(l, h, yc),
                              gated("a", l, h, ((0, ya), (2, yc)), m, True))
                beside(attend_first(l, h, yb), side)
                for _ in gated("a", l, h, ((1, yb),), m, False):
                    pass
                out_product(("a", l, "wo"), m, aux)

            def filters(l, o, hid, R):
                w3 = []
                for d in range(2):
                    w = get()
                    w.t = dma(w.ap[0:65, :], ins["w3"][l, 2 * o + d], w.free)
                    w3.append(w)
                acc = get()
                for tq in range(4):
                    win = get()
                    win.t = dma(win.ap, ins["win"][tq], win.free)
                    fs = []
                    for d in range(2):
                        b = get("P")
                        t = mm(b.ap, hid.ap[0:65, 128 * tq:128 * tq + 128], w3[d].ap[0:65, :], True, True, b.free,
                               hid.t, w3[d].t, inc=True)
                        f = get()
                        f.t = tt(V, f.ap, b.ap, win.ap, ALU.mult, t, win.t, f.free)
                        drop(b, f.t)
                        if d == 1 and tq == 0:
                            f.t = memset(V, f.ap[0:1, :], 0.0, f.t)
                        fs.append(f)
                    drop(win, fs[1].t, fs[0].t)
                    hid.last = t
                    for w in w3:
                        w.free = t
                    s, df = get(), get()
                    ta = tt(V, s.ap, fs[0].ap, fs[1].ap, ALU.add, fs[0].t, fs[1].t, s.free)
                    td = tt(G, df.ap, fs[0].ap, fs[1].ap, ALU.subtract, fs[0].t, fs[1].t, df.free)
                    R[0].append(split(s.ap, ta))
                    drop(s, R[0][-1][2])
                    R[1].append(split(df.ap, td))
                    drop(df, R[1][-1][2])
                    yield
                    for d in range(2):
                        f = fs[d]
                        if tq == 0 and d == 0:
                            tacc = act(acc.ap, f.ap, ACT.Abs, f.t, acc.free)
                            drop(f, tacc, ta, td)
                        else:
                            t1 = act(f.ap, f.ap, ACT.Abs, f.t, ta, td)
                            tacc = tt(G, acc.ap, acc.ap, f.ap, ALU.add, t1, tacc)
                            drop(f, tacc)
                for w in w3:
                    drop(w, t)
                yield
                b = get("P")
                t = mm(b.ap, ones, acc.ap, True, True, b.free, tacc, cst, inc=True)
                t = ts(V, acc.ap, b.ap, EPS, None, ALU.add, None, t)
                drop(b, t)
                t = recip(acc.ap, acc.ap, t)
                acc.t = ts(V, acc.ap, acc.ap, 2.0 / 1024, None, ALU.mult, None, t)
                return acc

            def sine(bank, rows, b1, fr, o, ow):
                n, x = get(), get()
                t = ts(V, x.ap[0:rows], bank.ap[0:rows], b1, fr, ALU.add, ALU.mult, bank.t, x.free, cst)
                drop(bank, t)
                tn = ts(V, n.ap[0:rows], x.ap[0:rows], 1.0 / (2 * np.pi), MAGIC, ALU.mult, ALU.add, t, n.free)
                tn = ts(V, n.ap[0:rows], n.ap[0:rows], MAGIC, None, ALU.subtract, None, tn)
                c1 = 6.28125
                c2 = float(np.float32(2 * np.pi - c1))
                c2 = float(np.frombuffer((np.array([c2], np.float32).view(np.uint32) & np.uint32(0xFFFFF000)).tobytes(), np.float32)[0])
                c3 = float(2 * np.pi - c1 - c2)
                for c in (c1, c2, c3):
                    t = stt(x.ap[0:rows], n.ap[0:rows], -c, x.ap[0:rows], ALU.mult, ALU.add, tn, t)
                t = ts(V, x.ap[0:rows], x.ap[0:rows], 3.1415925, -3.1415925, ALU.min, ALU.max, t)
                t = act(o.ap[0:rows], x.ap[0:rows], ACT.Sin, t, ow)
                drop(x, t)
                drop(n, t)
                return t

            def filter_mlp(l):
                w = get()
                tw = dma(w.ap[0:64, 0:128], ins["w12"][l], w.free)
                z = get()
                tz = dma(z.ap[0:33, :], ins["zpos"], z.free)
                yield
                b = get("P")
                b.t = mm(b.ap[0:64, :], w.ap[0:33, 0:64], z.ap[0:33, :], True, True, b.free, tw, tz, inc=True)
                drop(z, b.t)
                h1 = get()
                t = sine(b, 64, par(f"hb1{l}", 0, 64), par(f"hf1{l}", 0, 64), h1, h1.free)
                yield
                yield
                b = get("P")
                b.t = mm(b.ap[0:64, :], w.ap[0:64, 64:128], h1.ap[0:64, :], True, True, b.free, t, inc=True)
                drop(w, b.t)
                drop(h1, b.t)
                hid = get()
                t1 = memset(V, hid.ap[64:65, :], 1.0, hid.free)
                t2 = sine(b, 64, par(f"hb2{l}", 0, 64), par(f"hf2{l}", 0, 64), hid, hid.free)
                hid.t = (t1, t2)
                return hid

            def conv_chunk(l, part, c, h):
                s = scaled(("b", l, "hy", 4 * part + c), h)
                t = s.t
                o = get()
                V.wait(o.free)
                o.t = short_conv(s.ap, t, o.ap, [par(f"hconv{l}", 12 * j + 4 * part + c) for j in range(3)], 1)
                drop(s, o.t)
                return o

            def to_tokens(fm):
                tm = []
                for i in range(4):
                    b = get("P")
                    for c in range(4):
                        t = tp(b.ap[:, 128 * c:128 * c + 128], fm[c].ap[:, 256 * (i % 2) + i // 2:256 * (i % 2) + 256:2],
                               fm[c].t, b.free, inc=(c == 3))
                    o = get()
                    o.t = cp(A if i % 2 else V, o.ap, b.ap, t, o.free)
                    drop(b, o.t)
                    tm.append(o)
                for x in fm:
                    drop(x, t)
                return tm

            def spectra(l, o, R, u, aux):
                ye, yo = {}, {}
                low = None
                for j in (0, 2, 1, 3):
                    wh, wl, wt = weight(("dft", "f", j, l, o))
                    bk = [get("P") for _ in range(4)]
                    jobs = [(0, u, 0), (1, u, 4), (2, R[0], 0), (3, R[1], 4)]
                    for bi, src, k0 in jobs:
                        for k in range(4):
                            t = mm3(bk[bi].ap, (wh[:, k0 + k, :], wl[:, k0 + k, :]), cols(src[k], FULL), k == 0, k == 3,
                                    wt, bk[bi].free, src[k][2], inc=(k == 3))
                        bk[bi].t = t
                    weight_done(t)
                    fr, fi = get(), get()
                    tr = cp(A, fr.ap, bk[2].ap, bk[2].t, fr.free)
                    ti = cp(A, fi.ap, bk[3].ap, bk[3].t, fi.free)
                    drop(bk[2], tr)
                    drop(bk[3], ti)
                    a, b, c = get(), get(), get()
                    t1 = tt(V, a.ap, bk[0].ap, fr.ap, ALU.mult, bk[0].t, tr, a.free)
                    t2 = tt(V, b.ap, bk[1].ap, fi.ap, ALU.mult, bk[1].t, ti, b.free)
                    t3 = tt(V, c.ap, bk[0].ap, fi.ap, ALU.mult, bk[0].t, ti, c.free)
                    t4 = tt(V, fr.ap, bk[1].ap, fr.ap, ALU.mult, bk[1].t, t1)
                    drop(bk[0], t3)
                    drop(bk[1], t4)
                    drop(fi, t3)
                    E = V if j == 3 else G
                    t5 = tt(E, a.ap, a.ap, b.ap, ALU.subtract, t1, t2)
                    t6 = tt(E, c.ap, c.ap, fr.ap, ALU.add, t3, t4)
                    drop(b, t5)
                    drop(fr, t6)
                    a.t, c.t = t5, t6
                    aux.step()
                    if j < 2:
                        low = a, c
                        continue
                    for n, (x, z, side, other) in enumerate(((low[0], a, ye, yo), (low[1], c, yo, ye))):
                        d = get()
                        d.t = tt(E, d.ap, x.ap, z.ap, ALU.subtract, x.t, z.t, d.free)
                        x.t = tt(V, x.ap, x.ap, z.ap, ALU.add, x.t, z.t, d.t)
                        drop(z, x.t, d.t)
                        side[2 * n + j % 2] = split(x.ap, x.t)
                        other[2 * n + j % 2] = split(d.ap, d.t)
                        drop(x, side[2 * n + j % 2][2])
                        drop(d, other[2 * n + j % 2][2])
                for x in R[0] + R[1] + u:
                    drop_pair(x, t)
                return [[y[n] for n in range(4)] for y in (ye, yo)]

            def hyena(l, h, y, hid):
                def signals():
                    fm = []
                    for part in range(2):
                        fm.append([])
                        for c in range(4):
                            fm[part].append(conv_chunk(l, part, c, h))
                            if part and c == 0:
                                v = to_tokens(fm[0])
                                vs = [split(x.ap, x.t) for x in v]
                            yield
                    x1 = to_tokens(fm[1])
                    got.append((v, vs, x1))

                def skip(v, parts, o):
                    for j in range(4):
                        v[j].t = tt(G, v[j].ap, v[j].ap, skb.ap, ALU.mult, v[j].t, parts[j][2], skb.t)
                    if o == 0:
                        skb.t = dma(skb.ap, ins["skip"][l, 1], v[3].t)
                    else:
                        drop(skb, v[3].t)

                skb = get()
                skb.t = dma(skb.ap, ins["skip"][l, 0], skb.free)
                got = []
                R = ([], [])
                f = Aux(filters(l, 0, hid, R))
                sg = Aux(signals())
                while not (len(R[1]) == 4 and sg.done):
                    sg.step()
                    if len(R[1]) < 4:
                        f.step()
                v, vs, x1 = got[0]
                skip(v, vs, 0)
                Y = spectra(l, 0, R, vs, f)
                while not f.done:
                    f.step()
                rn = f.val
                R = ([], [])
                f = Aux(filters(l, 1, hid, R))
                x2 = [conv_chunk(l, 2, 0, h)]
                for j in range(4):
                    b = project(("dft", "i", j, l, 0), Y[j // 2])
                    t1 = tt(V, b.ap, b.ap, rn.ap, ALU.mult, b.t, rn.t)
                    t3 = tt(V, v[j].ap, b.ap, v[j].ap, ALU.add, t1, v[j].t)
                    drop(b, t3)
                    t4 = tt(G if j < 3 else V, v[j].ap, v[j].ap, x1[j].ap, ALU.mult, t3, x1[j].t)
                    v[j].t = t4
                    drop(x1[j], t4)
                    if len(R[1]) < 4:
                        f.step()
                for p in Y[0] + Y[1]:
                    drop_pair(p, b.t)
                drop(rn, t3)
                zs = [split(x.ap, x.t) for x in v]
                while len(R[1]) < 4:
                    f.step()
                drop(hid, b.t, R[0][-1][2], hid.t, hid.last)
                skip(v, zs, 1)
                x2.append(conv_chunk(l, 2, 1, h))
                Y = spectra(l, 1, R, zs, f)
                while not f.done:
                    f.step()
                rn = f.val
                x2.append(conv_chunk(l, 2, 2, h))
                for j in range(4):
                    b = project(("dft", "i", j, l, 1), Y[j // 2])
                    t1 = tt(V, b.ap, b.ap, rn.ap, ALU.mult, b.t, rn.t)
                    v[j].t = tt(V, v[j].ap, b.ap, v[j].ap, ALU.add, t1, v[j].t)
                    drop(b, v[j].t)
                for p in Y[0] + Y[1]:
                    drop_pair(p, b.t)
                drop(rn, v[3].t)
                x2.append(conv_chunk(l, 2, 3, h))
                for c in range(4):
                    b = get("P")
                    for i in range(4):
                        t = tp(b.ap[:, 128 * i:128 * i + 128], v[i].ap[:, 128 * c:128 * c + 128], v[i].t, b.free,
                               inc=(i == 3))
                    x = x2[c]
                    xp = x.ap.rearrange("p (n e) -> p e n", e=2)
                    t = tt(V, xp, b.ap.rearrange("p (e n) -> p e n", e=2), xp, ALU.mult, t, x.t)
                    drop(b, t)
                    y.append(split(x.ap, t))
                    drop(x, y[-1][2])
                for x in v:
                    drop(x, t)

            def attend_second(l, h, y):
                cos, sin = tables(1)
                ka = yield from rope(("b", l, "k", 0), h, cos, sin, rotB, par(f"akn{l}"))
                kb = get()
                t1 = cp(A, kb.ap[64:128, :], ka.ap[0:64, :], ka.t, kb.free)
                t2 = cp(V, kb.ap[0:64, :], ka.ap[64:128, :], ka.t, kb.free)
                kb.t = (t1, t2)
                ks = [ka, kb]
                wh, wl, wt = weight(("b", l, "v", 0))
                vb = get("P")
                for tq in range(4):
                    for k in range(8):
                        t = mm3(vb.ap[:, 128 * tq:128 * tq + 128], cols(h[k], slice(128 * tq, 128 * tq + 128)),
                                (wh[:, k, :], wl[:, k, :]), k == 0, k == 7, wt, vb.free, h[k][2], inc=(k == 7))
                weight_done(t)
                va = get()
                rt = h.by_token()
                for tq in range(4):
                    sl = slice(128 * tq, 128 * tq + 128)
                    va.t = h.used(act(va.ap[:, sl], vb.ap[:, sl], ACT.Copy, t, va.free, rt.t, scale=rt.ap[:, tq:tq + 1]))
                drop(vb, va.t)
                v = []
                for tq in range(4):
                    x = Tile(va.ap[:, 128 * tq:128 * tq + 128], "F")
                    x.t = va.t
                    v.append(x)
                yield

                def qc(c):
                    return rope(("b", l, "q", c), h, cos, sin, rotB, par(f"aqn{l}"), query=True)

                nxt, tail = Aux(qc(0)), Aux(None)
                last = []
                for c in range(4):
                    while not nxt.done:
                        nxt.step()
                        yield
                    q = nxt.val
                    nxt = Aux(qc(c + 1) if c < 3 else None)

                    def finish(b):
                        f = get()
                        t = cp(V, f.ap, b.ap, b.t, f.free)
                        drop(b, t)
                        y.append(split(f.ap, t))
                        drop(f, y[-1][2])
                        last.append(b.t)

                    def done_q(q, ks, t):
                        drop(q, t)

                    gi = c // 2
                    g = Aux(head_pair(q, (ks[gi], ks[1 - gi]), v, (64 * gi, 64 * gi), None, finish, done_q))
                    while not g.done:
                        g.step()
                        tail.step()
                        nxt.step()
                        yield
                    tail = Aux(g.val)
                while not tail.done:
                    tail.step()
                    yield
                drop(va, last)
                for k in ks:
                    drop(k, last)
                drop(cos, q.t)
                drop(sin, q.t)

            def gla(l, h, y):
                wl_ = get()
                ta = memset(V, wl_.ap[0:32, :], 0.0, wl_.free)
                t1 = dma(wl_.ap[0:16, 0:256], ins["wlr"][l, 0], ta)
                t2 = dma(wl_.ap[16:32, 256:512], ins["wlr"][l, 1], ta)
                wl_.t = (t1, t2)
                lr = scaled(("b", l, "lr", 0), h, 32)
                rst = get()
                tm0 = memset(V, rst.ap, 1.0, rst.free)
                rst.t = memset(V, rst.ap.rearrange("p (n c) -> p n c", c=64)[:, :, 0:1], 0.0, tm0)
                yield

                def front(hp):
                    lgs, es, tt_ = [], [], []
                    for d in range(2):
                        b = get("P")
                        t = mm(b.ap, wl_.ap[0:32, 256 * d + 128 * hp:256 * d + 128 * hp + 128], lr.ap[0:32, :],
                               True, True, b.free, wl_.t, lr.t, inc=True)
                        lg, e = get(), get()
                        t = ts(V, lg.ap, b.ap, par(f"glab{l}", 2 * d + hp), None, ALU.add, None, t, lg.free, cst)
                        drop(b, t)
                        te = act(e.ap, lg.ap, ACT.Abs, t, e.free)
                        te = act(e.ap, e.ap, ACT.Exp, te, scale=-1.0)
                        lgs.append(lg)
                        es.append(e)
                        tt_.append((t, te))
                    for d in range(2):
                        t, te = tt_[d]
                        t1 = act(es[d].ap, es[d].ap, ACT.Ln, te, bias=1.0)
                        tt_[d] = (ts(V, lgs[d].ap, lgs[d].ap, 0.0, None, ALU.min, None, t, te), t1)
                    for d in range(2):
                        lg, B = lgs[d], es[d]
                        t = tt(V, lg.ap, lg.ap, B.ap, ALU.subtract, tt_[d])
                        src, dst = (lg.ap, B.ap) if d == 0 else (lg.ap[:, ::-1], B.ap[:, ::-1])
                        B.t = V.put(lambda e_, src=src, dst=dst: e_.tensor_tensor_scan(dst, rst.ap, src, 0.0, ALU.mult,
                                                                                     ALU.add), (t, rst.t))
                    return lgs, es

                nf = front(0)
                yield
                v = []
                for i, b in enumerate(project_tok(("b", l, "gv"), h)):
                    x = get()
                    rt = h.by_token()
                    x.t = h.used(act(x.ap, b.ap, ACT.Copy, b.t, x.free, rt.t, scale=rt.ap[:, i:i + 1]))
                    drop(b, x.t)
                    v.append(x)
                yield
                for hp in range(2):
                    lgs, es = nf
                    k = scaled(("b", l, "gk", hp), h)
                    bq = project(("b", l, "gq", hp), h, raw=True)
                    q = get()
                    q.t = h.used(stt(q.ap, bq.ap, 0.125, h.r.ap, ALU.mult, ALU.mult, bq.t, q.free, h.r.t))
                    drop(bq, q.t)
                    yield
                    qd, kinv, sp, decs, t5s = [], [], [], [], []
                    for d in range(2):
                        lg, B = lgs[d], es[d]
                        t = B.t
                        B3 = B.ap.rearrange("p (n c) -> p n c", c=64)
                        Bl = B3[:, :, 63:64] if d == 0 else B3[:, :, 0:1]
                        t5 = tt(V, lg.ap.rearrange("p (n c) -> p n c", c=64), Bl.to_broadcast([128, 8, 64]), B3,
                                ALU.subtract, t)
                        t5 = act(lg.ap, lg.ap, ACT.Exp, t5, scale=1.0 / 16)
                        x = get()
                        tx = act(x.ap, B.ap, ACT.Exp, t, x.free, scale=-1.0 / 16)
                        x2 = get()
                        tx2 = act(x2.ap, B.ap, ACT.Exp, t, x2.free, scale=1.0 / 16)
                        dec = get("S")
                        tdec = act(dec.ap[:, 0:8], Bl.rearrange("p n c -> p (n c)"), ACT.Exp, t, dec.free, scale=1.0 / 16)
                        t5s.append(tt(V, lg.ap, lg.ap, k.ap, ALU.mult, t5, k.t))
                        x.t = tt(V, x.ap, x.ap, k.ap, ALU.mult, tx, k.t)
                        x2.t = tt(V, x2.ap, x2.ap, q.ap, ALU.mult, tx2, q.t)
                        kinv.append(x)
                        qd.append(x2)
                        decs.append((dec, tdec))
                        yield 2
                    kds = []
                    for d in range(2):
                        b = get("P")
                        for i in range(4):
                            t = tp(b.ap[:, 128 * i:128 * i + 128], lgs[d].ap[:, 128 * i:128 * i + 128], t5s[d], b.free,
                                   inc=(i == 3))
                        kd = es[d]
                        kd.t = cp(V if d else A, kd.ap, b.ap, t, decs[d][1], qd[d].t, kinv[d].t)
                        drop(b, kd.t)
                        drop(lgs[d], t)
                        kds.append(kd)
                    drop(q, qd[1].t)
                    drop(k, t5s[1], kinv[1].t)
                    yield 2
                    ams = [[], []]

                    def inside(hh):
                        half = slice(64 * hh, 64 * hh + 64)
                        for d in range(2):
                            b = get("P")
                            for i in range(4):
                                sl = slice(128 * i, 128 * i + 128)
                                t = mm(b.ap[:, sl], kinv[d].ap[half, sl], qd[d].ap[half, sl], True, True, b.free,
                                       kinv[d].t, qd[d].t, inc=(i == 3))
                            t_last = t
                            x = get()
                            t = ts(V, x.ap, b.ap, BIG, -BIG, ALU.min, ALU.max, t, x.free)
                            drop(b, t)
                            mk = (maskf if d == 0 else maskb).unsqueeze(1).to_broadcast([128, 4, 128])
                            x3 = x.ap.rearrange("p (i c) -> p i c", c=128)
                            x.t = tt(G, x3, x3, mk, ALU.mult, t, cst)
                            ams[hh].append(x)
                        kinv[0].last = t_last
                        a0, a1 = ams[hh]
                        a0.t = tt(G, a0.ap, a0.ap, a1.ap, ALU.add, a0.t, a1.t)
                        drop(a1, a0.t)

                    for d in range(2):
                        kd = kds[d]
                        dec, tdec = decs[d]
                        bs = [get("P"), get("P")]
                        for n in range(8):
                            rows = slice(64 * (n % 2), 64 * (n % 2) + 64)
                            for hh in range(2):
                                t = mm(bs[n % 2].ap[64 * hh:64 * hh + 64, 128 * (n // 2):128 * (n // 2) + 128],
                                       kd.ap[rows, 128 * (n // 2) + 64 * hh:128 * (n // 2) + 64 * hh + 64],
                                       v[n // 2].ap[rows, 256 * hp + 128 * hh:256 * hp + 128 * hh + 128], True, True,
                                       kd.t, bs[n % 2].free, v[n // 2].t, inc=(n == 7 and hh == 1))
                        drop(kd, t)
                        inside(d)
                        sA, sB = get(), get()
                        SS = [(sA if n < 4 else sB).ap[:, 128 * (n % 4):128 * (n % 4) + 128] for n in range(8)]
                        V.wait([sA.free, sB.free])
                        seq = list(range(7)) if d == 0 else list(range(7, 0, -1))
                        ts_ = t
                        for j, n in enumerate(seq):
                            nx = n + 1 if d == 0 else n - 1
                            ds = bs[n % 2].ap[:, 128 * (n // 2):128 * (n // 2) + 128]
                            if j == 0:
                                ts_ = cp(V, SS[nx], ds, ts_)
                            else:
                                ts_ = stt(SS[nx], SS[n], dec.ap[:, n:n + 1], ds, ALU.mult, ALU.add, ts_, tdec)
                        drop(bs[0], ts_)
                        drop(bs[1], ts_)
                        drop(dec, ts_)
                        sp.append((SS, ts_, sA, sB))
                        yield 2
                    for x in kinv:
                        drop(x, kinv[0].last)
                    if hp == 0:
                        nf = front(1)
                        yield
                    for hh in range(2):
                        half = slice(64 * hh, 64 * hh + 64)
                        am = ams[hh][0]
                        ob = get("P")
                        e0 = 256 * hp + 128 * hh
                        for i in range(4):
                            tl = mm(ob.ap[:, 128 * i:128 * i + 128], v[i].ap[:, e0:e0 + 128],
                                    am.ap[:, 128 * i:128 * i + 128], True, False, am.t, ob.free, v[i].t)
                            jobs = [(n, d) for n in (2 * i, 2 * i + 1) for d in range(2) if (n, d) not in ((0, 0), (7, 1))]
                            for n, d in jobs:
                                SS, tS = sp[d][0], sp[d][1]
                                tl = mm(ob.ap[:, 64 * n:64 * n + 64], SS[n][half, :], qd[d].ap[half, 64 * n:64 * n + 64],
                                        False, (n, d) == jobs[-1], tS, qd[d].t, inc=(n, d) == jobs[-1])
                        drop(am, tl)
                        sq = get()
                        t = act(sq.ap, ob.ap, ACT.Square, tl, sq.free)
                        bg = project(("b", l, "go", 2 * hp + hh), h)
                        sg = get()
                        tg = act(sg.ap, bg.ap, ACT.Silu, bg.t, sg.free)
                        drop(bg, tg)
                        ss = get("P")
                        ss.t = mm(ss.ap, ones, sq.ap, True, True, ss.free, t, cst, inc=True)
                        tr = rstd(ss, 1.0 / 128, sq.ap, 512, ss.t)
                        ty = stt(sq.ap, ob.ap, par(f"onorm{l}"), sq.ap, ALU.mult, ALU.mult, tr, tl, cst)
                        drop(ob, ty)
                        ty = tt(V, sq.ap, sq.ap, sg.ap, ALU.mult, ty, tg)
                        drop(sg, ty)
                        y.append(split(sq.ap, ty))
                        drop(sq, y[-1][2])
                        yield
                    for x in qd:
                        drop(x, tl)
                    for x in sp:
                        drop(x[2], tl)
                        drop(x[3], tl)
                for x in v + [lr, wl_]:
                    drop(x, tl)
                drop(rst, ts_)

            def memory_side(l):
                km, vm = [], [[None, None], [None, None]]
                mt = []
                acc = get()
                for j in range(4):
                    x = get()
                    x.t = dma(x.ap, ins["mem"][j], x.free)
                    mt.append(x)
                for j in range(4):
                    x = mt[j]
                    if j == 0:
                        ta = act(acc.ap, x.ap, ACT.Square, x.t, acc.free)
                    else:
                        sq = get()
                        t = act(sq.ap, x.ap, ACT.Square, x.t, sq.free)
                        ta = tt(V, acc.ap, acc.ap, sq.ap, ALU.add, t, ta)
                        drop(sq, ta)
                b = get("P")
                mm(b.ap[:, 0:256], ones, acc.ap[:, 0:256], True, False, b.free, ta, cst)
                b.t = mm(b.ap[:, 0:256], ones, acc.ap[:, 256:512], False, True, inc=True)
                tr = rstd(b, 1.0 / DM, acc.ap[:, 0:256], 256, b.t)
                mn, cuts = [], []
                for j in range(4):
                    x = mt[j]
                    for kk in range(2):
                        sl = slice(256 * kk, 256 * kk + 256)
                        t = stt(x.ap[:, sl], x.ap[:, sl], par(f"lnm{l}", 2 * j + kk), acc.ap[:, 0:256], ALU.mult, ALU.mult,
                                tr, x.t, cst)
                    p = split(x.ap, t)
                    drop(x, p[2])
                    mn += [p, p]
                    cuts += [slice(0, 256), slice(256, 512)]
                drop(acc, t)
                yield
                yield
                st.km, st.vm = km, vm
                for hd in range(4):
                    kt = get()
                    ss = get("P")
                    for kk in range(2):
                        b = project(("b", l, "xk", 2 * hd + kk), mn, n=256, cuts=cuts)
                        sq = get()
                        t = act(sq.ap[:, 0:256], b.ap[:, 0:256], ACT.Square, b.t, sq.free)
                        tk = act(kt.ap[:, 256 * kk:256 * kk + 256], b.ap[:, 0:256], ACT.Copy, b.t, kt.free, cst,
                                 scale=par(f"xkn{l}", kk))
                        drop(b, t, tk)
                        ss.t = mm(ss.ap[:, 0:256], ones, sq.ap[:, 0:256], kk == 0, kk == 1, t, ss.free, cst, inc=True)
                        if kk == 0:
                            drop(sq, ss.t)
                    tr = rstd(ss, 1.0 / 256, sq.ap[:, 0:256], 256, ss.t)
                    for kk in range(2):
                        kt.t = tt(V, kt.ap[:, 256 * kk:256 * kk + 256], kt.ap[:, 256 * kk:256 * kk + 256],
                                  sq.ap[:, 0:256], ALU.mult, tr, tk)
                    drop(sq, kt.t)
                    km.append(kt)
                    yield
                for half in range(2):
                    bs = project_tok(("b", l, "xv", half), mn, ntok=2, cuts=cuts)
                    for tq in range(2):
                        x = get()
                        x.t = cp(A, x.ap, bs[tq].ap, bs[tq].t, x.free)
                        drop(bs[tq], x.t)
                        vm[tq][half] = x
                    yield
                for p in mn[::2]:
                    drop_pair(p, bs[1].t)

            def cross(l, mem):
                mem.step()
                h = take_norm()
                mem.step()
                while len(st.km) < 4:
                    mem.step()
                km, vm = st.km, st.vm
                y = []

                def queries(hd):
                    qs = []
                    sqs = []
                    for kk in range(2):
                        b = project(("b", l, "xq", 2 * hd + kk), h)
                        sq = get()
                        sq.t = act(sq.ap, b.ap, ACT.Square, b.t, sq.free)
                        q = get()
                        q.t = act(q.ap, b.ap, ACT.Copy, b.t, q.free, cst, scale=par(f"xqn{l}", kk))
                        drop(b, sq.t, q.t)
                        qs.append(q)
                        sqs.append(sq)
                        yield
                    ss = get("P")
                    for i in range(4):
                        for kk in range(2):
                            ss.t = mm(ss.ap[:, i:i + 1], sqs[kk].ap[:, 128 * i:128 * i + 128], ones[:, 0:1], kk == 0, kk == 1,
                                      sqs[kk].t, ss.free, cst, inc=(i == 3 and kk == 1))
                    for sq in sqs:
                        drop(sq, ss.t)
                    r = qs[0].r = get("S")
                    tr = rstd(ss, 1.0 / 256, r.ap[:, 0:4], 4, r.free)
                    r.t = ts(V, r.ap[:, 0:4], r.ap[:, 0:4], 1.0 / 16, None, ALU.mult, None, tr)
                    return qs

                def scores(qs, hd):
                    ps = []
                    for i in range(4):
                        b = get("P")
                        for kk in range(2):
                            t = mm(b.ap[:, 0:256], qs[kk].ap[:, 128 * i:128 * i + 128],
                                   km[hd].ap[:, 256 * kk:256 * kk + 256], kk == 0, kk == 1, b.free, qs[kk].t, km[hd].t,
                                   inc=(kk == 1))
                        m, p = get("S"), get()
                        r = qs[0].r.ap[:, i:i + 1]
                        tm = V.put(lambda e, m=m, b=b: e.reduce_max(m.ap[:, 1:2], b.ap[:, 0:256], AX.X, negate=True),
                                   (t, m.free))
                        tm = ts(V, m.ap[:, 0:1], m.ap[:, 1:2], r, None, ALU.mult, None, tm, qs[0].r.t)
                        te = act(p.ap[:, 0:256], b.ap[:, 0:256], ACT.Exp, tm, p.free, bias=m.ap[:, 0:1], scale=r,
                                 accum_out=m.ap[:, 2:3])
                        drop(b, te)
                        p.t = te
                        ps.append((p, m))
                    for q in qs:
                        drop(q, t)
                    drop(qs[0].r, te)
                    for p, m in ps:
                        tr = recip(m.ap[:, 3:4], m.ap[:, 2:3], p.t)
                        p.t = ts(G, p.ap[:, 0:256], p.ap[:, 0:256], m.ap[:, 3:4], None, ALU.mult, None, tr, p.t)
                        drop(m, p.t)
                    return [p for p, _ in ps]

                def head(hd, qs):
                    ps = scores(qs, hd)
                    yield
                    bt = [get("P"), get("P")]
                    for kk in range(2):
                        for i in range(4):
                            t = tp(bt[kk].ap[:, 128 * i:128 * i + 128], ps[i].ap[:, 128 * kk:128 * kk + 128], ps[i].t,
                                   bt[kk].free, inc=(i == 3))
                        bt[kk].t = t
                    for p in ps:
                        drop(p, t)
                    pt = []
                    for kk in range(2):
                        x = get()
                        x.t = cp((V, A)[kk], x.ap, bt[kk].ap, bt[kk].t, x.free)
                        drop(bt[kk], x.t)
                        pt.append(x)
                    yield
                    for dc in range(2):
                        f = 256 * hd + 128 * dc
                        b = get("P")
                        for kk in range(2):
                            vv = vm[kk][f // 512]
                            t = mm(b.ap, vv.ap[:, f % 512:f % 512 + 128], pt[kk].ap, kk == 0, kk == 1, b.free, vv.t,
                                   pt[kk].t, inc=(kk == 1))
                        o = get()
                        to = cp(V, o.ap, b.ap, t, o.free)
                        drop(b, to)
                        y.append(split(o.ap, to))
                        drop(o, y[-1][2])
                    for x in pt:
                        drop(x, t)
                    last.append(t)

                last = []
                todo = [Aux(queries(0)), Aux(queries(1))]
                for q in todo:
                    while not q.done:
                        q.step()
                g = Aux(None)
                for hd in range(4):
                    qs = todo.pop(0).val
                    old, g = g, Aux(head(hd, qs))
                    nxt = Aux(queries(hd + 2) if hd < 2 else None)
                    todo.append(nxt)
                    old.step()
                    g.step()
                    if hd in (1, 2):
                        mem.step()
                    while not (nxt.done and old.done):
                        nxt.step()
                        old.step()
                while not (g.done and mem.done):
                    g.step()
                    mem.step()
                t = last[-1]
                for x in km + vm[0] + vm[1]:
                    drop(x, t)
                drop_h(h, t)
                out_product(("b", l, "xo"), y)

            def mlp(l, aux):
                h = take_norm()
                xn = []
                nm = None
                for half in range(2):
                    y = []
                    for c in range(16):
                        b = project(("b", l, "w1", 16 * half + c), h, raw=True)
                        r = get()
                        t = h.used(stt(r.ap, b.ap, 0.0, h.r.ap, ALU.max, ALU.mult, b.t, r.free, h.r.t))
                        drop(b, t)
                        t = tt(G, r.ap, r.ap, r.ap, ALU.mult, t)
                        y.append(split(r.ap, t))
                        drop(r, y[-1][2])
                    if half == 1:
                        drop_h(h, b.t)
                        nm = start_norm()
                    if half == 0:
                        nxt = load_x(0)
                    for c in range(8):
                        if half == 0:
                            x = nxt
                            if c < 7:
                                nxt = load_x(c + 1)
                        else:
                            x = xn[c]
                        b = project(("b", l, "w2", c, 2 * half), y[0:8], last=False)
                        b = project(("b", l, "w2", c, 2 * half + 1), y[8:16], bank=b, first=False)
                        add_out(b, x)
                        if half == 0:
                            xn.append(x)
                            continue
                        if nm is not None and c:
                            nm.add(xn[c - 1])
                        if aux is not None:
                            aux.step()
                    drop_h(y, b.t)
                if nm is not None:
                    nm.add(xn[7])
                st.x = xn

            def mix_second(l, hid, mem):
                h = take_norm()
                ya, yb, yc = [], [], []
                m = [None] * 8
                while not hid.done:
                    hid.step()
                hyena(l, h, yb, hid.val)
                beside(attend_second(l, h, ya), gated("b", l, h, ((1, yb),), m, True))
                beside(gla(l, h, yc), gated("b", l, h, ((0, ya),), m, True))
                for _ in gated("b", l, h, ((2, yc),), m, False):
                    pass
                out_product(("b", l, "wo"), m, mem)

            nm = start_norm()
            st.x = []
            if order is not None:
                issue(0)
                state["issued"] = 1
            for c in range(8):
                x = get()
                x.t = dma(x.ap, ins["x"][c], x.free)
                st.x.append(x)
            for x in st.x:
                nm.add(x)
            hid = [Aux(filter_mlp(l)) for l in range(2)]
            mem = [Aux(memory_side(l)) for l in range(2)]
            todo = [lambda: block_one(0, None), lambda: block_one(1, hid[0])]
            for l in range(2):
                todo += [lambda l=l: mix_second(l, hid[l], mem[l]), lambda l=l: cross(l, mem[l]),
                         lambda l=l: mlp(l, None if l else hid[1])]
            for f in todo[:steps]:
                f()
            for c in range(8):
                x = st.x[c]
                S.put(lambda e, c=c, x=x: e.dma_start(out[c], x.ap).then_inc(s_out, 16), x.t, inc=False)
            S.wait(Tok(s_out, 128))
            for i in range(len(s_misc)):
                S.wait(Tok(s_misc[i], 16 * mcount[i]))
            assert len(pools["F"]) == NF - 8 and len(pools["R"]) == NRT and len(pools["P"]) == 8, \
                {k: len(p) for k, p in pools.items()}
            return asked, rates, (M, V, A, G, S)

        _, plan, _ = emit(None, None)
        order, _, _ = emit(None, plan)
        _, _, (M, V, A, G, S) = emit(order, plan)

        block = ctx.enter_context(nc.Block())

        @block.tensor
        def _(e):
            M.play(e)

        @block.vector
        def _(e):
            V.play(e)

        @block.scalar
        def _(e):
            A.play(e)

        @block.gpsimd
        def _(e):
            G.play(e)

        @block.sync
        def _(e):
            S.play(e)


def tables():
    f = np.float32
    k = {}
    cst = np.zeros((128, 8, 128), f)
    p = np.arange(128)
    cst[:, 0] = np.eye(128)
    cst[:, 1] = 1
    cst[:, 2] = (p[:, None] // 64) == (p[None, :] // 64)
    for m in range(128):
        if m % 64 < 32:
            cst[m + 32, 3, m] = -1
        else:
            cst[m - 32, 3, m] = 1
        if m % 32 < 16:
            cst[m + 16, 4, m] = -1
        else:
            cst[m - 16, 4, m] = 1
    cst[:, 5] = np.where(p[None, :] <= p[:, None], 0, NEG)
    same = (p[:, None] // 64) == (p[None, :] // 64)
    cst[:, 6] = same & (p[:, None] <= p[None, :])
    cst[:, 7] = same & (p[:, None] > p[None, :])
    k["cst"] = cst
    rope = np.zeros((2, 2, 128, 512), f)
    inv = (f(1.0) / (f(10000.0) ** (np.arange(0, 64, 2, dtype=f) / f(64)))).astype(f)
    ang = np.arange(512, dtype=f)[:, None] * inv[None, :]
    rope[0, 0] = np.cos(ang).T[(p % 64) % 32]
    rope[0, 1] = np.sin(ang).T[(p % 64) % 32]
    inv = (f(10000.0) ** (-np.arange(16, dtype=f) / f(16))).astype(f)
    t = np.arange(512)
    pos = np.stack([t // 64, t % 64], 1).astype(f)
    ang = (pos[:, :, None] * inv).astype(f)
    q = p % 64
    rope[1, 0] = np.cos(ang)[:, q // 32, q % 16].T
    rope[1, 1] = np.sin(ang)[:, q // 32, q % 16].T
    k["rope"] = rope
    cnt = np.zeros((4, 16), f)
    for g in range(4):
        cnt[g] = f(1) / np.minimum(np.arange(16) + 1, 2 << g).astype(f)
    k["cnt"] = np.broadcast_to(cnt.reshape(1, 64), (128, 64)).copy()
    L = 512
    tn = np.arange(L, dtype=f) / f(L - 1)
    w = (f(2.0 * np.pi) * np.arange(L, dtype=f) / f(L)).astype(f)
    fr = np.linspace(1e-4, 15, 16, dtype=f)
    fw = w[:, None] * fr
    even_odd = np.concatenate([np.arange(0, L, 2), np.arange(1, L, 2)])
    k["zpos"] = np.concatenate([tn[:, None], np.cos(fw), -np.sin(fw)], -1).T.astype(f)[:, even_odd].copy()
    deltas = np.abs(np.linspace(np.log(1e-2) / 0.3, np.log(1e-2) / 1.5, 512, dtype=f))
    k["win"] = np.exp(-tn[:, None] * deltas).astype(f)[even_odd].reshape(4, 128, 512)
    om = 2 * np.pi * (np.arange(512) + 0.5) / 1024
    a = np.arange(512)[:, None] * om[None, :]
    a = a[even_odd][:, np.concatenate([np.arange(256), 511 - np.arange(256)])]
    k["C"], k["Sn"] = np.cos(a).astype(f), np.sin(a).astype(f)
    return k


def layout(x):
    k = tables()
    place = {}
    ins = {n: k[n] for n in ("cst", "rope", "cnt", "zpos", "win")}
    flat = {}

    def fm(w):
        n = w.shape[0] // 128
        return w.reshape(n, 128, w.shape[1]).transpose(1, 0, 2)

    def add(arr, key, w):
        lst = flat.setdefault(arr, [0, []])
        n, cols = w.shape[1], w.shape[2]
        place[key] = (arr, lst[0], n, cols)
        lst[0] += w.size
        lst[1].append(np.ascontiguousarray(w).reshape(-1))

    def chunks(arr, l, name, w, c0=0):
        for c in range(w.shape[1] // 128):
            add(arr, (arr[1], l, name, c0 + c), fm(w[:, 128 * c:128 * c + 128]))

    def tok(arr, key, w):
        for j in range(4):
            v = w[256 * j:256 * j + 256].reshape(2, 128, 512).transpose(1, 0, 2).reshape(128, 8, 128)
            add(arr, key + (j,), v)

    for l in range(2):
        w = x["w_in"][l]
        arr = f"wa{l}"
        names = ["cb", "cc", "cx", "cgate", "q", "k", "v", "agate"]
        for i, n in enumerate(names):
            s = w[:, 512 * i:512 * i + 512]
            if n == "v":
                tok(arr, ("a", l, "v"), s)
            else:
                chunks(arr, l, n, s)
        chunks(arr, l, "iq", w[:, 4096:4608])
        add(arr, ("a", l, "ik", 0), fm(np.concatenate([w[:, 4608:4672]] + [w[:, 4672:4680]] * 8, 1)))
        chunks(arr, l, "pu", w[:, 4680:5192])
        chunks(arr, l, "pgate", w[:, 5192:5704])
        chunks(arr, l, "gate", w[:, 5704:8776])
        for br, n in enumerate(("w_out_conv", "w_out_attn", "w_out_pool")):
            for c in range(8):
                add(arr, ("a", l, "br", br, c), fm(x[n][l][:, 128 * c:128 * c + 128]))
        chunks(arr, l, "wo", x["w_o"][l])
        w = x["w_in_2"][l]
        arr = f"wb{l}"
        chunks(arr, l, "q", w[:, 0:512])
        add(arr, ("b", l, "k", 0), fm(w[:, 512:640]))
        add(arr, ("b", l, "v", 0), fm(w[:, 640:768]))
        chunks(arr, l, "hy", w[:, 768:2304])
        chunks(arr, l, "gq", w[:, 2304:2560])
        chunks(arr, l, "gk", w[:, 2560:2816])
        tok(arr, ("b", l, "gv"), w[:, 2816:3328])
        chunks(arr, l, "go", w[:, 3328:3840])
        lr = w[:, 3840:3872]
        add(arr, ("b", l, "lr", 0), fm(np.concatenate([lr] * 4, 1)))
        chunks(arr, l, "gate", w[:, 3872:6944])
        for br, n in enumerate(("w_br_attn_2", "w_br_hyena_2", "w_br_gla_2")):
            for c in range(8):
                add(arr, ("b", l, "br", br, c), fm(x[n][l][:, 128 * c:128 * c + 128]))
        chunks(arr, l, "wo", x["w_out_2"][l])
        chunks(arr, l, "xq", x["x_wq_2"][l])
        chunks(arr, l, "xk", x["x_wk_2"][l])
        for half in range(2):
            tok(arr, ("b", l, "xv", half), x["x_wv_2"][l][:, 512 * half:512 * half + 512])
        chunks(arr, l, "xo", x["x_wo_2"][l])
        chunks(arr, l, "w1", x["mlp_w1_2"][l])
        for c in range(8):
            for g in range(4):
                add(arr, ("b", l, "w2", c, g), fm(x["mlp_w2_2"][l][1024 * g:1024 * g + 1024, 128 * c:128 * c + 128]))
    for j in range(4):
        sl = slice(128 * j, 128 * j + 128)
        add("wd", ("dft", "f", j), np.concatenate([fm(k[n][:, sl]) for n in ("C", "Sn")], 1))
        add("wd", ("dft", "i", j), np.concatenate([fm(k[n].T[0:256, sl]) for n in ("C", "Sn")], 1))
        for d in "fi":
            for l in range(2):
                for o in range(2):
                    place["dft", d, j, l, o] = place["dft", d, j]
    for arr, (_, lst) in flat.items():
        ins[arr] = np.concatenate(lst)
    par = []

    def col(name, a):
        place["par", name] = sum(q.shape[1] for q in par)
        b = np.zeros((128, a.shape[1]), np.float32)
        b[0:a.shape[0]] = a
        par.append(b)

    def vec(name, a):
        col(name, a.reshape(-1, 128).T)

    for l in range(2):
        vec(f"ng{l}", x["norm_g"][l])
        vec(f"conv{l}", x["conv_w"][l])
        col(f"qg{l}", np.concatenate([x["q_norm_g"][l]] * 2)[:, None])
        col(f"kg{l}", np.concatenate([x["k_norm_g"][l]] * 2)[:, None])
        vec(f"pscale{l}", x["pool_scale"][l])
        vec(f"lnmix{l}", x["ln_mix_2"][l])
        col(f"aqn{l}", np.concatenate([x["attn_qnorm_2"][l]] * 2)[:, None])
        col(f"akn{l}", np.concatenate([x["attn_knorm_2"][l]] * 2)[:, None])
        vec(f"hconv{l}", x["hy_conv_2"][l])
        col(f"hb1{l}", x["hy_b1_2"][l][:, None])
        col(f"hb2{l}", x["hy_b2_2"][l][:, None])
        col(f"hf1{l}", x["hy_freq_2"][l, 0][:, None])
        col(f"hf2{l}", x["hy_freq_2"][l, 1][:, None])
        vec(f"glab{l}", x["gla_b_lr_2"][l])
        vec(f"onorm{l}", x["gla_onorm_2"][l])
        vec(f"lnx{l}", x["ln_x_2"][l])
        vec(f"lnm{l}", x["ln_mem_2"][l])
        vec(f"xqn{l}", x["x_qnorm_2"][l])
        vec(f"xkn{l}", x["x_knorm_2"][l])
        vec(f"lnp{l}", x["ln_mlp_2"][l])
    n = sum(q.shape[1] for q in par)
    par.append(np.zeros((128, PB_COLS - n), np.float32))
    ins["par"] = np.concatenate(par, 1)
    ins["poolw"] = x["pool_w"].transpose(0, 2, 1, 3).reshape(2, 128, 512)
    ins["skip"] = np.broadcast_to(x["hy_skip_2"][:, :, None, :], (2, 2, 128, 512))
    w12 = np.zeros((2, 64, 128), np.float32)
    w12[:, 0:33, 0:64] = x["hy_w1_2"]
    w12[:, :, 64:128] = x["hy_w2_2"]
    ins["w12"] = w12
    w3 = np.concatenate([x["hy_w3_2"], x["hy_b3_2"][:, None, :]], 1)
    ins["w3"] = w3.reshape(2, 65, 4, 512).transpose(0, 2, 1, 3)
    ins["wlr"] = x["gla_w_lr_2"]
    ins["mem"] = x["mem_2"][0].T.reshape(4, 2, 128, 256).transpose(0, 2, 1, 3).reshape(4, 128, 512)
    ins["x"] = x["x"][0].T.reshape(8, 128, 512)
    return {n: np.ascontiguousarray(a) for n, a in ins.items()}, place


def kernel(**inputs):
    import concourse.bacc as _bacc
    from concourse.bass_utils import run_bass_kernel_spmd as _run

    arrays, place = layout({n: np.asarray(a) for n, a in inputs.items()})
    nc = _bacc.Bacc("TRN2", target_bir_lowering=False, num_devices=1)
    aps = {n: nc.dram_tensor(f"in_{n}", a.shape, mybir.dt.from_np(a.dtype), kind="ExternalInput").ap()
           for n, a in arrays.items()}
    out = nc.dram_tensor("out_x", [8, 128, 512], mybir.dt.float32, kind="ExternalOutput").ap()
    program(nc, aps, place, out)
    r = _run(nc, [{f"in_{n}": a for n, a in arrays.items()}], core_ids=[0])
    o = np.asarray(r.results[0]["out_x"])
    return np.ascontiguousarray(o.reshape(1024, 512).T).reshape(1, 512, 1024)
```
